# Optimizing a Trainium2 kernel written in Bass

```python
import math
import jax
import jax.numpy as jnp
from jax import lax
import numpy as np

D_MODEL = 1024
BATCH = 1
SEQ = 256
DEPTH = 1
DEC_BATCH = 1
DEC_SEQ = 512
PAST_LEN = 128

HEAD_DIM = 64
N_Q_HEADS = 8
N_KV_HEADS = 2
GQA_GROUP = N_Q_HEADS // N_KV_HEADS
ATTN_WIDTH = N_Q_HEADS * HEAD_DIM
KV_WIDTH = N_KV_HEADS * HEAD_DIM
WINDOW = 128
BLOCK = 128
ROPE_DIM = HEAD_DIM // 4
ROPE_THETA = 500000.0
HYENA_WIDTH = D_MODEL // 2
HYENA_ORDER = 2
SHORT_CONV = 3
FILTER_EMB = 33
FILTER_HIDDEN = 64
N_DIRS = 2
FILTER_OUT = N_DIRS * HYENA_ORDER * HYENA_WIDTH
DECAY_PCT_SHORT = 0.3
DECAY_PCT_LONG = 1.5
DECAY_TARGET = 1e-2
DECAY_SHIFT = 0.05
D_FF = 4 * D_MODEL
NORM_EPS = 1e-6
Q_END = ATTN_WIDTH
K_END = Q_END + KV_WIDTH
V_END = K_END + KV_WIDTH
HY_END = V_END + (HYENA_ORDER + 1) * HYENA_WIDTH
IN_PROJ_WIDTH = HY_END + 2 * D_MODEL
NEG_INF = -1e30

kernel_name = 'hybrid_swa_hyena_adaln_encoder'

def rmsnorm(x, g):
    xf = x.astype(jnp.float32)
    y = xf * lax.rsqrt(jnp.mean(xf * xf, axis=-1, keepdims=True) + NORM_EPS)
    return (y * g.astype(jnp.float32)).astype(x.dtype)

def modulate(h, shift, scale):
    return h * (1 + scale[:, None, :]) + shift[:, None, :]

def partial_rope(x):
    L = x.shape[1]
    half = ROPE_DIM // 2
    inv_freq = ROPE_THETA ** (-jnp.arange(half, dtype=jnp.float32) * 2.0 / ROPE_DIM)
    ang = jnp.arange(L, dtype=jnp.float32)[:, None] * inv_freq[None, :]
    cos = jnp.cos(ang)[:, None, :]
    sin = jnp.sin(ang)[:, None, :]
    xr = x[..., :ROPE_DIM].astype(jnp.float32)
    x1, x2 = xr[..., :half], xr[..., half:]
    rot = jnp.concatenate([x1 * cos - x2 * sin, x2 * cos + x1 * sin], axis=-1).astype(x.dtype)
    return jnp.concatenate([rot, x[..., ROPE_DIM:]], axis=-1)

def windowed_gqa_sink(q, k, v, sink):
    B, L = q.shape[0], q.shape[1]
    nb = L // BLOCK
    qb = q.reshape(B, nb, BLOCK, N_KV_HEADS, GQA_GROUP, HEAD_DIM)
    pad = ((0, 0), (BLOCK, BLOCK), (0, 0), (0, 0))

    def bands(t):
        tp = jnp.pad(t, pad).reshape(B, nb + 2, BLOCK, N_KV_HEADS, HEAD_DIM)
        return jnp.concatenate([tp[:, :nb], tp[:, 1:nb + 1], tp[:, 2:nb + 2]], axis=2)

    kb = bands(k)
    vb = bands(v)
    s = jnp.einsum('bnqhgd,bnjhd->bnhgqj', qb, kb,
                   preferred_element_type=jnp.float32) * (HEAD_DIM ** -0.5)
    blk = jnp.arange(nb)[:, None, None]
    qpos = blk * BLOCK + jnp.arange(BLOCK)[None, :, None]
    kpos = (blk - 1) * BLOCK + jnp.arange(3 * BLOCK)[None, None, :]
    valid = (jnp.abs(kpos - qpos) <= WINDOW) & (kpos >= 0) & (kpos < L)
    s = jnp.where(valid[None, :, None, None], s, NEG_INF)
    sk = sink.astype(jnp.float32).reshape(N_KV_HEADS, GQA_GROUP)[None, None, :, :, None, None]
    m = jnp.maximum(jnp.max(s, axis=-1, keepdims=True), sk)
    e = jnp.exp(s - m)
    p = e / (jnp.sum(e, axis=-1, keepdims=True) + jnp.exp(sk - m))
    o = jnp.einsum('bnhgqj,bnjhd->bnqhgd', p.astype(v.dtype), vb)
    return o.reshape(B, L, ATTN_WIDTH)

def hyena_filter_spectra(L, w1, b1, f1, w2, b2, f2, w3):
    f32 = jnp.float32
    t = jnp.linspace(0.0, 1.0, L, dtype=f32)[:, None]
    n_bands = (FILTER_EMB - 1) // 2
    w = 2.0 * math.pi * jnp.arange(L, dtype=f32)[:, None] / L
    fr = jnp.linspace(1e-4, n_bands - 1, n_bands, dtype=f32)[None, :]
    z = jnp.concatenate([t, jnp.cos(fr * w), -jnp.sin(fr * w)], axis=-1)
    h = jnp.sin(f1.astype(f32) * (z @ w1.astype(f32) + b1.astype(f32)))
    h = jnp.sin(f2.astype(f32) * (h @ w2.astype(f32) + b2.astype(f32)))
    h = (h @ w3.astype(f32)).reshape(L, N_DIRS, HYENA_ORDER, HYENA_WIDTH)
    max_decay = math.log(DECAY_TARGET) / DECAY_PCT_SHORT
    min_decay = math.log(DECAY_TARGET) / DECAY_PCT_LONG
    deltas = jnp.abs(jnp.linspace(min_decay, max_decay, HYENA_WIDTH, dtype=f32))
    decay = jnp.exp(-t * deltas[None, :])
    h = h * (decay + DECAY_SHIFT)[:, None, None, :]
    hf, hb = h[:, 0], h[:, 1]
    taps = jnp.concatenate([(hf[0] + hb[0])[None], hf[1:], jnp.zeros_like(hf[:1]), hb[1:][::-1]], axis=0)
    return jnp.fft.rfft(taps, axis=0)

def long_conv(u, spec, bias):
    L = u.shape[1]
    uf = u.astype(jnp.float32)
    y = jnp.fft.irfft(jnp.fft.rfft(uf, n=2 * L, axis=1) * spec[None], n=2 * L, axis=1)[:, :L]
    return y + uf * bias.astype(jnp.float32)

def hyena_branch(u, conv_w, conv_b, spec, hyena_bias):
    L = u.shape[1]
    pad = SHORT_CONV // 2
    up = jnp.pad(u, ((0, 0), (pad, pad), (0, 0)))
    uc = conv_b
    for i in range(SHORT_CONV):
        uc = uc + up[:, i:i + L] * conv_w[i]
    x1, x2, v = jnp.split(uc, HYENA_ORDER + 1, axis=-1)
    z = x1.astype(jnp.float32) * long_conv(v, spec[:, 0], hyena_bias[0])
    z = x2.astype(jnp.float32) * long_conv(z, spec[:, 1], hyena_bias[1])
    return z.astype(u.dtype)

def run_trunk(x, c, w_ada, b_ada, norm1_g, w_in, attn_sink, conv_w, conv_b,
              filt_w1, filt_b1, filt_freq1, filt_w2, filt_b2, filt_freq2, filt_w3,
              hyena_bias, w_attn_o, w_hyena_o, w_out, norm2_g, w_up, w_down,
              w_ada_final, b_ada_final, final_g):
    B, L, _ = x.shape
    c_act = jax.nn.silu(c)
    for l in range(DEPTH):
        mod = c_act @ w_ada[l] + b_ada[l]
        sh1, sc1, g1, sh2, sc2, g2 = jnp.split(mod, 6, axis=-1)
        h = modulate(rmsnorm(x, norm1_g[l]), sh1, sc1)
        proj = h @ w_in[l]
        q = partial_rope(proj[..., :Q_END].reshape(B, L, N_Q_HEADS, HEAD_DIM))
        k = partial_rope(proj[..., Q_END:K_END].reshape(B, L, N_KV_HEADS, HEAD_DIM))
        v = proj[..., K_END:V_END].reshape(B, L, N_KV_HEADS, HEAD_DIM)
        attn = windowed_gqa_sink(q, k, v, attn_sink[l])
        spec = hyena_filter_spectra(L, filt_w1[l], filt_b1[l], filt_freq1[l],
                                    filt_w2[l], filt_b2[l], filt_freq2[l], filt_w3[l])
        hy = hyena_branch(proj[..., V_END:HY_END], conv_w[l], conv_b[l], spec, hyena_bias[l])
        gate_a, gate_h = jnp.split(proj[..., HY_END:], 2, axis=-1)
        merged = (jax.nn.sigmoid(gate_a) * (attn @ w_attn_o[l])
                  + jax.nn.sigmoid(gate_h) * (hy @ w_hyena_o[l]))
        x = x + g1[:, None, :] * (merged @ w_out[l])
        h = modulate(rmsnorm(x, norm2_g[l]), sh2, sc2)
        x = x + g2[:, None, :] * (jnp.square(jax.nn.relu(h @ w_up[l])) @ w_down[l])
    shf, scf = jnp.split(c_act @ w_ada_final + b_ada_final, 2, axis=-1)
    return modulate(rmsnorm(x, final_g), shf, scf)

def setup_inputs(seed: int = 0) -> dict:
    key = jax.random.key(seed)
    ks = jax.random.split(key, 32)

    def nrm(k, shape, scale):
        return jax.random.normal(k, shape, jnp.float32) * scale

    return {
        'x_prompt': nrm(ks[0], (BATCH, SEQ, D_MODEL), 1.0),
        'x_sample': nrm(ks[1], (DEC_BATCH, DEC_SEQ, D_MODEL), 1.0),
        'c_prompt': nrm(ks[2], (BATCH, D_MODEL), 1.0),
        'c_sample': nrm(ks[3], (DEC_BATCH, D_MODEL), 1.0),
        'w_ada': nrm(ks[4], (DEPTH, D_MODEL, 6 * D_MODEL), 0.5 * D_MODEL ** -0.5),
        'b_ada': nrm(ks[5], (DEPTH, 6 * D_MODEL), 0.02),
        'norm1_g': 1.0 + nrm(ks[6], (DEPTH, D_MODEL), 0.05),
        'w_in': nrm(ks[7], (DEPTH, D_MODEL, IN_PROJ_WIDTH), D_MODEL ** -0.5),
        'attn_sink': nrm(ks[8], (DEPTH, N_Q_HEADS), 0.5),
        'conv_w': nrm(ks[9], (DEPTH, SHORT_CONV, (HYENA_ORDER + 1) * HYENA_WIDTH), SHORT_CONV ** -0.5),
        'conv_b': nrm(ks[10], (DEPTH, (HYENA_ORDER + 1) * HYENA_WIDTH), 0.02),
        'filt_w1': nrm(ks[11], (DEPTH, FILTER_EMB, FILTER_HIDDEN), FILTER_EMB ** -0.5),
        'filt_b1': nrm(ks[12], (DEPTH, FILTER_HIDDEN), 0.1),
        'filt_freq1': 1.0 + nrm(ks[13], (DEPTH, FILTER_HIDDEN), 0.05),
        'filt_w2': nrm(ks[14], (DEPTH, FILTER_HIDDEN, FILTER_HIDDEN), FILTER_HIDDEN ** -0.5),
        'filt_b2': nrm(ks[15], (DEPTH, FILTER_HIDDEN), 0.1),
        'filt_freq2': 1.0 + nrm(ks[16], (DEPTH, FILTER_HIDDEN), 0.05),
        'filt_w3': nrm(ks[17], (DEPTH, FILTER_HIDDEN, FILTER_OUT), 0.01),
        'hyena_bias': nrm(ks[18], (DEPTH, HYENA_ORDER, HYENA_WIDTH), 0.1),
        'w_attn_o': nrm(ks[19], (DEPTH, ATTN_WIDTH, D_MODEL), ATTN_WIDTH ** -0.5),
        'w_hyena_o': nrm(ks[20], (DEPTH, HYENA_WIDTH, D_MODEL), HYENA_WIDTH ** -0.5),
        'w_out': nrm(ks[21], (DEPTH, D_MODEL, D_MODEL), D_MODEL ** -0.5),
        'norm2_g': 1.0 + nrm(ks[22], (DEPTH, D_MODEL), 0.05),
        'w_up': nrm(ks[23], (DEPTH, D_MODEL, D_FF), D_MODEL ** -0.5),
        'w_down': nrm(ks[24], (DEPTH, D_FF, D_MODEL), D_FF ** -0.5),
        'w_ada_final': nrm(ks[25], (D_MODEL, 2 * D_MODEL), 0.5 * D_MODEL ** -0.5),
        'b_ada_final': nrm(ks[26], (2 * D_MODEL,), 0.02),
        'final_g': 1.0 + nrm(ks[27], (D_MODEL,), 0.05),
    }

def reference(x_prompt, x_sample, c_prompt, c_sample, w_ada, b_ada, norm1_g, w_in, attn_sink,
              conv_w, conv_b, filt_w1, filt_b1, filt_freq1, filt_w2, filt_b2, filt_freq2, filt_w3,
              hyena_bias, w_attn_o, w_hyena_o, w_out, norm2_g, w_up, w_down,
              w_ada_final, b_ada_final, final_g):
    weights = (w_ada, b_ada, norm1_g, w_in, attn_sink, conv_w, conv_b,
               filt_w1, filt_b1, filt_freq1, filt_w2, filt_b2, filt_freq2, filt_w3,
               hyena_bias, w_attn_o, w_hyena_o, w_out, norm2_g, w_up, w_down,
               w_ada_final, b_ada_final, final_g)
    y_prompt = run_trunk(x_prompt, c_prompt, *weights)
    y_sample = run_trunk(x_sample, c_sample, *weights)
    return (y_prompt, y_sample)


_drawn_inputs = setup_inputs


def setup_inputs(seed=0):
    import zlib

    import numpy as np

    out = dict(_drawn_inputs(seed))
    spreads = {}
    factors = {'norm1_g': 8.0,
     'attn_sink': 8.0,
     'conv_b': 6.709,
     'filt_freq1': 8.0,
     'filt_freq2': 8.0,
     'hyena_bias': 5.27,
     'norm2_g': 8.0,
     'w_up': 6.626,
     'w_down': 6.023}
    for name, (base, spread) in spreads.items():
        noise = np.random.default_rng([zlib.crc32(name.encode()), seed]).standard_normal(out[name].shape)
        drawn = base * np.exp(spread * noise) if base else spread * noise
        out[name] = jnp.asarray(drawn.astype(out[name].dtype))
    for name, factor in factors.items():
        out[name] = (out[name] * factor).astype(out[name].dtype)
    return out
```

```python
from contextlib import ExitStack

import concourse.bass as bass
from concourse import mybir

F32 = mybir.dt.float32
F32R = mybir.dt.float32r
ALU = mybir.AluOpType
ACT = mybir.ActivationFunctionType

P = 128
D = 1024
KD = D // P
TS, TP = 512, 256
T = TS + TP
NTB = T // P
GROUPS = ((0, TS), (TS, TP))
HD = 64
NJ = 4
QKV = 768
HY0 = QKV
HW = 512
GATE0 = HY0 + 3 * HW
DFF = 4 * D
NCH = DFF // D
EPS = 1e-6
PI = 3.141592653589793
TWO_PI_A = 6.28125
TWO_PI_B = 0.0019350051879882812
TWO_PI_C = 2 * PI - TWO_PI_A - TWO_PI_B
MAGIC = 12582912.0

T_HY, T_Q, T_K, T_V, T_GATE, T_MERGE, T_OUT, T_MLP = 0, 12, 16, 17, 18, 34, 42, 50
A_MERGE, A_OUT, A_MLP = 34, 50, 58
MOD_A = 8
MOD_N = 32
SH1, SC1, G1, SH2, SC2, G2, SHF, SCF = (8 * i for i in range(8))

V_C, V_N1, V_N2, V_NF, V_HB, V_BA, V_CB, V_N = 0, 16, 24, 32, 40, 48, 112, 124

UNITS = ((0, 0, 2), (0, 2, 2), (1, 0, 4))
STEPS = [(u, r) for r in range(2) for u in range(3)]
ATT = [(qb, kv) for qb in range(NTB) for kv in range(2)]


def att_keys(qb):
    lo, hi = (0, 4) if qb < 4 else (4, 6)
    first, last = max(qb - 1, lo), min(qb + 1, hi - 1)
    return first, last - first + 1, P * (first - qb + 1)


def program(nc, a, out_p, out_s):
    with ExitStack() as ctx:
        def sem(name):
            return ctx.enter_context(nc.semaphore(name))

        def region(*layouts, keep=None):
            got = []
            for layout in layouts[:-1]:
                with ExitStack() as e:
                    got.append([e.enter_context(nc.sbuf_tensor(*t)) for t in layout])
            got.append([ctx.enter_context(nc.sbuf_tensor(*t)) for t in layouts[-1]])
            return got

        def sb(name, shape, dt=F32):
            return ctx.enter_context(nc.sbuf_tensor(name, shape, dt))

        raw = [sb(f"w_raw{i}", [P, KD, P]) for i in range(2)]
        whi = [sb(f"w_hi{i}", [P, KD, P], F32R) for i in range(2)]
        wlo = [sb(f"w_lo{i}", [P, KD, P], F32R) for i in range(2)]
        (w3, w3eo, ftab, dec, taps), (tabF, tabI, tabFp, tabIp, eo, eoT, Y, cm, spec), (act,) = region(
            [("filt_w3", [64, 2048], F32), ("filt_w3eo", [64, 2, 1024], F32), ("filt_tab", [P, 4, 2, 256], F32),
             ("filt_decay", [P, 4, 512], F32), ("filt_taps", [P, 2, 4, 512], F32)],
            [("dft_fwd", [P, 4, 2, 256], F32), ("dft_inv", [P, 4, 2, 256], F32), ("dft_fwd_p", [P, 4, P], F32),
             ("dft_inv_p", [P, 4, P], F32), ("hy_fold", [P, 1024], F32), ("hy_foldT", [P, 1024], F32),
             ("hy_prod", [P, 4, 2, 256], F32), ("hy_cross", [P, 1024], F32), ("hy_spec", [P, 2, 4, 256], F32)],
            [("act_hilo", [P, 2, KD, T], F32R)])
        (zh, fa, fb, fk, h1, fout, sqA, accA, rstdA, tnA, hfA), (cos, sin, rt, vtmp), (gates,), (hid,) = region(
            [("filt_zh", [64, T], F32), ("filt_arg", [64, T], F32), ("filt_red", [64, T], F32),
             ("filt_turn", [64, T], F32), ("filt_h1", [64, T], F32), ("filt_out", [P, 2, 2, 512], F32),
             ("n0_sq", [P, T], F32), ("n0_acc", [P, T], F32), ("n0_rstd", [P, T], F32),
             ("n0_t", [P, 2, T], F32), ("n0_h", [P, 2, T], F32)],
            [("rope_cos", [P, T], F32), ("rope_sin", [P, T], F32), ("rope_rot", [P, T], F32),
             ("v_tmp", [P, T], F32)],
            [("gates", [P, 16, T], F32)],
            [("hidden_hilo", [P, 2, KD, T], F32R)])
        (modB,), (S, PT), (xT,) = region(
            [("mod_ringB", [P, 3, KD, 256], F32)],
            [("att_s", [P, 2, NJ, 384], F32), ("att_pT", [P, 2, 3, NJ * P], F32)],
            [("xT", [P, KD, T], F32)])
        (modA, xnat, ftab_p, dec_p), (xv, qk, V), (tmp, sqB, accB, rstdB, tnB, hfB, onat) = region(
            [("mod_ringA", [P, 3, KD, 256], F32), ("x_rows", [P, NTB, D], F32), ("filt_tab_p", [P, 4, P], F32),
             ("filt_decay_p", [P, 2, 512], F32)],
            [("hy_xv", [P, 12, T], F32), ("qk", [P, 5, T], F32), ("v_rows", [P, NTB, P], F32)],
            [("ev_tmp", [P, 3, T], F32), ("n_sq", [P, T], F32), ("n_acc", [P, T], F32), ("n_rstd", [P, T], F32),
             ("n_t", [P, 2, T], F32), ("n_h", [P, 2, T], F32), ("y_rows", [P, NTB, D], F32)])
        NB = [(sqA, accA, rstdA, tnA, hfA), (sqB, accB, rstdB, tnB, hfB), (sqB, accB, rstdB, tnB, hfB)]

        ident = sb("ident", [P, P])
        ones = sb("ones", [P, P])
        rot = sb("rope_perm", [P, P])
        mask = sb("mask", [P, 384])
        vrow = sb("vec_rows", [P, P])
        vrow2 = sb("conv_rows", [36, P])
        vT = sb("vecT", [P, V_N])
        cwT = sb("conv_wT", [P, 36])
        csig = sb("c_sig", [P, 16])
        cact = sb("c_act", [P, 16])
        modT = sb("modT", [P, 64, 2])
        asc = sb("norm_scale", [P, 3, KD, 2])
        fE = sb("filt_even", [P, 512])
        fw1 = sb("filt_w1", [33, 64])
        fw2 = sb("filt_w2", [64, 64])
        fv = sb("filt_vec", [64, 4])
        sink = sb("sink", [P, 8])
        mx = sb("att_max", [P, 2, NJ])
        nmx = sb("att_negmax", [P, 2, NJ])
        sd = sb("att_sinkd", [P, 2, NJ])
        es = sb("att_sinke", [P, 2, NJ])
        den = sb("att_den", [P, 2, NJ])
        rden = sb("att_rden", [P, 2, NJ])
        epsc = sb("eps", [P, 1])

        acc_ps = ctx.enter_context(nc.psum_tensor("acc_ps", [P, 2, 1024], F32))
        wk = ctx.enter_context(nc.psum_tensor("wk", [P, 2048], F32))

        xT_d = nc.dram_tensor("xT_spill", [P, KD * T], F32).ap()
        spec_d = [nc.dram_tensor(f"spec{g}", [2, 2, P, (4, 2)[g] * 512], F32).ap() for g in range(2)]

        landed = [sem(f"w_landed{i}") for i in range(2)]
        hi_done, lo_done = sem("w_hi_done"), sem("w_lo_done")
        acc_ready = sem("acc_ready")
        acc_free = [sem(f"acc_free{i}") for i in range(2)]
        ld_vec, ld_filt, ld_filt2, ld_rope, ld_tab, ld_x2 = (
            sem(n) for n in ("ld_vec", "ld_filt", "ld_filt2", "ld_rope", "ld_tab", "ld_xback"))
        ld_x = [sem(f"ld_x{i}") for i in range(NTB)]
        ld_mod = [sem(f"ld_mod{i}") for i in range(6)]
        ones_set = sem("ones_set")
        vt_ready, vt_copied, csig_done, cact_done = (sem(n) for n in ("vt_ready", "vt_copied", "csig", "cact"))
        xt_ready, xt_copied, xt_spilled = sem("xt_ready"), sem("xt_copied"), sem("xt_spilled")
        fm_ready, f_arg, f_sin, w3_sum = sem("fm_ready"), sem("f_arg"), sem("f_sin"), sem("w3_sum")
        f_ready, f_free, f_even = sem("f_ready"), sem("f_free"), sem("f_even")
        f_stored = [sem(f"f_stored{i}") for i in range(2)]
        mod_used, mod_done, asc_done = sem("mod_used"), sem("mod_done"), sem("asc_done")
        n_sq, n_acc, n_ps, n_std, n_rstd, n_t, n_hf, n_hi, n_lo = (
            sem(n) for n in ("n_sq", "n_acc", "n_ps", "n_std", "n_rstd", "n_t", "n_hf", "n_hi", "n_lo"))
        cv_mid, cv_part = sem("cv_mid"), sem("cv_part")
        rot_ready, rope_step, rope_done = sem("rot_ready"), sem("rope_step"), sem("rope_done")
        v_turned, v_rows = sem("v_turned"), sem("v_rows_done")
        fold_done, turn_ready, turn_copied = sem("fold_done"), sem("turn_ready"), sem("turn_copied")
        ld_spec, fwd_ready, cross_step, prod_done = (
            sem(n) for n in ("ld_spec", "fwd_ready", "cross_step", "prod_done"))
        inv_ready, inv_copied, y_done, y_step, z_done = (
            sem(n) for n in ("inv_ready", "inv_copied", "y_done", "y_step", "z_done"))
        s_ready, s_max, s_neg, s_sd, s_es, s_exp, s_den, s_rden, s_norm = (
            sem(n) for n in ("s_ready", "s_max", "s_neg", "s_sd", "s_es", "s_exp", "s_den", "s_rden", "s_norm"))
        p_ready, p_copied, o_ready, o_copied = (sem(n) for n in ("p_ready", "p_copied", "o_ready", "o_copied"))
        sp_hi, sp_lo = sem("sp_hi"), sem("sp_lo")
        f_step, rope_mul = sem("f_step"), sem("rope_mul")
        mg_done, mg_hi, mg_lo = sem("mg_done"), sem("mg_hi"), sem("mg_lo")
        up_sq, hid_hi, hid_lo = sem("up_sq"), sem("hid_hi"), sem("hid_lo")
        y_turned, y_copied, stored = sem("y_turned"), sem("y_copied"), sem("stored")

        def uses_to(t):
            if not isinstance(t, int) or t >= T_OUT:
                return t + A_OUT - T_OUT + 1
            return t + 1 if t < T_MERGE else A_MERGE + 2 * (t - T_MERGE) + 2

        n_dma = [2 if T_Q <= t < T_K else 3 if T_MERGE <= t < T_OUT else 1 for t in range(T_MLP)]
        landed_at = [16 * sum(n_dma[t % 2:t + 1:2]) for t in range(T_MLP)]
        landed_base = [sum(n_dma[s::2]) for s in range(2)]

        w_in = a["w_in"][0].rearrange("(k p) n -> p k n", p=P)
        w_ada = a["w_ada"][0].rearrange("(k p) n -> p k n", p=P)
        w_adaf = a["w_ada_final"].rearrange("(k p) n -> p k n", p=P)
        w_ao = a["w_attn_o"][0].rearrange("(h j p) n -> h p j n", h=2, p=HD)
        w_ho = a["w_hyena_o"][0].rearrange("(k p) n -> p k n", p=P)
        w_out = a["w_out"][0].rearrange("(k p) n -> p k n", p=P)
        w_up = a["w_up"][0].rearrange("(k p) n -> p k n", p=P)
        w_down = a["w_down"][0].rearrange("(c k p) n -> p c k n", k=KD, p=P)

        FU, tap_end, spec_end = [], {}, {}
        for g in range(2):
            for r in range(2):
                FU += [(g, r, 0, e, mp) for e in range(2) for mp in range(2 - g)]
                tap_end[g, r] = len(FU)
                FU += [(g, r, 1, pq, kt) for pq in range(2) for kt in range(2 - g)]
                spec_end[g, r] = len(FU)

        s_bank, p_bank, p_first, bank_reader = {0: 0}, {}, {}, [(s_max, j + 1) for j in range(NJ)]
        for n in range(len(ATT)):
            if n + 1 < len(ATT):
                s_bank[n + 1] = len(bank_reader)
                bank_reader += [(s_max, NJ * (n + 1) + j + 1) for j in range(NJ)]
            p_first[n] = sum(att_keys(q)[1] for q, _ in ATT[:n])
            p_bank[n] = len(bank_reader)
            bank_reader += [(p_copied, p_first[n] + kb + 1) for kb in range(att_keys(ATT[n][0])[1])]

        block = ctx.enter_context(nc.Block())

        @block.sync
        def _(sp):
            def weights(t):
                s = t % 2
                if t >= 2:
                    sp.wait_ge(hi_done, t - 1)
                    sp.wait_ge(lo_done, t - 1)
                if t < T_Q:
                    parts = [(raw[s][:], w_in[:, :, HY0 + P * t:HY0 + P * t + P])]
                elif t < T_K:
                    j = t - T_Q
                    parts = [(raw[s][:, :, HD * h:HD * h + HD],
                              w_in[:, :, (NJ * h + j) * HD:(NJ * h + j + 1) * HD]) for h in range(2)]
                elif t < T_GATE:
                    c = 2 * NJ * HD + P * (t - T_K)
                    parts = [(raw[s][:], w_in[:, :, c:c + P])]
                elif t < T_MERGE:
                    c = GATE0 + P * (t - T_GATE)
                    parts = [(raw[s][:], w_in[:, :, c:c + P])]
                elif t < T_OUT:
                    c = P * (t - T_MERGE)
                    parts = [(raw[s][HD * h:HD * h + HD, 0:4, :], w_ao[h, :, :, c:c + P]) for h in range(2)]
                    parts.append((raw[s][:, 4:8, :], w_ho[:, :, c:c + P]))
                else:
                    c = P * (t - T_OUT)
                    parts = [(raw[s][:], w_out[:, :, c:c + P])]
                for dst, src in parts:
                    sp.dma_start(dst, src).then_inc(landed[s], 16)

            def mod_load(c):
                src = w_ada[:, :, 256 * c:256 * c + 256] if c < 24 else w_adaf[:, :, 256 * (c - 24):256 * (c - 23)]
                if c < MOD_A:
                    if c >= 3:
                        sp.wait_ge(mod_used, c - 2)
                    sp.dma_start(modA[:, c % 3], src).then_inc(ld_mod[c % 3], 16)
                else:
                    b = c - MOD_A
                    if b >= 3:
                        sp.wait_ge(mod_used, c - 2)
                    sp.dma_start(modB[:, b % 3], src).then_inc(ld_mod[3 + b % 3], 16)

            for b in range(NTB):
                src = a["x_sample"][0, P * b:P * b + P, :] if b < 4 else a["x_prompt"][0, P * (b - 4):P * (b - 3), :]
                sp.dma_start(xnat[:, b], src).then_inc(ld_x[b], 16)
            for c in range(3):
                mod_load(c)
            weights(0)
            weights(1)
            sp.wait_ge(xt_copied, 12)
            sp.dma_start(xT_d, xT[:].rearrange("p k n -> p (k n)")).then_inc(xt_spilled, 16)
            for c in range(3, MOD_A):
                mod_load(c)
            sp.wait_ge(xt_spilled, 16)
            sp.wait_ge(n_t, KD)
            for t in range(2, T_MERGE + 2):
                c = MOD_A + t - 2
                if c < MOD_N:
                    mod_load(c)
                weights(t)
                if t == 4:
                    sp.wait_ge(n_lo, KD)
                    sp.wait_ge(f_stored[0], 16 * 6)
                    sp.wait_ge(f_stored[1], 16 * 6)
                    sp.dma_start(cos[:], a["t_cos"]).then_inc(ld_rope, 16)
                    sp.dma_start(sin[:], a["t_sin"]).then_inc(ld_rope, 16)
            sp.wait_ge(acc_ready, T_MERGE)
            for n, (u, r) in enumerate(STEPS):
                g, ct0, nct = UNITS[u]
                if n >= 1:
                    sp.wait_ge(prod_done, 4 * n)
                for pq in range(2):
                    src = spec_d[g][r, pq]
                    if g == 0:
                        src = src.rearrange("p (b n) -> p b n", b=4)[:, :, P * ct0:P * ct0 + 256]
                    else:
                        src = src.rearrange("p (b n) -> p b n", b=4)
                    sp.dma_start(spec[:, pq], src).then_inc(ld_spec, 16)
                if n == 0:
                    for dst, name in ((tabF, "t_fwd_s"), (tabFp, "t_fwd_p"), (tabI, "t_inv_s"), (tabIp, "t_inv_p")):
                        sp.dma_start(dst[:], a[name]).then_inc(ld_tab, 16)
                    weights(T_MERGE + 2)
                    weights(T_MERGE + 3)
            sp.wait_ge(o_copied, len(ATT))
            sp.dma_start(xT[:].rearrange("p k n -> p (k n)"), xT_d).then_inc(ld_x2, 16)
            for t in range(T_MERGE + 4, T_MLP):
                weights(t)
            with sp.Fori(0, NCH) as c:
                with sp.Fori(0, KD // 2) as i:
                    for s in range(2):
                        t = T_MLP + c * 16 + i * 2 + s
                        sp.wait_ge(hi_done, t - 1)
                        sp.wait_ge(lo_done, t - 1)
                        sp.dma_start(raw[s][:], w_up[:, :, bass.ds(c * D + i * 256 + s * P, P)]).then_inc(landed[s], 16)
                with sp.Fori(0, KD // 2) as i:
                    for s in range(2):
                        t = T_MLP + KD + c * 16 + i * 2 + s
                        sp.wait_ge(hi_done, t - 1)
                        sp.wait_ge(lo_done, t - 1)
                        sp.dma_start(raw[s][:], w_down[:, bass.ds(c, 1), :, bass.ds(i * 256 + s * P, P)]
                                     .rearrange("p c k n -> p (c k) n")).then_inc(landed[s], 16)
            for half in range(2):
                sp.wait_ge(y_copied, 4 * half + 4)
                c = slice(512 * half, 512 * half + 512)
                sp.dma_start(out_s[0].rearrange("(b p) n -> p b n", p=P)[:, :, c], onat[:, 0:4, c]).then_inc(stored, 16)
                sp.dma_start(out_p[0].rearrange("(b p) n -> p b n", p=P)[:, :, c], onat[:, 4:6, c]).then_inc(stored, 16)
            sp.wait_ge(stored, 64)

        @block.gpsimd
        def _(pool):
            pool.dma_start(zh[0:33, :], a["t_z"]).then_inc(ld_filt, 16)
            pool.dma_start(fw1[:], a["filt_w1"][0]).then_inc(ld_filt, 16)
            pool.dma_start(fw2[:], a["filt_w2"][0]).then_inc(ld_filt, 16)
            for i, n in enumerate(("filt_b1", "filt_freq1", "filt_b2", "filt_freq2")):
                pool.dma_start(fv[:, i:i + 1], a[n].rearrange("o f -> f o")).then_inc(ld_filt, 16)
            pool.dma_start(w3[:], a["filt_w3"][0]).then_inc(ld_filt2, 16)
            pool.dma_start(dec[:], a["t_decay_s"]).then_inc(ld_filt2, 16)
            pool.dma_start(ftab[:], a["t_filt_s"]).then_inc(ld_filt2, 16)
            pool.dma_start(dec_p[:], a["t_decay_p"]).then_inc(ld_filt2, 16)
            pool.dma_start(ftab_p[:], a["t_filt_p"]).then_inc(ld_filt2, 16)
            pool.memset(ones[:], 1.0).then_inc(ones_set, 1)
            pool.memset(epsc[:], EPS).then_inc(ones_set, 1)
            e = 0
            for f, (g, r, kind, pq, kt) in enumerate(FU):
                if kind == 1:
                    pool.wait_ge(f_free, f + 1)
                    dst = spec_d[g][r, pq].rearrange("p (s k n) -> p s k n", s=2, n=512)[:, :, kt, :]
                    pool.dma_start(dst, fout[:, e % 2]).then_inc(f_stored[e % 2], 16)
                    e += 1

            def fold(n):
                u, r = STEPS[n]
                g, ct0, nct = UNITS[u]
                c0, L = GROUPS[g]
                src = xv[:, 8 + ct0:8 + ct0 + nct, c0:c0 + L]
                back = src[:, :, ::-1]
                e4 = eo[:].rearrange("p (c e n) -> p c e n", e=2, n=L // 2)
                if n == 0:
                    for s in range(2):
                        pool.wait_ge(acc_free[s], T_Q // 2)
                    pool.wait_ge(acc_ready, T_MERGE)
                if n >= 1:
                    pool.wait_ge(turn_ready, n)
                if n >= 2:
                    pool.wait_ge(y_done, n - 1)
                if r == 1:
                    pool.wait_ge(z_done, n - 2)
                for i, op in enumerate((ALU.add, ALU.subtract)):
                    last = pool.tensor_tensor(e4[:, :, i, :], src[:, :, 0:L // 2], back[:, :, 0:L // 2], op)
                last.then_inc(fold_done, 1)

            def unfold(n):
                u, r = STEPS[n]
                g, ct0, nct = UNITS[u]
                L = GROUPS[g][1]
                y4 = eo[:].rearrange("p (c e n) -> p c e n", e=2, n=L // 2)
                full = cm[:].rearrange("p (c n) -> p c n", n=L)
                pool.wait_ge(inv_copied, n + 1)
                pool.wait_ge(prod_done, 4 * n + 4)
                pool.tensor_tensor(full[:, :, 0:L // 2], y4[:, :, 0, :], y4[:, :, 1, :], ALU.add)
                pool.tensor_tensor(full[:, :, ::-1][:, :, 0:L // 2], y4[:, :, 0, :], y4[:, :, 1, :],
                                   ALU.subtract).then_inc(y_done, 1)

            fold(0)
            for n in range(len(STEPS)):
                if n + 1 < len(STEPS):
                    fold(n + 1)
                unfold(n)

        @block.tensor
        def _(pe):
            def gemm_k(slot, s, k, kw, src, first, last):
                for i, (w, x) in enumerate(((whi[s], 0), (whi[s], 1), (wlo[s], 0))):
                    for c0, L in GROUPS:
                        mm = pe.matmul(acc_ps[:, slot, c0:c0 + L], w[:, kw, :], src[:, x, k, c0:c0 + L],
                                       start=(first and i == 0), stop=(last and i == 2))
                return mm

            def gemm(t, src, parts=None, k_waits=()):
                s = t % 2
                pe.wait_ge(hi_done, t + 1)
                pe.wait_ge(lo_done, t + 1)
                parts = parts or [(t, range(KD))]
                for a_i, ks in parts:
                    if a_i >= 2:
                        pe.wait_ge(acc_free[a_i % 2], a_i // 2)
                    for k in ks:
                        for sm, base in k_waits:
                            pe.wait_ge(sm, base + k)
                        mm = gemm_k(a_i % 2, s, k, k, src, k == ks[0], k == ks[-1])
                    if ks[-1] != KD - 1:
                        mm.then_inc(acc_ready, 1)
                mm.then_inc(acc_ready, 1)

            def mod_chunk(c):
                ring, sm, i = (modA, 0, c) if c < MOD_A else (modB, 3, c - MOD_A)
                pe.wait_ge(ld_mod[sm + i % 3], 16 * (i // 3 + 1))
                if c >= 1:
                    pe.wait_ge(mod_done, c)
                for j in range(2):
                    for k in range(KD):
                        mm = pe.matmul(wk[:, 1536 + 2 * (2 * c + j):1536 + 2 * (2 * c + j) + 2],
                                       ring[:, i % 3, k, P * j:P * j + P], cact[:, k::KD],
                                       start=(k == 0), stop=(k == KD - 1))
                mm.then_inc(mod_used, 1)

            def norm_sum(q):
                pe.wait_ge(n_acc, KD * q + KD)
                for c0, L in GROUPS:
                    mm = pe.matmul(wk[:, c0:c0 + L], ones[:], NB[q][1][:, c0:c0 + L], start=True, stop=True)
                mm.then_inc(n_ps, 1)

            pe.wait_ge(ld_vec, 16 * 12)
            pe.transpose(wk[:, 1024:1024 + V_N], vrow[0:V_N, :], ident[0:V_N, 0:V_N])
            pe.transpose(wk[:, 1280:1316], vrow2[:], ident[0:36, 0:36]).then_inc(vt_ready, 1)

            def filt_mlp(layer):
                for c0, L in GROUPS:
                    if layer == 0:
                        mm = pe.matmul(acc_ps[0:64, 0, c0:c0 + L], fw1[:], zh[0:33, c0:c0 + L], start=True, stop=True)
                    else:
                        mm = pe.matmul(acc_ps[0:64, 1, c0:c0 + L], fw2[:], h1[:, c0:c0 + L], start=True, stop=True)
                mm.then_inc(fm_ready, 1)

            def turn_x(u):
                b, h = u // 2, u % 2
                pe.wait_ge(ld_x[b], 16)
                if u >= 2:
                    pe.wait_ge(xt_copied, u - 1)
                for k in range(4):
                    mm = pe.transpose(wk[:, 512 * (u % 2) + P * k:512 * (u % 2) + P * k + P],
                                      xnat[:, b, P * (4 * h + k):P * (4 * h + k) + P], ident[:])
                mm.then_inc(xt_ready, 1)

            pe.wait_ge(ld_filt, 16 * 7)
            filt_mlp(0)
            for u in range(6):
                turn_x(u)
            pe.wait_ge(f_sin, 1)
            filt_mlp(1)
            for u in range(6, 12):
                turn_x(u)
            pe.wait_ge(f_sin, 2)
            pe.wait_ge(w3_sum, 1)
            pe.wait_ge(ld_filt2, 16 * 5)
            for f, (g, r, kind, p, q) in enumerate(FU):
                c0, L = GROUPS[g]
                n_e = 2 - g
                if f >= 2:
                    pe.wait_ge(f_free, f - 1)
                if kind == 0:
                    for j in range(2):
                        m = 2 * q + j
                        odd, jj = (m // n_e, m % n_e)
                        t0 = c0 + 256 * jj + odd
                        mm = pe.matmul(acc_ps[:, f % 2, 512 * j:512 * j + 512], zh[:, t0:t0 + 255:2],
                                       w3eo[:, p, 512 * r:512 * r + 512], start=True, stop=True)
                else:
                    pe.wait_ge(f_free, tap_end[g, r])
                    tab = ftab if g == 0 else ftab_p[:].rearrange("p m (j n) -> p m j n", j=1)
                    for odd in range(2):
                        for j in range(n_e):
                            mm = pe.matmul(acc_ps[:, f % 2, 512 * odd:512 * odd + 512],
                                           tab[:, 2 * p + odd, j, P * q:P * q + P], taps[:, p, odd * n_e + j, :],
                                           start=(j == 0), stop=(j == n_e - 1))
                mm.then_inc(f_ready, 1)
            pe.wait_ge(cact_done, 1)
            for c in range(MOD_A):
                mod_chunk(c)
            pe.wait_ge(ones_set, 2)
            norm_sum(0)
            pe.wait_ge(f_free, len(FU))

            def rope_turn(j):
                pe.wait_ge(acc_free[(T_Q + j) % 2], (T_Q + j) // 2 + 1)
                if j >= 1:
                    pe.wait_ge(rope_step, j)
                for c0, L in GROUPS:
                    mm = pe.matmul(wk[:, c0:c0 + L], rot[:], qk[:, j, c0:c0 + L], start=True, stop=True)
                mm.then_inc(rot_ready, 1)

            for t in range(T_MERGE):
                gemm(t, act, k_waits=((n_hi, 1), (n_lo, 1)) if t == 0 else ())
                if t < MOD_N - MOD_A:
                    mod_chunk(MOD_A + t)
                if T_Q < t <= T_V:
                    rope_turn(t - 1 - T_Q)
                if t == T_GATE:
                    pe.wait_ge(acc_free[T_V % 2], T_V // 2 + 1)
                    pe.wait_ge(rope_step, 5)
                    for b in range(NTB):
                        mm = pe.transpose(wk[:, P * b:P * b + P], vtmp[:, P * b:P * b + P], ident[:])
                    mm.then_inc(v_turned, 1)

            def bank_next(b):
                if b >= 3:
                    pe.wait_ge(*bank_reader[b - 3])
                return 512 * (b % 3)

            def scores(n):
                qb, kv = ATT[n]
                first, nk, _ = att_keys(qb)
                h = slice(HD * kv, HD * kv + HD)
                for j in range(NJ):
                    c = bank_next(s_bank[n] + j)
                    pe.matmul(wk[:, c:c + P * nk], qk[h, j, P * qb:P * qb + P], qk[h, 4, P * first:P * (first + nk)],
                              start=True, stop=True).then_inc(s_ready, 1)

            def values(n):
                qb, kv = ATT[n]
                first, nk, _ = att_keys(qb)
                pe.wait_ge(s_norm, n + 1)
                done = p_first[n]
                for kb in range(nk):
                    c = bank_next(p_bank[n] + kb)
                    for j in range(NJ):
                        mm = pe.transpose(wk[:, c + P * j:c + P * j + P], S[:, n % 2, j, P * kb:P * kb + P], ident[:])
                    mm.then_inc(p_ready, 1)
                if n >= 1:
                    pe.wait_ge(o_copied, n)
                for kb in range(nk):
                    pe.wait_ge(p_copied, done + kb + 1)
                    mm = pe.matmul(wk[:, 1536:2048], V[:, first + kb, :], PT[:, n % 2, kb, :],
                                   start=(kb == 0), stop=(kb == nk - 1))
                mm.then_inc(o_ready, 1)

            def turn(n):
                g, _, nct = UNITS[STEPS[n][0]]
                h = GROUPS[g][1] // 2
                e4 = eo[:].rearrange("p (c e n) -> p c e n", e=2, n=h)
                pe.wait_ge(fold_done, n + 1)
                if n >= 1:
                    pe.wait_ge(prod_done, 4 * n - 2)
                for e in range(2):
                    for j in range(h // P):
                        for ct in range(nct):
                            mm = pe.transpose(
                                acc_ps[:, 0, 512 * e + j * 256 + P * ct:512 * e + j * 256 + P * ct + P],
                                e4[:, ct, e, P * j:P * j + P], ident[:])
                mm.then_inc(turn_ready, 1)

            def forward(n):
                g, _, nct = UNITS[STEPS[n][0]]
                pe.wait_ge(turn_copied, n + 1)
                for b in range(4):
                    if b == 2 and n >= 1:
                        pe.wait_ge(inv_copied, n)
                    ks, x = b // 2, b % 2
                    for d in range(2):
                        e = ks ^ d
                        o = acc_ps[:, b // 2, 512 * (b % 2) + 256 * d:512 * (b % 2) + 256 * d + 256]
                        if g == 0:
                            for j in range(2):
                                mm = pe.matmul(o, tabF[:, 2 * ks + d, j, P * x:P * x + P],
                                               eoT[:, 512 * e + 256 * j:512 * e + 256 * j + 256],
                                               start=(j == 0), stop=(j == 1))
                        else:
                            mm = pe.matmul(o, tabFp[:, 2 * ks + d, :], eoT[:, 512 * e + 256 * x:512 * e + 256 * x + 256],
                                           start=True, stop=True)
                    mm.then_inc(fwd_ready, 1)

            def inverse(n):
                g, _, nct = UNITS[STEPS[n][0]]
                pe.wait_ge(prod_done, 4 * n + 4)
                for ct in range(nct):
                    for part in range(2):
                        if g == 0:
                            o = acc_ps[:, 1, 512 * ct + 256 * part:512 * ct + 256 * part + 256]
                            terms = [(Y[:, 2 * ks + kt, ks ^ part, P * ct:P * ct + P], tabI[:, 2 * ks + (ks ^ part), kt, :])
                                     for ks in range(2) for kt in range(2)]
                        else:
                            o = acc_ps[:, 1, 256 * ct + P * part:256 * ct + P * part + P]
                            terms = [(Y[:, 2 * ks + ct // 2, ks ^ part, P * (ct % 2):P * (ct % 2) + P],
                                      tabIp[:, 2 * ks + (ks ^ part), :]) for ks in range(2)]
                        for i, (w, x) in enumerate(terms):
                            mm = pe.matmul(o, w, x, start=(i == 0), stop=(i == len(terms) - 1))
                mm.then_inc(inv_ready, 1)

            pe.wait_ge(rope_done, 5)
            pe.wait_ge(v_rows, 1)
            pe.wait_ge(mod_done, MOD_N)
            scores(0)
            for s in range(2):
                pe.wait_ge(acc_free[s], T_MERGE // 2)
            turn(0)
            pe.wait_ge(ld_tab, 16 * 4)
            for n in range(len(STEPS)):
                forward(n)
                scores(2 * n + 1)
                values(2 * n)
                if n + 1 < len(STEPS):
                    turn(n + 1)
                inverse(n)
                if 2 * n + 2 < len(ATT):
                    scores(2 * n + 2)
                values(2 * n + 1)

            pe.wait_ge(inv_copied, len(STEPS))
            for m in range(KD):
                gemm(T_MERGE + m, act, parts=[(A_MERGE + 2 * m, range(4)), (A_MERGE + 2 * m + 1, range(4, 8))],
                     k_waits=((sp_hi, 1), (sp_lo, 1)) if m == 0 else ())
            for m in range(KD):
                gemm(T_OUT + m, hid, parts=[(A_OUT + m, range(KD))],
                     k_waits=((mg_hi, 1), (mg_lo, 1)) if m == 0 else ())
            norm_sum(1)

            with pe.Fori(0, NCH) as c:
                with pe.Fori(0, KD // 2) as i:
                    for s in range(2):
                        pe.wait_ge(hi_done, T_MLP + 1 + c * 16 + i * 2 + s)
                        pe.wait_ge(lo_done, T_MLP + 1 + c * 16 + i * 2 + s)
                        pe.wait_ge(acc_free[s], A_MLP // 2 + c * 8 + i)
                        for k in range(KD):
                            if s == 0:
                                pe.wait_ge(n_hi, KD + k + 1)
                                pe.wait_ge(n_lo, KD + k + 1)
                            mm = gemm_k(s, s, k, k, act, k == 0, k == KD - 1)
                        mm.then_inc(acc_ready, 1)
                with pe.Fori(0, KD // 2) as i:
                    for s in range(2):
                        pe.wait_ge(hi_done, T_MLP + KD + 1 + c * 16 + i * 2 + s)
                        pe.wait_ge(lo_done, T_MLP + KD + 1 + c * 16 + i * 2 + s)
                        pe.wait_ge(acc_free[s], A_MLP // 2 + KD // 2 + c * 8 + i)
                        for k in range(KD):
                            if s == 0 and k in (0, KD - 2, KD - 1):
                                need = KD - 2 if k == 0 else k + 1
                                pe.wait_ge(hid_hi, need + c * 8)
                                pe.wait_ge(hid_lo, need + c * 8)
                            mm = gemm_k(s, s, k, k, hid, k == 0, k == KD - 1)
                        mm.then_inc(acc_ready, 1)
            norm_sum(2)
            for s in range(2):
                pe.wait_ge(acc_free[s], A_MLP // 2 + 32)
            for k in range(KD):
                pe.wait_ge(n_hf, 32 + 2 * k + 2)
                if k >= 2:
                    pe.wait_ge(y_copied, k - 1)
                for b in range(NTB):
                    mm = pe.transpose(acc_ps[:, k % 2, P * b:P * b + P], hfB[:, k % 2, P * b:P * b + P], ident[:])
                mm.then_inc(y_turned, 1)

        @block.scalar
        def _(act_e):
            r0 = 0
            for src, n in ((a["c_sample"], 8), (a["c_prompt"], 8), (a["norm1_g"], 8), (a["norm2_g"], 8)):
                act_e.dma_start(vrow[r0:r0 + n, :], src.rearrange("o (k p) -> (o k) p", p=P)).then_inc(ld_vec, 16)
                r0 += n
            act_e.dma_start(vrow[V_NF:V_HB, :], a["final_g"].rearrange("(k p) -> k p", p=P)).then_inc(ld_vec, 16)
            act_e.dma_start(vrow[V_HB:V_BA, :], a["hyena_bias"][0].rearrange("o (k p) -> (o k) p", p=P)).then_inc(ld_vec, 16)
            act_e.dma_start(vrow[V_BA:V_BA + 48, :], a["b_ada"].rearrange("o (k p) -> (o k) p", p=P)).then_inc(ld_vec, 16)
            act_e.dma_start(vrow[V_BA + 48:V_CB, :], a["b_ada_final"].rearrange("(k p) -> k p", p=P)).then_inc(ld_vec, 16)
            act_e.dma_start(vrow[V_CB:V_N, :], a["conv_b"].rearrange("o (k p) -> (o k) p", p=P)).then_inc(ld_vec, 16)
            act_e.dma_start(vrow2[:], a["conv_w"][0].rearrange("i (k p) -> (i k) p", p=P)).then_inc(ld_vec, 16)
            act_e.dma_start(ident[:], a["t_ident"]).then_inc(ld_vec, 16)
            act_e.dma_start(sink[:], a["attn_sink"].partition_broadcast(P)).then_inc(ld_vec, 16)
            act_e.dma_start(rot[:], a["t_rot"]).then_inc(ld_rope, 16)
            act_e.dma_start(mask[:], a["t_mask"]).then_inc(ld_rope, 16)

            def split_w(t, s=None, count=None):
                s = t % 2 if s is None else s
                act_e.wait_ge(landed[s], landed_at[t] if count is None else count)
                if count is not None or t >= 2:
                    act_e.wait_ge(acc_ready, uses_to(t - 2))
                act_e.activation(whi[s][:], raw[s][:], ACT.Copy).then_inc(hi_done, 1)

            def square(q, k):
                sq, _, _, tn, _ = NB[q]
                if k >= 2:
                    act_e.wait_ge(n_acc, KD * q + k - 1)
                dst = sq[:] if k % 2 == 0 else tn[:, 1]
                act_e.activation(dst, xT[:, k, :], ACT.Square).then_inc(n_sq, 1)

            def norm_std(q):
                act_e.wait_ge(n_ps, q + 1)
                act_e.activation(NB[q][2][:], wk[:, 0:T], ACT.Sqrt, bias=epsc[:, 0:1], scale=1.0 / D).then_inc(n_std, 1)

            def norm_apply(q, k):
                tn, hf = NB[q][3], NB[q][4]
                act_e.wait_ge(n_t, KD * q + k + 1)
                if k >= 2:
                    if q < 2:
                        act_e.wait_ge(n_lo, KD * q + k - 1)
                    else:
                        act_e.wait_ge(y_turned, k - 1)
                sh = (SH1, SH2, SHF)[q]
                for g, (c0, L) in enumerate(GROUPS):
                    act_e.activation(hf[:, k % 2, c0:c0 + L], tn[:, k % 2, c0:c0 + L], ACT.Identity,
                                     bias=modT[:, sh + k, g:g + 1], scale=asc[:, q, k, g:g + 1]).then_inc(n_hf, 1)
                if q < 2:
                    act_e.wait_ge(n_hf, 16 * q + 2 * k + 2)
                    act_e.activation(act[:, 0, k, :], hf[:, k % 2, :], ACT.Copy).then_inc(n_hi, 1)

            act_e.wait_ge(vt_copied, 2)
            act_e.activation(csig[:], vT[:, V_C:V_C + 16], ACT.Sigmoid).then_inc(csig_done, 1)

            def xt_copy(u):
                b, h = u // 2, u % 2
                act_e.wait_ge(xt_ready, u + 1)
                act_e.activation(xT[:, 4 * h:4 * h + 4, P * b:P * b + P],
                                 wk[:, 512 * (u % 2):512 * (u % 2) + 512].rearrange("p (k n) -> p k n", k=4),
                                 ACT.Copy).then_inc(xt_copied, 1)

            for u in range(6):
                xt_copy(u)
            act_e.wait_ge(f_arg, 1)
            act_e.activation(h1[:], fb[:], ACT.Sin).then_inc(f_sin, 1)
            for u in range(6, 12):
                xt_copy(u)
            act_e.wait_ge(f_arg, 2)
            act_e.activation(zh[:], fb[:], ACT.Sin).then_inc(f_sin, 1)
            act_e.wait_ge(xt_copied, 12)
            for k in range(KD):
                square(0, k)
            split_w(0)
            split_w(1)
            last_spec = 0
            for f, (g, r, kind, pq, kt) in enumerate(FU):
                if kind == 1:
                    act_e.wait_ge(f_ready, f + 1)
                    if last_spec:
                        act_e.wait_ge(f_free, last_spec)
                    act_e.activation(fE[:], acc_ps[:, f % 2, 0:512], ACT.Copy).then_inc(f_even, 1)
                    last_spec = f + 1
            norm_std(0)
            act_e.wait_ge(asc_done, 2)
            act_e.wait_ge(f_ready, len(FU))
            for k in range(KD):
                norm_apply(0, k)

            for t in range(T_MERGE):
                s = t % 2
                act_e.wait_ge(acc_ready, t + 1)
                src = acc_ps[:, s, 0:T]
                if t < T_Q:
                    act_e.activation(xv[:, t, :], src, ACT.Identity, bias=vT[:, V_CB + t:V_CB + t + 1],
                                     scale=cwT[:, 12 + t:13 + t]).then_inc(cv_mid, 1)
                elif t < T_V:
                    act_e.activation(qk[:, t - T_Q, :], src, ACT.Copy).then_inc(acc_free[s], 1)
                elif t == T_V:
                    act_e.activation(vtmp[:], src, ACT.Copy).then_inc(acc_free[s], 1)
                else:
                    if t == T_GATE:
                        act_e.wait_ge(v_turned, 1)
                        act_e.activation(V[:].rearrange("p b n -> p (b n)"), wk[:, 0:T], ACT.Copy).then_inc(v_rows, 1)
                        act_e.wait_ge(rope_done, 5)
                    act_e.activation(gates[:, t - T_GATE, :], src, ACT.Sigmoid).then_inc(acc_free[s], 1)
                split_w(t + 2)

            def expo(n):
                b = n % 2
                nk = att_keys(ATT[n][0])[1]
                act_e.wait_ge(s_sd, n + 1)
                act_e.activation(es[:, b], sd[:, b], ACT.Exp).then_inc(s_es, 1)
                for j in range(NJ):
                    act_e.activation(S[:, b, j, 0:P * nk], S[:, b, j, 0:P * nk], ACT.Exp, bias=nmx[:, b, j:j + 1],
                                     accum_out=den[:, b, j:j + 1]).then_inc(s_exp, 1)

            def values_out(n):
                qb, kv = ATT[n]
                nk = att_keys(qb)[1]
                for kb in range(nk):
                    c = 512 * ((p_bank[n] + kb) % 3)
                    act_e.wait_ge(p_ready, p_first[n] + kb + 1)
                    act_e.activation(PT[:, n % 2, kb, :], wk[:, c:c + 512], ACT.Copy).then_inc(p_copied, 1)
                h = slice(HD * kv, HD * kv + HD)
                act_e.wait_ge(o_ready, n + 1)
                act_e.activation(qk[h, 0:NJ, P * qb:P * qb + P], wk[h, 1536:2048].rearrange("p (j n) -> p j n", j=NJ),
                                 ACT.Copy).then_inc(o_copied, 1)

            def turn_out(n):
                act_e.wait_ge(turn_ready, n + 1)
                if n == 0:
                    act_e.wait_ge(acc_ready, T_MERGE)
                if n >= 1:
                    act_e.wait_ge(fwd_ready, 4 * n)
                act_e.activation(eoT[:], acc_ps[:, 0, :], ACT.Copy).then_inc(turn_copied, 1)

            def inverse_out(n):
                act_e.wait_ge(inv_ready, n + 1)
                act_e.activation(eo[:], acc_ps[:, 1, :], ACT.Copy).then_inc(inv_copied, 1)

            turn_out(0)
            for n in range(len(STEPS)):
                expo(2 * n)
                values_out(2 * n)
                expo(2 * n + 1)
                if n + 1 < len(STEPS):
                    turn_out(n + 1)
                inverse_out(n)
                values_out(2 * n + 1)

            act_e.wait_ge(z_done, len(STEPS))
            act_e.wait_ge(o_copied, len(ATT))
            for k in range(KD):
                src = qk[:, k, :] if k < 4 else xv[:, 4 + k, :]
                act_e.activation(act[:, 0, k, :], src, ACT.Copy).then_inc(sp_hi, 1)

            for m in range(KD):
                act_e.wait_ge(mg_done, m + 1)
                act_e.activation(hid[:, 0, m, :], tmp[:, 2, :] if m % 2 else sqB[:], ACT.Copy).then_inc(mg_hi, 1)
                split_w(T_MERGE + m + 2)
            for m in range(KD):
                act_e.wait_ge(acc_free[m % 2], A_OUT // 2 + m // 2 + 1)
                square(1, m)
                if m < KD - 2:
                    split_w(T_OUT + m + 2)
                else:
                    s = m % 2
                    split_w(T_OUT + m + 2, s, 16 * (landed_base[s] + 1))
            norm_std(1)
            act_e.wait_ge(asc_done, 4)
            for k in range(KD):
                norm_apply(1, k)

            def up(c):
                with act_e.Fori(0, KD // 2) as i:
                    for s in range(2):
                        u = c * 8 + i * 2 + s
                        act_e.wait_ge(acc_ready, A_MLP + 1 + c * 16 + i * 2 + s)
                        act_e.activation(tmp[:, s, :], acc_ps[:, s, 0:T], ACT.Relu)\
                            .then_inc(acc_free[s], 1)
                        split_w(T_MLP + 2 + c * 16 + i * 2 + s, s, (landed_base[s] + 2 + c * 8 + i) * 16)
                        act_e.wait_ge(up_sq, u + 1)
                        act_e.activation(hid[:, 0, bass.ds(i * 2 + s, 1), :].rearrange("p o n -> p (o n)"),
                                         hfB[:, s, :], ACT.Copy).then_inc(hid_hi, 1)

            with act_e.Fori(0, NCH - 1) as c:
                up(c)
                with act_e.Fori(0, KD // 2) as i:
                    for s in range(2):
                        split_w(T_MLP + KD + 2 + c * 16 + i * 2 + s, s, (landed_base[s] + 6 + c * 8 + i) * 16)
            up(NCH - 1)
            for m in range(KD):
                if m < KD - 2:
                    t = T_MLP + 16 * (NCH - 1) + KD + m + 2
                    split_w(t, m % 2, 16 * (landed_base[m % 2] + (t - T_MLP) // 2 + 1))
                act_e.wait_ge(acc_free[m % 2], A_OUT // 2 + 1 + KD * NCH + m // 2)
                square(2, m)
            norm_std(2)
            act_e.wait_ge(asc_done, 6)
            for k in range(KD):
                norm_apply(2, k)

        @block.vector
        def _(dve):
            def split_w(t, s=None, count=None):
                s = t % 2 if s is None else s
                dve.wait_ge(landed[s], landed_at[t] if count is None else count)
                dve.wait_ge(hi_done, t + 1)
                dve.tensor_tensor(wlo[s][:], raw[s][:], whi[s][:], ALU.subtract).then_inc(lo_done, 1)

            def norm_acc(q, k):
                sq, acc, _, tn, _ = NB[q]
                dve.wait_ge(n_sq, KD * q + k + 1)
                if k == 0:
                    dve.tensor_copy(acc[:], sq[:]).then_inc(n_acc, 1)
                else:
                    dve.wait_ge(n_acc, KD * q + k)
                    dve.tensor_tensor(acc[:], acc[:], sq[:] if k % 2 == 0 else tn[:, 1], ALU.add).then_inc(n_acc, 1)

            def norm_rstd(q):
                rstd = NB[q][2]
                dve.wait_ge(n_std, q + 1)
                dve.reciprocal(rstd[:], rstd[:]).then_inc(n_rstd, 1)
                dve.wait_ge(n_rstd, q + 1)

            def norm_scale(q):
                for g in range(2):
                    v = (V_N1, V_N2, V_NF)[q]
                    sc = (SC1, SC2, SCF)[q]
                    dve.scalar_tensor_tensor(asc[:, q, :, g], modT[:, sc:sc + KD, g], 1.0, vT[:, v:v + KD],
                                             ALU.add, ALU.mult).then_inc(asc_done, 1)

            def norm_t(q, k):
                if k >= 2:
                    dve.wait_ge(n_hf, 16 * q + 2 * k - 2)
                dve.tensor_tensor(NB[q][3][:, k % 2], xT[:, k, :], NB[q][2][:], ALU.mult).then_inc(n_t, 1)

            def norm_lo(q, k):
                dve.wait_ge(n_hi, KD * q + k + 1)
                dve.tensor_tensor(act[:, 1, k, :], NB[q][4][:, k % 2], act[:, 0, k, :], ALU.subtract).then_inc(n_lo, 1)

            def norm_apply(q):
                for k in range(KD + 1):
                    if k < KD:
                        norm_t(q, k)
                    if k >= 1:
                        norm_lo(q, k - 1)

            def mod_out(c):
                dve.wait_ge(mod_used, c + 1)
                for g in range(2):
                    last = dve.tensor_tensor(
                        modT[:, 2 * c:2 * c + 2, g],
                        wk[:, 1536 + 4 * c:1536 + 4 * c + 4].rearrange("p (j g) -> p j g", g=2)[:, :, g],
                        vT[:, V_BA + 2 * c:V_BA + 2 * c + 2], ALU.add)
                last.then_inc(mod_done, 1)

            def chain(ins):
                steps[0] += 1
                ins.then_inc(f_step, 1)
                dve.wait_ge(f_step, steps[0])

            steps = [0]
            dve.wait_ge(vt_ready, 1)
            dve.tensor_copy(vT[:], wk[:, 1024:1024 + V_N]).then_inc(vt_copied, 1)
            dve.tensor_copy(cwT[:], wk[:, 1280:1316]).then_inc(vt_copied, 1)
            dve.wait_ge(csig_done, 1)
            dve.wait_ge(vt_copied, 2)
            dve.tensor_tensor(cact[:], csig[:], vT[:, V_C:V_C + 16], ALU.mult).then_inc(cact_done, 1)
            dve.wait_ge(ld_filt, 16 * 7)
            for layer in range(2):
                dve.wait_ge(fm_ready, layer + 1)
                chain(dve.tensor_scalar(fa[:], acc_ps[0:64, layer, 0:T], fv[:, 2 * layer:2 * layer + 1],
                                        fv[:, 2 * layer + 1:2 * layer + 2], ALU.add, ALU.mult))
                chain(dve.tensor_scalar(fk[:], fa[:], 0.5 / PI, MAGIC, ALU.mult, ALU.add))
                chain(dve.tensor_scalar(fk[:], fk[:], MAGIC, None, ALU.subtract))
                if layer == 1:
                    dve.wait_ge(f_sin, 1)
                for part, src in ((TWO_PI_A, fa), (TWO_PI_B, fb), (TWO_PI_C, fb)):
                    chain(dve.scalar_tensor_tensor(fb[:], fk[:], -part, src[:], ALU.mult, ALU.add))
                dve.tensor_scalar(fb[:], fb[:], 3.1415925, -3.1415925, ALU.min, ALU.max).then_inc(f_arg, 1)
                if layer == 0:
                    dve.wait_ge(ld_filt2, 16 * 5)
                    dve.tensor_tensor(w3eo[:, 0, :], w3[:, 0:1024], w3[:, 1024:2048], ALU.add)
                    dve.tensor_tensor(w3eo[:, 1, :], w3[:, 0:1024], w3[:, 1024:2048], ALU.subtract).then_inc(w3_sum, 1)
            for k in range(KD):
                norm_acc(0, k)
            split_w(0)
            split_w(1)
            e = 0
            for f, (g, r, kind, p, q) in enumerate(FU):
                dve.wait_ge(f_ready, f + 1)
                if kind == 0:
                    prev = [spec_end[x] for x in ((0, 0), (0, 1), (1, 0), (1, 1)) if spec_end[x] <= f]
                    if prev:
                        dve.wait_ge(f_ready, prev[-1])
                    d = dec if g == 0 else dec_p
                    dve.tensor_tensor(taps[:, p, 2 * q:2 * q + 2, :].rearrange("p m n -> p (m n)"),
                                      acc_ps[:, f % 2, :], d[:, 2 * q:2 * q + 2, :].rearrange("p m n -> p (m n)"),
                                      ALU.mult).then_inc(f_free, 1)
                else:
                    dve.wait_ge(f_even, e + 1)
                    if e >= 2:
                        dve.wait_ge(f_stored[e % 2], 16 * (e // 2))
                    odd = acc_ps[:, f % 2, 512:1024]
                    dve.tensor_tensor(fout[:, e % 2, 0, :], odd, fE[:], ALU.add)
                    a0, a1 = (fE[:], odd) if p == 0 else (odd, fE[:])
                    dve.tensor_tensor(fout[:, e % 2, 1, :], a0, a1, ALU.subtract).then_inc(f_free, 1)
                    e += 1
            for c in range(MOD_A):
                mod_out(c)
            dve.wait_ge(mod_done, MOD_A)
            norm_scale(0)
            norm_rstd(0)
            norm_apply(0)

            def conv_sides(t):
                s = t % 2
                dve.wait_ge(cv_mid, t + 1)
                for c0, L in GROUPS:
                    dve.scalar_tensor_tensor(xv[:, t, c0 + 1:c0 + L], acc_ps[:, s, c0:c0 + L - 1], cwT[:, t:t + 1],
                                             xv[:, t, c0 + 1:c0 + L], ALU.mult, ALU.add).then_inc(cv_part, 1)
                for g, (c0, L) in enumerate(GROUPS):
                    dve.wait_ge(cv_part, 2 * t + 1 + g)
                    last = dve.scalar_tensor_tensor(xv[:, t, c0:c0 + L - 1], acc_ps[:, s, c0 + 1:c0 + L],
                                                    cwT[:, 24 + t:25 + t], xv[:, t, c0:c0 + L - 1], ALU.mult, ALU.add)
                last.then_inc(acc_free[s], 1)

            def rope(j):
                dve.wait_ge(rot_ready, j + 1)
                if j >= 1:
                    dve.wait_ge(rope_done, j)
                dve.tensor_tensor(rt[:], wk[:, 0:T], sin[:], ALU.mult).then_inc(rope_step, 1)
                dve.tensor_tensor(qk[:, j, :], qk[:, j, :], cos[:], ALU.mult).then_inc(rope_mul, 1)
                dve.wait_ge(rope_step, j + 1)
                dve.wait_ge(rope_mul, j + 1)
                dve.tensor_tensor(qk[:, j, :], qk[:, j, :], rt[:], ALU.add).then_inc(rope_done, 1)

            for t in range(T_MERGE):
                if t < T_Q:
                    conv_sides(t)
                if t == T_Q:
                    dve.wait_ge(ld_rope, 16 * 4)
                split_w(t + 2)
                if t < MOD_N - MOD_A:
                    mod_out(MOD_A + t)
                if T_Q < t <= T_V:
                    rope(t - 1 - T_Q)
            dve.wait_ge(mod_done, MOD_N)
            norm_scale(1)
            norm_scale(2)

            def softmax_in(n):
                qb, kv = ATT[n]
                _, nk, m0 = att_keys(qb)
                b = n % 2
                if n >= 2:
                    dve.wait_ge(p_ready, sum(att_keys(q)[1] for q, _ in ATT[:n - 1]))
                for j in range(NJ):
                    c = 512 * ((s_bank[n] + j) % 3)
                    dve.wait_ge(s_ready, NJ * n + j + 1)
                    dve.tensor_tensor_reduce(S[:, b, j, 0:P * nk], wk[:, c:c + P * nk], mask[:, m0:m0 + P * nk],
                                             HD ** -0.5, sink[:, NJ * kv + j:NJ * kv + j + 1], ALU.add, ALU.max,
                                             mx[:, b, j:j + 1]).then_inc(s_max, 1)
                dve.wait_ge(s_max, NJ * n + NJ)
                dve.tensor_scalar(nmx[:, b], mx[:, b], -1.0, None, ALU.mult).then_inc(s_neg, 1)
                dve.tensor_tensor(sd[:, b], sink[:, NJ * kv:NJ * kv + NJ], mx[:, b], ALU.subtract).then_inc(s_sd, 1)

            def softmax_out(n):
                b = n % 2
                nk = att_keys(ATT[n][0])[1]
                dve.wait_ge(s_exp, NJ * n + NJ)
                dve.wait_ge(s_es, n + 1)
                dve.tensor_tensor(den[:, b], den[:, b], es[:, b], ALU.add).then_inc(s_den, 1)
                dve.wait_ge(s_den, n + 1)
                dve.reciprocal(rden[:, b], den[:, b]).then_inc(s_rden, 1)
                dve.wait_ge(s_rden, n + 1)
                for j in range(NJ):
                    last = dve.tensor_scalar(S[:, b, j, 0:P * nk], S[:, b, j, 0:P * nk], rden[:, b, j:j + 1], None, ALU.mult)
                last.then_inc(s_norm, 1)

            def products(n):
                dve.wait_ge(ld_spec, 32 * (n + 1))
                for b in range(4):
                    dve.wait_ge(fwd_ready, 4 * n + b + 1)
                    if b >= 1:
                        dve.wait_ge(prod_done, 4 * n + b)
                    elif n >= 1:
                        dve.wait_ge(z_done, n)
                    src = acc_ps[:, b // 2, 512 * (b % 2):512 * (b % 2) + 512].rearrange("p (d n) -> p d n", d=2)
                    for pq in range(2):
                        dve.tensor_tensor(cm[:, 512 * pq:512 * pq + 512].rearrange("p (d n) -> p d n", d=2), src,
                                          spec[:, pq, b:b + 1, :].broadcast_to([P, 2, 256]), ALU.mult).then_inc(cross_step, 1)
                    dve.wait_ge(cross_step, 8 * n + 2 * b + 2)
                    dve.tensor_tensor(Y[:, b, 0, :], cm[:, 0:256], cm[:, 768:1024], ALU.add)
                    dve.tensor_tensor(Y[:, b, 1, :], cm[:, 256:512], cm[:, 512:768], ALU.subtract).then_inc(prod_done, 1)

            def combine(n):
                u, r = STEPS[n]
                g, ct0, nct = UNITS[u]
                c0, L = GROUPS[g]
                full = cm[:].rearrange("p (c n) -> p c n", n=L)
                dve.wait_ge(y_done, n + 1)
                for ct in range(nct):
                    hb = V_HB + 4 * r + ct0 + ct
                    dve.scalar_tensor_tensor(full[:, ct, :], xv[:, 8 + ct0 + ct, c0:c0 + L], vT[:, hb:hb + 1],
                                             full[:, ct, :], ALU.mult, ALU.add).then_inc(y_step, 1)
                    steps_y[0] += 1
                dve.wait_ge(y_step, steps_y[0])
                dve.tensor_tensor(xv[:, 8 + ct0:8 + ct0 + nct, c0:c0 + L], full,
                                  xv[:, 4 * r + ct0:4 * r + ct0 + nct, c0:c0 + L], ALU.mult).then_inc(z_done, 1)

            steps_y = [0]
            softmax_in(0)
            for n in range(len(STEPS)):
                products(n)
                softmax_out(2 * n)
                softmax_in(2 * n + 1)
                combine(n)
                softmax_out(2 * n + 1)
                if 2 * n + 2 < len(ATT):
                    softmax_in(2 * n + 2)

            for k in range(KD):
                src = qk[:, k, :] if k < 4 else xv[:, 4 + k, :]
                dve.wait_ge(sp_hi, k + 1)
                dve.tensor_tensor(act[:, 1, k, :], src, act[:, 0, k, :], ALU.subtract).then_inc(sp_lo, 1)

            for m in range(KD):
                if m >= 1:
                    dve.wait_ge(mg_done, m)
                for x in range(2):
                    dve.wait_ge(acc_ready, A_MERGE + 2 * m + x + 1)
                    dve.tensor_tensor(tmp[:, x, :], acc_ps[:, x, 0:T], gates[:, KD * x + m, :], ALU.mult)\
                        .then_inc(acc_free[x], 1)
                mg = tmp[:, 2, :] if m % 2 else sqB[:]
                for x in range(2):
                    dve.wait_ge(acc_free[x], A_MERGE // 2 + m + 1)
                dve.tensor_tensor(mg, tmp[:, 0, :], tmp[:, 1, :], ALU.add).then_inc(mg_done, 1)
                split_w(T_MERGE + m + 2)
                dve.wait_ge(mg_hi, m + 1)
                dve.tensor_tensor(hid[:, 1, m, :], mg, hid[:, 0, m, :], ALU.subtract).then_inc(mg_lo, 1)

            def residual(s, m, gate, before):
                if before is not None:
                    dve.wait_ge(acc_free[s], before)
                for g, (c0, L) in enumerate(GROUPS):
                    row = xT[:, bass.ds(m, 1), c0:c0 + L].rearrange("p o n -> p (o n)")
                    last = dve.scalar_tensor_tensor(
                        row, acc_ps[:, s, c0:c0 + L], modT[:, bass.ds(gate + m, 1), g:g + 1].rearrange("p o n -> p (o n)"),
                        row, ALU.mult, ALU.add)
                last.then_inc(acc_free[s], 1)

            dve.wait_ge(ld_x2, 16)
            for m in range(KD):
                dve.wait_ge(acc_ready, A_OUT + m + 1)
                residual(m % 2, m, G1, None)
                if m < KD - 2:
                    split_w(T_OUT + m + 2)
                else:
                    split_w(T_OUT + m + 2, m % 2, 16 * (landed_base[m % 2] + 1))
                if m >= 1:
                    norm_acc(1, m - 1)
            norm_acc(1, KD - 1)
            norm_rstd(1)
            norm_apply(1)

            def up(c):
                with dve.Fori(0, KD // 2) as i:
                    for s in range(2):
                        u = c * 8 + i * 2 + s
                        dve.wait_ge(acc_free[s], A_MLP // 2 + 1 + c * 8 + i)
                        dve.tensor_tensor(hfB[:, s, :], tmp[:, s, :], tmp[:, s, :], ALU.mult).then_inc(up_sq, 1)
                        split_w(T_MLP + 2 + c * 16 + i * 2 + s, s, (landed_base[s] + 2 + c * 8 + i) * 16)
                        dve.wait_ge(hid_hi, u + 1)
                        m = bass.ds(i * 2 + s, 1)
                        dve.tensor_tensor(hid[:, 1, m, :].rearrange("p o n -> p (o n)"), hfB[:, s, :],
                                          hid[:, 0, m, :].rearrange("p o n -> p (o n)"), ALU.subtract).then_inc(hid_lo, 1)
                        dve.wait_ge(hid_lo, u + 1)

            with dve.Fori(0, NCH - 1) as c:
                up(c)
                with dve.Fori(0, KD // 2) as i:
                    for s in range(2):
                        dve.wait_ge(acc_ready, A_MLP + KD + 1 + c * 16 + i * 2 + s)
                        residual(s, i * 2 + s, G2, A_OUT // 2 + 1 + c * 8 + i)
                        split_w(T_MLP + KD + 2 + c * 16 + i * 2 + s, s, (landed_base[s] + 6 + c * 8 + i) * 16)
            up(NCH - 1)
            for m in range(KD):
                dve.wait_ge(acc_ready, A_MLP + 16 * (NCH - 1) + KD + m + 1)
                residual(m % 2, m, G2, A_OUT // 2 + 1 + KD * (NCH - 1) + m // 2)
                if m < KD - 2:
                    t = T_MLP + 16 * (NCH - 1) + KD + m + 2
                    split_w(t, m % 2, 16 * (landed_base[m % 2] + (t - T_MLP) // 2 + 1))
                if m >= 1:
                    norm_acc(2, m - 1)
            norm_acc(2, KD - 1)
            norm_rstd(2)
            for k in range(KD + 1):
                if k < KD:
                    norm_t(2, k)
                if k >= 1:
                    dve.wait_ge(y_turned, k)
                    dve.tensor_copy(onat[:, :, P * (k - 1):P * k],
                                    acc_ps[:, (k - 1) % 2, 0:T].rearrange("p (b n) -> p b n", b=NTB)).then_inc(y_copied, 1)


def tables():
    import numpy as np

    f = np.float32
    out = {"t_ident": np.eye(P)}
    dist = np.arange(3 * P)[None, :] - P - np.arange(P)[:, None]
    out["t_mask"] = np.where(np.abs(dist) <= 128, 0.0, -8e30)
    rot = np.zeros((P, P))
    for h in range(0, P, HD):
        for d in range(8):
            rot[h + d + 8, h + d] = -1.0
            rot[h + d, h + d + 8] = 1.0
    out["t_rot"] = rot
    pos = np.concatenate([np.arange(TS), np.arange(TP)])
    inv = f(500000.0) ** (-np.arange(8, dtype=f) * f(2.0) / f(16.0))
    ang = (pos.astype(f)[:, None] * inv[None, :]).astype(f).astype(np.float64)
    cos, sin = np.ones((P, T)), np.zeros((P, T))
    for h in range(0, P, HD):
        for d in range(16):
            cos[h + d] = np.cos(ang[:, d % 8])
            sin[h + d] = np.sin(ang[:, d % 8])
    out["t_cos"], out["t_sin"] = cos, sin
    zs = []
    for L in (TS, TP):
        t = np.linspace(0.0, 1.0, L, dtype=f)
        w = (f(2.0 * PI) * np.arange(L, dtype=f) / f(L)).astype(f)
        fr = np.linspace(1e-4, 15, 16, dtype=f)
        fw = (fr[:, None] * w[None, :]).astype(f).astype(np.float64)
        zs.append(np.concatenate([t[None].astype(np.float64), np.cos(fw), -np.sin(fw)], axis=0))
    out["t_z"] = np.concatenate(zs, axis=1)
    lo, hi = np.log(1e-2) / 1.5, np.log(1e-2) / 0.3
    deltas = np.abs(np.linspace(lo, hi, HW, dtype=f)).astype(np.float64)

    def rows(m):
        return m.reshape(-1, P, m.shape[1]).transpose(1, 0, 2)

    for L, n in ((TS, "s"), (TP, "p")):
        half = L // 2
        i = np.arange(half)
        m = np.concatenate([2 * i, 2 * i + 1])
        t = np.linspace(0.0, 1.0, L, dtype=f).astype(np.float64)[m]
        out[f"t_decay_{n}"] = rows(np.exp(-t[:, None] * deltas[None, :]) + 0.05)
        k1 = 2 * i
        k2 = L - 1 - k1
        mats = []
        for fn in (np.cos, np.sin):
            for odd in range(2):
                mats.append(rows(fn(np.pi * (k1[None, :] + 0.5) * (2 * i + odd)[:, None] / L)))
        out[f"t_filt_{n}"] = np.stack(mats, 1)
        fwd, inv_t = [], []
        for k in (k1, k2):
            th = np.pi * (k[None, :] + 0.5) * (i[:, None] + 0.5) / L
            for sg in (1, -1):
                m = np.cos(th) + sg * np.sin(th)
                fwd.append(rows(m))
                inv_t.append(rows(m.T / (2 * L)))
        out[f"t_fwd_{n}"] = np.stack(fwd, 1)
        out[f"t_inv_{n}"] = np.stack(inv_t, 1)
        if n == "p":
            for q in ("t_filt_p", "t_fwd_p", "t_inv_p"):
                out[q] = out[q][:, :, 0, :]
    return {k: np.ascontiguousarray(v.astype(f)) for k, v in out.items()}


_INS = ["x_prompt", "x_sample", "c_prompt", "c_sample", "w_ada", "b_ada", "norm1_g", "w_in", "attn_sink", "conv_w",
        "conv_b", "filt_w1", "filt_b1", "filt_freq1", "filt_w2", "filt_b2", "filt_freq2", "filt_w3", "hyena_bias",
        "w_attn_o", "w_hyena_o", "w_out", "norm2_g", "w_up", "w_down", "w_ada_final", "b_ada_final", "final_g"]


def kernel(**inputs):
    import numpy as np
    import concourse.bacc as bacc
    from concourse.bass_utils import run_bass_kernel_spmd

    nc = bacc.Bacc("TRN2", target_bir_lowering=False, num_devices=1)
    arrays, a = {}, {}
    host = {n: np.ascontiguousarray(inputs[n]) for n in _INS}
    host.update(tables())
    for n, v in host.items():
        arrays["in_" + n] = v
        a[n] = nc.dram_tensor("in_" + n, v.shape, mybir.dt.from_np(v.dtype), kind="ExternalInput").ap()
    out_p = nc.dram_tensor("out_p", (1, TP, D), F32, kind="ExternalOutput").ap()
    out_s = nc.dram_tensor("out_s", (1, TS, D), F32, kind="ExternalOutput").ap()
    program(nc, a, out_p, out_s)
    r = run_bass_kernel_spmd(nc, [arrays], core_ids=[0])
    return r.results[0]["out_p"], r.results[0]["out_s"]
```

```python
from contextlib import ExitStack

import concourse.bass as bass
from concourse import mybir

F32 = mybir.dt.float32
F32R = mybir.dt.float32r
ALU = mybir.AluOpType
ACT = mybir.ActivationFunctionType

P = 128
D = 1024
KD = D // P
TS, TP = 512, 256
T = TS + TP
NTB = T // P
GROUPS = ((0, TS), (TS, TP))
HD = 64
NJ = 4
QKV = 768
HY0 = QKV
HW = 512
GATE0 = HY0 + 3 * HW
DFF = 4 * D
NCH = DFF // D
EPS = 1e-6
PI = 3.141592653589793
TWO_PI_A = 6.28125
TWO_PI_B = 0.0019350051879882812
TWO_PI_C = 2 * PI - TWO_PI_A - TWO_PI_B
MAGIC = 12582912.0

T_Q, T_K, T_V, T_HY, T_GATE, T_MERGE, T_OUT, T_MLP = 0, 4, 5, 6, 18, 34, 42, 50
A_MERGE, A_OUT, A_MLP = 34, 50, 58
MOD_N = 64
MOD_A = 16
SH1, SC1, G1, SH2, SC2, G2, SHF, SCF = (8 * i for i in range(8))

V_C, V_N1, V_N2, V_NF, V_HB, V_BA, V_CB, V_N = 0, 16, 24, 32, 40, 48, 112, 124

UNITS = ((0, 0, 2), (0, 2, 2), (1, 0, 4))
STEPS = [(u, r) for r in range(2) for u in range(3)]
ATT = [(qb, kv) for qb in range(NTB) for kv in range(2)]

STAGES = {t: [] for t in range(T_MERGE)}
for _n in range(len(ATT)):
    STAGES[T_HY + 2 + _n].append(("values", _n))
for _n in range(len(ATT)):
    STAGES[T_HY + 1 + _n].append(("scores", _n))
for _n in range(len(STEPS)):
    STAGES[T_GATE + 1 + 2 * _n].insert(1 if _n == 0 else 0, ("turn", _n))
    STAGES[T_GATE + 2 + 2 * _n].append(("forward", _n))
    STAGES[T_GATE + 3 + 2 * _n].append(("inverse", _n))

MOD_BATCH = [(3 * b, min(3, MOD_A - 3 * b)) for b in range(6)]
for _t in range(T_GATE):
    MOD_BATCH.append((sum(MOD_BATCH[-1]), 2 if _t < T_HY else 3))
assert sum(MOD_BATCH[-1]) == MOD_N
MB_A = 6
MOD_ENDS = [m + n for m, n in MOD_BATCH[:MB_A]]


def split_stages(t):
    n = 1 if STAGES[t] and STAGES[t][0][0] == "values" else 0
    return STAGES[t][:n], STAGES[t][n:]


def att_keys(qb):
    lo, hi = (0, 4) if qb < 4 else (4, 6)
    first, last = max(qb - 1, lo), min(qb + 1, hi - 1)
    return first, last - first + 1, P * (first - qb + 1)


def program(nc, a, out_p, out_s):
    with ExitStack() as ctx:
        def sem(name):
            return ctx.enter_context(nc.semaphore(name))

        def region(*layouts, keep=None):
            got = []
            for layout in layouts[:-1]:
                with ExitStack() as e:
                    got.append([e.enter_context(nc.sbuf_tensor(*t)) for t in layout])
            got.append([ctx.enter_context(nc.sbuf_tensor(*t)) for t in layouts[-1]])
            return got

        def sb(name, shape, dt=F32):
            return ctx.enter_context(nc.sbuf_tensor(name, shape, dt))

        raw = [sb(f"w_raw{i}", [P, KD, P]) for i in range(2)]
        whi = [sb(f"w_hi{i}", [P, KD, P], F32R) for i in range(2)]
        wlo = [sb(f"w_lo{i}", [P, KD, P], F32R) for i in range(2)]
        (w3, w3eo, ftab, dec, taps), (act,) = region(
            [("filt_w3", [64, 2048], F32), ("filt_w3eo", [64, 2, 1024], F32), ("filt_tab", [P, 4, 2, 256], F32),
             ("filt_decay", [P, 4, 512], F32), ("filt_taps", [P, 2, 4, 512], F32)],
            [("act_hilo", [P, 2, KD, T], F32R)])
        ((zh, fa, fb, fk, h1, fout, sqA, accA, rstdA, tnA, hfA, vrow, vrow2),
         (cos, sin, rt, vtmp, S, PT, _, mask, rot),
         (gst, tabFp, tabIp, _, tabI, spec, tabF, cm), (hid,)) = region(
            [("filt_zh", [64, T], F32), ("filt_arg", [64, T], F32), ("filt_red", [64, T], F32),
             ("filt_turn", [64, T], F32), ("filt_h1", [64, T], F32), ("filt_out", [P, 2, 2, 512], F32),
             ("n0_sq", [P, T], F32), ("n0_acc", [P, T], F32), ("n0_rstd", [P, T], F32),
             ("n0_t", [P, 2, T], F32), ("n0_h", [P, 2, T], F32), ("vec_rows", [P, P], F32),
             ("conv_rows", [36, P], F32)],
            [("rope_cos", [P, T], F32), ("rope_sin", [P, T], F32), ("rope_rot", [P, T], F32),
             ("v_tmp", [P, T], F32), ("att_s", [P, 2, NJ, 384], F32), ("att_pT", [P, 2, 3, NJ * P], F32),
             ("r2_gap1", [P, 2560], F32), ("mask", [P, 384], F32), ("rope_perm", [P, P], F32)],
            [("gates_out", [P, 2, T], F32), ("dft_fwd_p", [P, 4, P], F32), ("dft_inv_p", [P, 4, P], F32),
             ("r2_gap2", [P, 512], F32), ("dft_inv", [P, 4, 2, 256], F32), ("hy_spec", [P, 2, 2, 4, 256], F32),
             ("dft_fwd", [P, 4, 2, 256], F32), ("hy_cross", [P, 1024], F32)],
            [("hidden_hilo", [P, 2, KD, T], F32R)])
        (mrawB, mhiB, mloB), (eo, eoT, Y, yeo, yfull), (xT,) = region(
            [("mod_rawB", [P, 2, KD, P], F32), ("mod_hiB", [P, 2, KD, P], F32R), ("mod_loB", [P, 2, KD, P], F32R)],
            [("hy_fold", [P, 1024], F32), ("hy_foldT", [P, 1024], F32), ("hy_prod", [P, 4, 2, 256], F32),
             ("hy_halves", [P, 1024], F32), ("hy_y", [P, 1024], F32)],
            [("xT", [P, KD, T], F32)])
        ((mrawA, mhiA, mloA, xnat, ftab_p, dec_p), (xv, qk, V), (_, gin),
         (tmp, sqB, accB, rstdB, tnB, hfB, onat)) = region(
            [("mod_rawA", [P, 2, KD, P], F32), ("mod_hiA", [P, 2, KD, P], F32R), ("mod_loA", [P, 2, KD, P], F32R),
             ("x_rows", [P, NTB, D], F32), ("filt_tab_p", [P, 4, P], F32), ("filt_decay_p", [P, 2, 512], F32)],
            [("hy_xv", [P, 12, T], F32), ("qk", [P, 5, T], F32), ("v_rows", [P, NTB, P], F32)],
            [("r4_gap", [P, 4 * T], F32), ("gates_in", [P, 2, 2, T], F32)],
            [("ev_tmp", [P, 3, T], F32), ("n_sq", [P, T], F32), ("n_acc", [P, T], F32), ("n_rstd", [P, T], F32),
             ("n_t", [P, 2, T], F32), ("n_h", [P, 2, T], F32), ("y_rows", [P, NTB, D], F32)])
        NB = [(sqA, accA, rstdA, tnA, hfA), (sqB, accB, rstdB, tnB, hfB), (sqB, accB, rstdB, tnB, hfB)]

        ident = sb("ident", [P, P])
        ones = sb("ones", [P, P])
        cst = sb("c_hilo", [P, KD, 66], F32R)
        sel = sb("mod_sel", [4, 2])
        mrow = sb("mod_rows", [4, 3 * P])
        vT = sb("vecT", [P, V_N])
        cwT = sb("conv_wT", [P, 36])
        csig = sb("c_sig", [P, 16])
        cact = sb("c_act", [P, 16])
        modT = sb("modT", [P, 64, 2])
        asc = sb("norm_scale", [P, 3, KD, 2])
        fE = sb("filt_even", [P, 512])
        fw1 = sb("filt_w1", [33, 64])
        fw2 = sb("filt_w2", [64, 64])
        fv = sb("filt_vec", [64, 4])
        sink = sb("sink", [P, 8])
        mx = sb("att_max", [P, 2, NJ])
        nmx = sb("att_negmax", [P, 2, NJ])
        sd = sb("att_sinkd", [P, 2, NJ])
        es = sb("att_sinke", [P, 2, NJ])
        den = sb("att_den", [P, 2, NJ])
        rden = sb("att_rden", [P, 2, NJ])
        epsc = sb("eps", [P, 1])

        acc_ps = ctx.enter_context(nc.psum_tensor("acc_ps", [P, 2, 1024], F32))
        wk = ctx.enter_context(nc.psum_tensor("wk", [P, 2048], F32))

        xT_d = nc.dram_tensor("xT_spill", [P, KD * T], F32).ap()
        gate_d = nc.dram_tensor("gate_spill", [P, 16 * T], F32).ap().rearrange("p (i n) -> p i n", n=T)
        spec_d = [nc.dram_tensor(f"spec{g}", [2, 2, P, (4, 2)[g] * 512], F32).ap() for g in range(2)]

        landed = [sem(f"w_landed{i}") for i in range(2)]
        hi_done, lo_done = sem("w_hi_done"), sem("w_lo_done")
        acc_ready = sem("acc_ready")
        acc_free = [sem(f"acc_free{i}") for i in range(2)]
        ld_vec, ld_z, ld_filt, ld_filt2, ld_rope, ld_tab, ld_x2 = (
            sem(n) for n in ("ld_vec", "ld_z", "ld_filt", "ld_filt2", "ld_rope", "ld_tab", "ld_xback"))
        ld_x = [sem(f"ld_x{i}") for i in range(NTB)]
        ld_mod = [sem(f"ld_mod{i}") for i in range(2)]
        ld_spec = [sem(f"ld_spec{i}") for i in range(2)]
        ld_gate = [sem(f"ld_gate{i}") for i in range(2)]
        gate_made = sem("gate_made")
        gate_stored = [sem(f"gate_stored{i}") for i in range(2)]
        cst_zero, cst_hi, cst_lo, sel_done = (
            sem(n) for n in ("cst_zero", "cst_hi", "cst_lo", "sel_done"))
        m_hi, m_lo, m_row, m_sum = sem("mod_hi"), sem("mod_lo"), sem("mod_row"), sem("mod_sum")
        ones_set = sem("ones_set")
        vt_ready, vt_copied, csig_done, cact_done = (sem(n) for n in ("vt_ready", "vt_copied", "csig", "cact"))
        xt_ready, xt_copied, xt_spilled = sem("xt_ready"), sem("xt_copied"), sem("xt_spilled")
        fm_ready, f_arg, f_sin, w3_sum = sem("fm_ready"), sem("f_arg"), sem("f_sin"), sem("w3_sum")
        f_ready, f_free, f_even = sem("f_ready"), sem("f_free"), sem("f_even")
        f_stored = [sem(f"f_stored{i}") for i in range(2)]
        mod_used, mod_done, asc_done = sem("mod_used"), sem("mod_done"), sem("asc_done")
        n_sq, n_acc, n_ps, n_std, n_rstd, n_t, n_hf, n_hi, n_lo = (
            sem(n) for n in ("n_sq", "n_acc", "n_ps", "n_std", "n_rstd", "n_t", "n_hf", "n_hi", "n_lo"))
        cv_mid, cv_part = sem("cv_mid"), sem("cv_part")
        rot_ready, rope_step, rope_done = sem("rot_ready"), sem("rope_step"), sem("rope_done")
        v_turned, v_rows = sem("v_turned"), sem("v_rows_done")
        fold_done, turn_ready, turn_copied = sem("fold_done"), sem("turn_ready"), sem("turn_copied")
        fwd_ready, cross_step, prod_done = sem("fwd_ready"), sem("cross_step"), sem("prod_done")
        inv_ready, inv_copied, y_done, y_step, z_done = (
            sem(n) for n in ("inv_ready", "inv_copied", "y_done", "y_step", "z_done"))
        s_ready, s_max, s_neg, s_sd, s_es, s_exp, s_den, s_rden, s_norm = (
            sem(n) for n in ("s_ready", "s_max", "s_neg", "s_sd", "s_es", "s_exp", "s_den", "s_rden", "s_norm"))
        p_ready, p_copied, o_ready, o_copied = (sem(n) for n in ("p_ready", "p_copied", "o_ready", "o_copied"))
        sp_hi, sp_lo = sem("sp_hi"), sem("sp_lo")
        f_step, rope_mul = sem("f_step"), sem("rope_mul")
        mg_done, mg_hi, mg_lo = sem("mg_done"), sem("mg_hi"), sem("mg_lo")
        up_sq, hid_hi, hid_lo = sem("up_sq"), sem("hid_hi"), sem("hid_lo")
        y_turned, y_copied, stored = sem("y_turned"), sem("y_copied"), sem("stored")

        def uses_to(t):
            if not isinstance(t, int) or t >= T_OUT:
                return t + A_OUT - T_OUT + 1
            return t + 1 if t < T_MERGE else A_MERGE + 2 * (t - T_MERGE) + 2

        n_dma = [2 if T_Q <= t < T_K else 3 if T_MERGE <= t < T_OUT else 1 for t in range(T_MLP)]
        landed_at = [16 * sum(n_dma[t % 2:t + 1:2]) for t in range(T_MLP)]
        landed_base = [sum(n_dma[s::2]) for s in range(2)]

        w_in = a["w_in"][0].rearrange("(k p) n -> p k n", p=P)
        w_ada = a["w_ada"][0].rearrange("(k p) n -> p k n", p=P)
        w_adaf = a["w_ada_final"].rearrange("(k p) n -> p k n", p=P)
        w_ao = a["w_attn_o"][0].rearrange("(h j p) n -> h p j n", h=2, p=HD)
        w_ho = a["w_hyena_o"][0].rearrange("(k p) n -> p k n", p=P)
        w_out = a["w_out"][0].rearrange("(k p) n -> p k n", p=P)
        w_up = a["w_up"][0].rearrange("(k p) n -> p k n", p=P)
        w_down = a["w_down"][0].rearrange("(c k p) n -> p c k n", k=KD, p=P)

        FU, tap_end, spec_end = [], {}, {}
        for g in range(2):
            for r in range(2):
                FU += [(g, r, 0, e, mp) for e in range(2) for mp in range(2 - g)]
                tap_end[g, r] = len(FU)
                FU += [(g, r, 1, pq, kt) for pq in range(2) for kt in range(2 - g)]
                spec_end[g, r] = len(FU)

        bank_of, bank_reader = {}, []
        p_first = [sum(att_keys(q)[1] for q, _ in ATT[:n]) for n in range(len(ATT))]
        for t in range(T_MERGE):
            for kind, n in STAGES[t]:
                bank_of[kind, n] = len(bank_reader)
                if kind == "scores":
                    bank_reader += [(s_max, NJ * n + j + 1) for j in range(NJ)]
                elif kind == "values":
                    bank_reader += [(p_copied, p_first[n] + kb + 1) for kb in range(att_keys(ATT[n][0])[1])]
                    bank_reader += [(o_copied, n + 1)]
                elif kind == "turn":
                    bank_reader += [(turn_copied, 2 * n + e + 1) for e in range(2)]
                elif kind == "forward":
                    bank_reader += [(prod_done, 4 * n + b + 1) for b in range(4)]
                else:
                    bank_reader += [(inv_copied, 2 * n + e + 1) for e in range(2)]

        def bank(kind, n, i):
            return 512 * ((bank_of[kind, n] + i) % 3)

        def mod_bufs(mt):
            return (mrawA, mhiA, mloA) if mt < MOD_A else (mrawB, mhiB, mloB)

        block = ctx.enter_context(nc.Block())

        @block.sync
        def _(sp):
            def weights(t):
                s = t % 2
                if t >= 2:
                    sp.wait_ge(hi_done, t - 1)
                    sp.wait_ge(lo_done, t - 1)
                if t < T_K:
                    j = t - T_Q
                    parts = [(raw[s][:, :, HD * h:HD * h + HD],
                              w_in[:, :, (NJ * h + j) * HD:(NJ * h + j + 1) * HD]) for h in range(2)]
                elif t < T_MERGE:
                    c = 2 * NJ * HD + P * (t - T_K)
                    parts = [(raw[s][:], w_in[:, :, c:c + P])]
                elif t < T_OUT:
                    c = P * (t - T_MERGE)
                    parts = [(raw[s][HD * h:HD * h + HD, 0:4, :], w_ao[h, :, :, c:c + P]) for h in range(2)]
                    parts.append((raw[s][:, 4:8, :], w_ho[:, :, c:c + P]))
                else:
                    c = P * (t - T_OUT)
                    parts = [(raw[s][:], w_out[:, :, c:c + P])]
                for dst, src in parts:
                    sp.dma_start(dst, src).then_inc(landed[s], 16)

            def mod_load(mt):
                if mt >= 2:
                    sp.wait_ge(m_hi, mt - 1)
                    sp.wait_ge(m_lo, mt - 1)
                src = w_ada[:, :, P * mt:P * mt + P] if mt < 48 else w_adaf[:, :, P * (mt - 48):P * (mt - 47)]
                sp.dma_start(mod_bufs(mt)[0][:, mt % 2], src).then_inc(ld_mod[mt % 2], 16)

            sp.dma_start(zh[0:33, :], a["t_z"]).then_inc(ld_z, 16)
            for b in range(NTB):
                src = a["x_sample"][0, P * b:P * b + P, :] if b < 4 else a["x_prompt"][0, P * (b - 4):P * (b - 3), :]
                sp.dma_start(xnat[:, b], src).then_inc(ld_x[b], 16)
            for mt in range(MOD_A):
                mod_load(mt)
                if mt == 3:
                    weights(0)
                if mt == 5:
                    weights(1)
            sp.wait_ge(xt_copied, 12)
            sp.dma_start(xT_d, xT[:].rearrange("p k n -> p (k n)")).then_inc(xt_spilled, 16)
            sp.wait_ge(xt_spilled, 16)
            sp.wait_ge(n_t, KD)
            for mt in range(MOD_A, MOD_A + 2):
                mod_load(mt)
            sp.wait_ge(n_lo, KD)
            sp.wait_ge(f_stored[0], 16 * 6)
            sp.wait_ge(f_stored[1], 16 * 6)
            for dst, name in ((rot, "t_rot"), (cos, "t_cos"), (sin, "t_sin"), (mask, "t_mask")):
                sp.dma_start(dst[:], a[name]).then_inc(ld_rope, 16)
            mt = MOD_A + 2
            for t in range(2, T_MERGE + 2):
                weights(t)
                for _ in range(2 if t - 2 < T_HY else 3):
                    if mt < MOD_N:
                        mod_load(mt)
                        mt += 1
                if t == 10:
                    sp.wait_ge(v_rows, 1)
                    for dst, name in ((tabF, "t_fwd_s"), (tabFp, "t_fwd_p"), (tabIp, "t_inv_p")):
                        sp.dma_start(dst[:], a[name]).then_inc(ld_tab, 16)
                if t >= 21 and t % 2:
                    n = (t - 21) // 2 + 1
                    if n == 1:
                        sp.wait_ge(o_copied, len(ATT))
                        sp.dma_start(tabI[:], a["t_inv_s"]).then_inc(ld_tab, 16)
                    for n in ((0, 1) if n == 1 else (n,)):
                        if n >= len(STEPS):
                            continue
                        u, rr = STEPS[n]
                        g, ct0, nct = UNITS[u]
                        if n >= 2:
                            sp.wait_ge(prod_done, 4 * n - 4)
                        for pq in range(2):
                            src = spec_d[g][rr, pq].rearrange("p (b n) -> p b n", b=4)
                            if g == 0:
                                src = src[:, :, P * ct0:P * ct0 + 256]
                            sp.dma_start(spec[:, n % 2, pq], src).then_inc(ld_spec[n % 2], 16)
            weights(T_MERGE + 2)
            weights(T_MERGE + 3)
            sp.wait_ge(z_done, len(STEPS))
            sp.dma_start(xT[:].rearrange("p k n -> p (k n)"), xT_d).then_inc(ld_x2, 16)
            for t in range(T_MERGE + 4, T_MLP):
                weights(t)
            with sp.Fori(0, NCH) as c:
                with sp.Fori(0, KD // 2) as i:
                    for s in range(2):
                        t = T_MLP + c * 16 + i * 2 + s
                        sp.wait_ge(hi_done, t - 1)
                        sp.wait_ge(lo_done, t - 1)
                        sp.dma_start(raw[s][:], w_up[:, :, bass.ds(c * D + i * 256 + s * P, P)]).then_inc(landed[s], 16)
                with sp.Fori(0, KD // 2) as i:
                    for s in range(2):
                        t = T_MLP + KD + c * 16 + i * 2 + s
                        sp.wait_ge(hi_done, t - 1)
                        sp.wait_ge(lo_done, t - 1)
                        sp.dma_start(raw[s][:], w_down[:, bass.ds(c, 1), :, bass.ds(i * 256 + s * P, P)]
                                     .rearrange("p c k n -> p (c k) n")).then_inc(landed[s], 16)
            for half in range(2):
                sp.wait_ge(y_copied, 4 * half + 4)
                c = slice(512 * half, 512 * half + 512)
                sp.dma_start(out_s[0].rearrange("(b p) n -> p b n", p=P)[:, :, c], onat[:, 0:4, c]).then_inc(stored, 16)
                sp.dma_start(out_p[0].rearrange("(b p) n -> p b n", p=P)[:, :, c], onat[:, 4:6, c]).then_inc(stored, 16)
            sp.wait_ge(stored, 64)

        @block.gpsimd
        def _(pool):
            pool.memset(cst[:].bitcast(F32), 0.0).then_inc(cst_zero, 1)
            pool.memset(ones[:], 1.0).then_inc(ones_set, 1)
            pool.memset(epsc[:], EPS).then_inc(ones_set, 1)
            pool.dma_start(fw1[:], a["filt_w1"][0]).then_inc(ld_filt, 16)
            pool.dma_start(fw2[:], a["filt_w2"][0]).then_inc(ld_filt, 16)
            for i, n in enumerate(("filt_b1", "filt_freq1", "filt_b2", "filt_freq2")):
                pool.dma_start(fv[:, i:i + 1], a[n].rearrange("o f -> f o")).then_inc(ld_filt, 16)
            pool.dma_start(w3[:], a["filt_w3"][0]).then_inc(ld_filt2, 16)
            pool.dma_start(dec[:], a["t_decay_s"]).then_inc(ld_filt2, 16)
            pool.dma_start(ftab[:], a["t_filt_s"]).then_inc(ld_filt2, 16)
            pool.dma_start(dec_p[:], a["t_decay_p"]).then_inc(ld_filt2, 16)
            pool.dma_start(ftab_p[:], a["t_filt_p"]).then_inc(ld_filt2, 16)
            e = 0
            for f, (g, r, kind, pq, kt) in enumerate(FU):
                if kind == 1:
                    pool.wait_ge(f_free, f + 1)
                    dst = spec_d[g][r, pq].rearrange("p (s k n) -> p s k n", s=2, n=512)[:, :, kt, :]
                    pool.dma_start(dst, fout[:, e % 2]).then_inc(f_stored[e % 2], 16)
                    e += 1

            def fold(n):
                u, r = STEPS[n]
                g, ct0, nct = UNITS[u]
                c0, L = GROUPS[g]
                src = xv[:, 8 + ct0:8 + ct0 + nct, c0:c0 + L]
                back = src[:, :, ::-1]
                e4 = eo[:].rearrange("p (c e n) -> p c e n", e=2, n=L // 2)
                if n == 0:
                    for s in range(2):
                        pool.wait_ge(acc_free[s], T_GATE // 2)
                    pool.wait_ge(mod_used, MOD_N)
                if n >= 1:
                    pool.wait_ge(turn_ready, 2 * n)
                if r == 1:
                    pool.wait_ge(z_done, n - 2)
                for i, op in enumerate((ALU.add, ALU.subtract)):
                    last = pool.tensor_tensor(e4[:, :, i, :], src[:, :, 0:L // 2], back[:, :, 0:L // 2], op)
                last.then_inc(fold_done, 1)

            def unfold(n):
                u, r = STEPS[n]
                g, ct0, nct = UNITS[u]
                L = GROUPS[g][1]
                y4 = yeo[:].rearrange("p (c e n) -> p c e n", e=2, n=L // 2)
                full = yfull[:].rearrange("p (c n) -> p c n", n=L)
                pool.wait_ge(inv_copied, 2 * n + 2)
                if n >= 1:
                    pool.wait_ge(z_done, n)
                pool.tensor_tensor(full[:, :, 0:L // 2], y4[:, :, 0, :], y4[:, :, 1, :], ALU.add)
                pool.tensor_tensor(full[:, :, ::-1][:, :, 0:L // 2], y4[:, :, 0, :], y4[:, :, 1, :],
                                   ALU.subtract).then_inc(y_done, 1)

            fold(0)
            for n in range(len(STEPS)):
                if n + 1 < len(STEPS):
                    fold(n + 1)
                unfold(n)

        @block.tensor
        def _(pe):
            def gemm_k(slot, s, k, kw, src, first, last):
                for i, (w, x) in enumerate(((whi[s], 0), (whi[s], 1), (wlo[s], 0))):
                    for c0, L in GROUPS:
                        mm = pe.matmul(acc_ps[:, slot, c0:c0 + L], w[:, kw, :], src[:, x, k, c0:c0 + L],
                                       start=(first and i == 0), stop=(last and i == 2))
                return mm

            def gemm(t, src, parts=None, k_waits=()):
                s = t % 2
                pe.wait_ge(hi_done, t + 1)
                pe.wait_ge(lo_done, t + 1)
                parts = parts or [(t, range(KD))]
                for a_i, ks in parts:
                    if a_i >= 2:
                        pe.wait_ge(acc_free[a_i % 2], a_i // 2)
                    for k in ks:
                        for sm, base in k_waits:
                            pe.wait_ge(sm, base + k)
                        mm = gemm_k(a_i % 2, s, k, k, src, k == ks[0], k == ks[-1])
                    if ks[-1] != KD - 1:
                        mm.then_inc(acc_ready, 1)
                mm.then_inc(acc_ready, 1)

            def mod_tile(b, i):
                mt = MOD_BATCH[b][0] + i
                _, mhi, mlo = mod_bufs(mt)
                pe.wait_ge(m_hi, mt + 1)
                pe.wait_ge(m_lo, mt + 1)
                if i == 0 and b >= 1:
                    pe.wait_ge(mod_done, b)
                o = wk[0:66, 1536 + P * i:1536 + P * i + P]
                for k in range(KD):
                    pe.matmul(o, cst[:, k, :], mhi[:, mt % 2, k, :], start=(k == 0), stop=False)
                    mm = pe.matmul(o, cst[:, k, :], mlo[:, mt % 2, k, :], start=False, stop=(k == KD - 1))
                mm.then_inc(mod_used, 1)

            def mod_sum(b):
                pe.wait_ge(m_row, b + 1)
                for i in range(MOD_BATCH[b][1]):
                    mm = pe.matmul(wk[:, 1920 + 2 * i:1920 + 2 * i + 2], mrow[:, P * i:P * i + P], sel[:],
                                   start=True, stop=True)
                mm.then_inc(m_sum, 1)

            def norm_sum(q):
                pe.wait_ge(n_acc, KD * q + KD)
                for c0, L in GROUPS:
                    mm = pe.matmul(wk[:, c0:c0 + L], ones[:], NB[q][1][:, c0:c0 + L], start=True, stop=True)
                mm.then_inc(n_ps, 1)

            pe.wait_ge(ld_vec, 16 * 12)
            pe.transpose(wk[:, 1024:1024 + V_N], vrow[0:V_N, :], ident[0:V_N, 0:V_N])
            pe.transpose(wk[:, 1280:1316], vrow2[:], ident[0:36, 0:36]).then_inc(vt_ready, 1)

            def filt_mlp(layer):
                for c0, L in GROUPS:
                    if layer == 0:
                        mm = pe.matmul(acc_ps[0:64, 0, c0:c0 + L], fw1[:], zh[0:33, c0:c0 + L], start=True, stop=True)
                    else:
                        mm = pe.matmul(acc_ps[0:64, 1, c0:c0 + L], fw2[:], h1[:, c0:c0 + L], start=True, stop=True)
                mm.then_inc(fm_ready, 1)

            def turn_x(u):
                b, h = u // 2, u % 2
                pe.wait_ge(ld_x[b], 16)
                if u >= 2:
                    pe.wait_ge(xt_copied, u - 1)
                for k in range(4):
                    mm = pe.transpose(wk[:, 512 * (u % 2) + P * k:512 * (u % 2) + P * k + P],
                                      xnat[:, b, P * (4 * h + k):P * (4 * h + k) + P], ident[:])
                mm.then_inc(xt_ready, 1)

            pe.wait_ge(ld_filt, 16 * 6)
            pe.wait_ge(ld_z, 16)
            filt_mlp(0)
            for u in range(6):
                turn_x(u)
            pe.wait_ge(f_sin, 1)
            filt_mlp(1)
            for u in range(6, 12):
                turn_x(u)
            pe.wait_ge(f_sin, 2)
            pe.wait_ge(w3_sum, 1)
            pe.wait_ge(ld_filt2, 16 * 5)
            for f, (g, r, kind, p, q) in enumerate(FU):
                c0, L = GROUPS[g]
                n_e = 2 - g
                if f >= 2:
                    pe.wait_ge(f_free, f - 1)
                if kind == 0:
                    for j in range(2):
                        m = 2 * q + j
                        odd, jj = (m // n_e, m % n_e)
                        t0 = c0 + 256 * jj + odd
                        mm = pe.matmul(acc_ps[:, f % 2, 512 * j:512 * j + 512], zh[:, t0:t0 + 255:2],
                                       w3eo[:, p, 512 * r:512 * r + 512], start=True, stop=True)
                else:
                    pe.wait_ge(f_free, tap_end[g, r])
                    tab = ftab if g == 0 else ftab_p[:].rearrange("p m (j n) -> p m j n", j=1)
                    for odd in range(2):
                        for j in range(n_e):
                            mm = pe.matmul(acc_ps[:, f % 2, 512 * odd:512 * odd + 512],
                                           tab[:, 2 * p + odd, j, P * q:P * q + P], taps[:, p, odd * n_e + j, :],
                                           start=(j == 0), stop=(j == n_e - 1))
                mm.then_inc(f_ready, 1)
                mt = f - 2
                if mt == 0:
                    pe.wait_ge(cst_lo, 1)
                    pe.wait_ge(sel_done, 1)
                if mt in MOD_ENDS:
                    mod_sum(MOD_ENDS.index(mt))
                if 0 <= mt < MOD_A:
                    mod_tile(mt // 3, mt % 3)
            pe.wait_ge(ones_set, 2)
            norm_sum(0)
            pe.wait_ge(f_free, len(FU))

            def rope_turn(j):
                pe.wait_ge(acc_free[(T_Q + j) % 2], (T_Q + j) // 2 + 1)
                if j >= 1:
                    pe.wait_ge(rope_step, j)
                for c0, L in GROUPS:
                    mm = pe.matmul(wk[:, c0:c0 + L], rot[:], qk[:, j, c0:c0 + L], start=True, stop=True)
                mm.then_inc(rot_ready, 1)

            def turn_v():
                pe.wait_ge(acc_free[T_V % 2], T_V // 2 + 1)
                pe.wait_ge(rope_step, 5)
                for b in range(NTB):
                    mm = pe.transpose(wk[:, P * b:P * b + P], vtmp[:, P * b:P * b + P], ident[:])
                mm.then_inc(v_turned, 1)

            def take(kind, n, i):
                b = bank_of[kind, n] + i
                if b >= 3:
                    pe.wait_ge(*bank_reader[b - 3])
                return 512 * (b % 3)

            def scores(n):
                qb, kv = ATT[n]
                first, nk, _ = att_keys(qb)
                h = slice(HD * kv, HD * kv + HD)
                for j in range(NJ):
                    c = take("scores", n, j)
                    pe.matmul(wk[:, c:c + P * nk], qk[h, j, P * qb:P * qb + P], qk[h, 4, P * first:P * (first + nk)],
                              start=True, stop=True).then_inc(s_ready, 1)

            def values(n):
                qb, kv = ATT[n]
                first, nk, _ = att_keys(qb)
                pe.wait_ge(s_norm, n + 1)
                done = p_first[n]
                for kb in range(nk):
                    c = take("values", n, kb)
                    for j in range(NJ):
                        mm = pe.transpose(wk[:, c + P * j:c + P * j + P], S[:, n % 2, j, P * kb:P * kb + P], ident[:])
                    mm.then_inc(p_ready, 1)
                c = take("values", n, nk)
                for kb in range(nk):
                    pe.wait_ge(p_copied, done + kb + 1)
                    mm = pe.matmul(wk[:, c:c + 512], V[:, first + kb, :], PT[:, n % 2, kb, :],
                                   start=(kb == 0), stop=(kb == nk - 1))
                mm.then_inc(o_ready, 1)

            def turn(n):
                g, _, nct = UNITS[STEPS[n][0]]
                h = GROUPS[g][1] // 2
                e4 = eo[:].rearrange("p (c e n) -> p c e n", e=2, n=h)
                pe.wait_ge(fold_done, n + 1)
                for e in range(2):
                    c = take("turn", n, e)
                    for j in range(h // P):
                        for ct in range(nct):
                            mm = pe.transpose(wk[:, c + j * 256 + P * ct:c + j * 256 + P * ct + P],
                                              e4[:, ct, e, P * j:P * j + P], ident[:])
                    mm.then_inc(turn_ready, 1)

            def forward(n):
                g, _, nct = UNITS[STEPS[n][0]]
                pe.wait_ge(turn_copied, 2 * n + 2)
                if n == 0:
                    pe.wait_ge(ld_tab, 16 * 4)
                for b in range(4):
                    c = take("forward", n, b)
                    ks, x = b // 2, b % 2
                    for d in range(2):
                        e = ks ^ d
                        o = wk[:, c + 256 * d:c + 256 * d + 256]
                        if g == 0:
                            for j in range(2):
                                mm = pe.matmul(o, tabF[:, 2 * ks + d, j, P * x:P * x + P],
                                               eoT[:, 512 * e + 256 * j:512 * e + 256 * j + 256],
                                               start=(j == 0), stop=(j == 1))
                        else:
                            mm = pe.matmul(o, tabFp[:, 2 * ks + d, :], eoT[:, 512 * e + 256 * x:512 * e + 256 * x + 256],
                                           start=True, stop=True)
                    mm.then_inc(fwd_ready, 1)

            def inverse(n):
                g, _, nct = UNITS[STEPS[n][0]]
                pe.wait_ge(prod_done, 4 * n + 4)
                for ct in range(nct):
                    per = nct // 2
                    if ct % per == 0:
                        c = take("inverse", n, ct // per)
                    for part in range(2):
                        if g == 0:
                            o = wk[:, c + 256 * part:c + 256 * part + 256]
                            terms = [(Y[:, 2 * ks + kt, ks ^ part, P * ct:P * ct + P], tabI[:, 2 * ks + (ks ^ part), kt, :])
                                     for ks in range(2) for kt in range(2)]
                        else:
                            o = wk[:, c + 256 * (ct % 2) + P * part:c + 256 * (ct % 2) + P * part + P]
                            terms = [(Y[:, 2 * ks + ct // 2, ks ^ part, P * (ct % 2):P * (ct % 2) + P],
                                      tabIp[:, 2 * ks + (ks ^ part), :]) for ks in range(2)]
                        for i, (w, x) in enumerate(terms):
                            mm = pe.matmul(o, w, x, start=(i == 0), stop=(i == len(terms) - 1))
                    if ct % per == per - 1:
                        mm.then_inc(inv_ready, 1)

            run = {"scores": scores, "values": values, "turn": turn, "forward": forward, "inverse": inverse}
            for t in range(T_MERGE):
                b = MB_A + t
                gemm(t, act, k_waits=((n_hi, 1), (n_lo, 1)) if t == 0 else ())
                if 0 < t <= T_GATE:
                    mod_sum(b - 1)
                if 1 <= t <= T_V:
                    rope_turn(t - 1)
                if t == T_HY:
                    turn_v()
                    pe.wait_ge(v_rows, 1)
                first, rest = split_stages(t)
                for kind, n in first:
                    run[kind](n)
                for i in range(2 if t < T_GATE else 0):
                    mod_tile(b, i)
                for kind, n in rest:
                    run[kind](n)
                if t < T_GATE and MOD_BATCH[b][1] == 3:
                    mod_tile(b, 2)

            for m in range(KD):
                gemm(T_MERGE + m, act, parts=[(A_MERGE + 2 * m, range(4)), (A_MERGE + 2 * m + 1, range(4, 8))],
                     k_waits=((sp_hi, 1), (sp_lo, 1)) if m == 0 else ())
            for m in range(KD):
                gemm(T_OUT + m, hid, parts=[(A_OUT + m, range(KD))],
                     k_waits=((mg_hi, 1), (mg_lo, 1)) if m == 0 else ())
            norm_sum(1)

            with pe.Fori(0, NCH) as c:
                with pe.Fori(0, KD // 2) as i:
                    for s in range(2):
                        pe.wait_ge(hi_done, T_MLP + 1 + c * 16 + i * 2 + s)
                        pe.wait_ge(lo_done, T_MLP + 1 + c * 16 + i * 2 + s)
                        pe.wait_ge(acc_free[s], A_MLP // 2 + c * 8 + i)
                        for k in range(KD):
                            if s == 0:
                                pe.wait_ge(n_hi, KD + k + 1)
                                pe.wait_ge(n_lo, KD + k + 1)
                            mm = gemm_k(s, s, k, k, act, k == 0, k == KD - 1)
                        mm.then_inc(acc_ready, 1)
                with pe.Fori(0, KD // 2) as i:
                    for s in range(2):
                        pe.wait_ge(hi_done, T_MLP + KD + 1 + c * 16 + i * 2 + s)
                        pe.wait_ge(lo_done, T_MLP + KD + 1 + c * 16 + i * 2 + s)
                        pe.wait_ge(acc_free[s], A_MLP // 2 + KD // 2 + c * 8 + i)
                        for k in range(KD):
                            if s == 0 and k in (0, KD - 2, KD - 1):
                                need = KD - 2 if k == 0 else k + 1
                                pe.wait_ge(hid_hi, need + c * 8)
                                pe.wait_ge(hid_lo, need + c * 8)
                            mm = gemm_k(s, s, k, k, hid, k == 0, k == KD - 1)
                        mm.then_inc(acc_ready, 1)
            norm_sum(2)
            for s in range(2):
                pe.wait_ge(acc_free[s], A_MLP // 2 + 32)
            for k in range(KD):
                pe.wait_ge(n_hf, 32 + 2 * k + 2)
                if k >= 2:
                    pe.wait_ge(y_copied, k - 1)
                for b in range(NTB):
                    mm = pe.transpose(acc_ps[:, k % 2, P * b:P * b + P], hfB[:, k % 2, P * b:P * b + P], ident[:])
                mm.then_inc(y_turned, 1)

        @block.scalar
        def _(act_e):
            r0 = 0
            for src, n in ((a["c_sample"], 8), (a["c_prompt"], 8), (a["norm1_g"], 8), (a["norm2_g"], 8)):
                act_e.dma_start(vrow[r0:r0 + n, :], src.rearrange("o (k p) -> (o k) p", p=P)).then_inc(ld_vec, 16)
                r0 += n
            act_e.dma_start(vrow[V_NF:V_HB, :], a["final_g"].rearrange("(k p) -> k p", p=P)).then_inc(ld_vec, 16)
            act_e.dma_start(vrow[V_HB:V_BA, :], a["hyena_bias"][0].rearrange("o (k p) -> (o k) p", p=P)).then_inc(ld_vec, 16)
            act_e.dma_start(vrow[V_BA:V_BA + 48, :], a["b_ada"].rearrange("o (k p) -> (o k) p", p=P)).then_inc(ld_vec, 16)
            act_e.dma_start(vrow[V_BA + 48:V_CB, :], a["b_ada_final"].rearrange("(k p) -> k p", p=P)).then_inc(ld_vec, 16)
            act_e.dma_start(vrow[V_CB:V_N, :], a["conv_b"].rearrange("o (k p) -> (o k) p", p=P)).then_inc(ld_vec, 16)
            act_e.dma_start(vrow2[:], a["conv_w"][0].rearrange("i (k p) -> (i k) p", p=P)).then_inc(ld_vec, 16)
            act_e.dma_start(ident[:], a["t_ident"]).then_inc(ld_vec, 16)
            act_e.dma_start(sink[:], a["attn_sink"].partition_broadcast(P)).then_inc(ld_vec, 16)

            def split_mod(mt):
                raw_m, mhi, _ = mod_bufs(mt)
                act_e.wait_ge(ld_mod[mt % 2], 16 * (mt // 2 + 1))
                if mt >= 2:
                    act_e.wait_ge(mod_used, mt - 1)
                act_e.activation(mhi[:, mt % 2], raw_m[:, mt % 2], ACT.Copy).then_inc(m_hi, 1)

            def split_w(t, s=None, count=None):
                s = t % 2 if s is None else s
                act_e.wait_ge(landed[s], landed_at[t] if count is None else count)
                if count is not None or t >= 2:
                    act_e.wait_ge(acc_ready, uses_to(t - 2))
                act_e.activation(whi[s][:], raw[s][:], ACT.Copy).then_inc(hi_done, 1)

            def square(q, k):
                sq, _, _, tn, _ = NB[q]
                if k >= 2:
                    act_e.wait_ge(n_acc, KD * q + k - 1)
                dst = sq[:] if k % 2 == 0 else tn[:, 1]
                act_e.activation(dst, xT[:, k, :], ACT.Square).then_inc(n_sq, 1)

            def norm_std(q):
                act_e.wait_ge(n_ps, q + 1)
                act_e.activation(NB[q][2][:], wk[:, 0:T], ACT.Sqrt, bias=epsc[:, 0:1], scale=1.0 / D).then_inc(n_std, 1)

            def norm_apply(q, k):
                tn, hf = NB[q][3], NB[q][4]
                act_e.wait_ge(n_t, KD * q + k + 1)
                if k >= 2:
                    if q < 2:
                        act_e.wait_ge(n_lo, KD * q + k - 1)
                    else:
                        act_e.wait_ge(y_turned, k - 1)
                sh = (SH1, SH2, SHF)[q]
                for g, (c0, L) in enumerate(GROUPS):
                    act_e.activation(hf[:, k % 2, c0:c0 + L], tn[:, k % 2, c0:c0 + L], ACT.Identity,
                                     bias=modT[:, sh + k, g:g + 1], scale=asc[:, q, k, g:g + 1]).then_inc(n_hf, 1)
                if q < 2:
                    act_e.wait_ge(n_hf, 16 * q + 2 * k + 2)
                    act_e.activation(act[:, 0, k, :], hf[:, k % 2, :], ACT.Copy).then_inc(n_hi, 1)

            act_e.wait_ge(vt_copied, 2)
            act_e.activation(csig[:], vT[:, V_C:V_C + 16], ACT.Sigmoid).then_inc(csig_done, 1)

            act_e.wait_ge(cact_done, 1)
            act_e.wait_ge(cst_zero, 1)
            act_e.activation(cst[:, :, 0:2], cact[:].rearrange("p (g k) -> p k g", g=2), ACT.Copy).then_inc(cst_hi, 1)

            def xt_copy(u):
                b, h = u // 2, u % 2
                act_e.wait_ge(xt_ready, u + 1)
                act_e.activation(xT[:, 4 * h:4 * h + 4, P * b:P * b + P],
                                 wk[:, 512 * (u % 2):512 * (u % 2) + 512].rearrange("p (k n) -> p k n", k=4),
                                 ACT.Copy).then_inc(xt_copied, 1)

            for u in range(6):
                xt_copy(u)
            act_e.wait_ge(f_arg, 1)
            act_e.activation(h1[:], fb[:], ACT.Sin).then_inc(f_sin, 1)
            for u in range(6, 12):
                xt_copy(u)
            act_e.wait_ge(f_arg, 2)
            act_e.activation(zh[:], fb[:], ACT.Sin).then_inc(f_sin, 1)
            act_e.wait_ge(xt_copied, 12)
            for k in range(KD):
                square(0, k)
            last_spec = 0
            split_mod(0)
            split_mod(1)
            for f, (g, r, kind, pq, kt) in enumerate(FU):
                if kind == 1:
                    act_e.wait_ge(f_ready, f + 1)
                    if last_spec:
                        act_e.wait_ge(f_free, last_spec)
                    act_e.activation(fE[:], acc_ps[:, f % 2, 0:512], ACT.Copy).then_inc(f_even, 1)
                    last_spec = f + 1
                if 2 <= f < MOD_A:
                    split_mod(f)
                if f in (7, 9):
                    split_w((f - 7) // 2)
            norm_std(0)
            act_e.wait_ge(asc_done, 2)
            act_e.wait_ge(f_ready, len(FU))
            for k in range(KD):
                norm_apply(0, k)

            def expo(n):
                b = n % 2
                nk = att_keys(ATT[n][0])[1]
                act_e.wait_ge(s_sd, n + 1)
                act_e.activation(es[:, b], sd[:, b], ACT.Exp).then_inc(s_es, 1)
                for j in range(NJ):
                    act_e.activation(S[:, b, j, 0:P * nk], S[:, b, j, 0:P * nk], ACT.Exp, bias=nmx[:, b, j:j + 1],
                                     accum_out=den[:, b, j:j + 1]).then_inc(s_exp, 1)

            def values_out(n):
                qb, kv = ATT[n]
                nk = att_keys(qb)[1]
                for kb in range(nk):
                    c = bank("values", n, kb)
                    act_e.wait_ge(p_ready, p_first[n] + kb + 1)
                    act_e.activation(PT[:, n % 2, kb, :], wk[:, c:c + 512], ACT.Copy).then_inc(p_copied, 1)
                h = slice(HD * kv, HD * kv + HD)
                act_e.wait_ge(o_ready, n + 1)
                c = bank("values", n, nk)
                act_e.activation(qk[h, 0:NJ, P * qb:P * qb + P], wk[h, c:c + 512].rearrange("p (j n) -> p j n", j=NJ),
                                 ACT.Copy).then_inc(o_copied, 1)

            def turn_out(n):
                for e in range(2):
                    c = bank("turn", n, e)
                    act_e.wait_ge(turn_ready, 2 * n + e + 1)
                    if n >= 1:
                        act_e.wait_ge(fwd_ready, 4 * n)
                    act_e.activation(eoT[:, 512 * e:512 * e + 512], wk[:, c:c + 512], ACT.Copy).then_inc(turn_copied, 1)

            def inverse_out(n):
                for h in range(2):
                    c = bank("inverse", n, h)
                    act_e.wait_ge(inv_ready, 2 * n + h + 1)
                    if n >= 1:
                        act_e.wait_ge(y_done, n)
                    act_e.activation(yeo[:, 512 * h:512 * h + 512], wk[:, c:c + 512], ACT.Copy).then_inc(inv_copied, 1)

            run = {"scores": expo, "values": values_out, "turn": turn_out, "inverse": inverse_out,
                   "forward": lambda n: None}
            for i in range(2):
                split_mod(MOD_A + i)
            for t in range(T_MERGE):
                s = t % 2
                act_e.wait_ge(acc_ready, t + 1)
                src = acc_ps[:, s, 0:T]
                if t < T_V:
                    act_e.activation(qk[:, t, :], src, ACT.Copy).then_inc(acc_free[s], 1)
                elif t == T_V:
                    act_e.activation(vtmp[:], src, ACT.Copy).then_inc(acc_free[s], 1)
                elif t < T_GATE:
                    m = t - T_HY
                    act_e.activation(xv[:, m, :], src, ACT.Identity, bias=vT[:, V_CB + m:V_CB + m + 1],
                                     scale=cwT[:, 12 + m:13 + m]).then_inc(cv_mid, 1)
                else:
                    i = t - T_GATE
                    if i >= 2:
                        act_e.wait_ge(gate_stored[i % 2], 16 * (i // 2))
                    act_e.activation(gst[:, i % 2, :], src, ACT.Sigmoid).then_inc(acc_free[s], 1)
                if t == T_HY:
                    act_e.wait_ge(v_turned, 1)
                    act_e.activation(V[:].rearrange("p b n -> p (b n)"), wk[:, 0:T], ACT.Copy).then_inc(v_rows, 1)
                split_w(t + 2)
                if t >= T_GATE:
                    i = t - T_GATE
                    act_e.wait_ge(acc_free[s], t // 2 + 1)
                    act_e.dma_start(gate_d[:, i, :], gst[:, i % 2, :]).then_inc(gate_stored[i % 2], 16)
                b = MB_A + t
                first, rest = split_stages(t)
                for kind, n in first:
                    run[kind](n)
                if t < T_GATE and MOD_BATCH[b][1] == 3:
                    split_mod(MOD_BATCH[b][0] + 2)
                for kind, n in rest:
                    run[kind](n)
                if t < T_GATE - 1:
                    for i in range(2):
                        split_mod(MOD_BATCH[b + 1][0] + i)

            act_e.wait_ge(z_done, len(STEPS))
            act_e.wait_ge(o_copied, len(ATT))
            act_e.wait_ge(acc_ready, T_MERGE)
            for i in range(2):
                act_e.wait_ge(gate_stored[i], 16 * KD)

            def gates_back(m):
                for x in range(2):
                    act_e.dma_start(gin[:, m % 2, x, :], gate_d[:, KD * x + m, :]).then_inc(ld_gate[m % 2], 16)

            gates_back(0)
            gates_back(1)
            for k in range(KD):
                src = qk[:, k, :] if k < 4 else xv[:, 4 + k, :]
                act_e.activation(act[:, 0, k, :], src, ACT.Copy).then_inc(sp_hi, 1)

            for m in range(KD):
                act_e.wait_ge(mg_done, m + 1)
                act_e.activation(hid[:, 0, m, :], tmp[:, 2, :] if m % 2 else sqB[:], ACT.Copy).then_inc(mg_hi, 1)
                if m + 2 < KD:
                    gates_back(m + 2)
                split_w(T_MERGE + m + 2)
            for m in range(KD):
                act_e.wait_ge(acc_free[m % 2], A_OUT // 2 + m // 2 + 1)
                square(1, m)
                if m < KD - 2:
                    split_w(T_OUT + m + 2)
                else:
                    s = m % 2
                    split_w(T_OUT + m + 2, s, 16 * (landed_base[s] + 1))
            norm_std(1)
            act_e.wait_ge(asc_done, 4)
            for k in range(KD):
                norm_apply(1, k)

            def up(c):
                with act_e.Fori(0, KD // 2) as i:
                    for s in range(2):
                        u = c * 8 + i * 2 + s
                        act_e.wait_ge(acc_ready, A_MLP + 1 + c * 16 + i * 2 + s)
                        act_e.activation(tmp[:, s, :], acc_ps[:, s, 0:T], ACT.Relu)\
                            .then_inc(acc_free[s], 1)
                        split_w(T_MLP + 2 + c * 16 + i * 2 + s, s, (landed_base[s] + 2 + c * 8 + i) * 16)
                        act_e.wait_ge(up_sq, u + 1)
                        act_e.activation(hid[:, 0, bass.ds(i * 2 + s, 1), :].rearrange("p o n -> p (o n)"),
                                         hfB[:, s, :], ACT.Copy).then_inc(hid_hi, 1)

            with act_e.Fori(0, NCH - 1) as c:
                up(c)
                with act_e.Fori(0, KD // 2) as i:
                    for s in range(2):
                        split_w(T_MLP + KD + 2 + c * 16 + i * 2 + s, s, (landed_base[s] + 6 + c * 8 + i) * 16)
            up(NCH - 1)
            for m in range(KD):
                if m < KD - 2:
                    t = T_MLP + 16 * (NCH - 1) + KD + m + 2
                    split_w(t, m % 2, 16 * (landed_base[m % 2] + (t - T_MLP) // 2 + 1))
                act_e.wait_ge(acc_free[m % 2], A_OUT // 2 + 1 + KD * NCH + m // 2)
                square(2, m)
            norm_std(2)
            act_e.wait_ge(asc_done, 6)
            for k in range(KD):
                norm_apply(2, k)

        @block.vector
        def _(dve):
            def split_w(t, s=None, count=None):
                s = t % 2 if s is None else s
                dve.wait_ge(landed[s], landed_at[t] if count is None else count)
                dve.wait_ge(hi_done, t + 1)
                dve.tensor_tensor(wlo[s][:], raw[s][:], whi[s][:], ALU.subtract).then_inc(lo_done, 1)

            def norm_acc(q, k):
                sq, acc, _, tn, _ = NB[q]
                dve.wait_ge(n_sq, KD * q + k + 1)
                if k == 0:
                    dve.tensor_copy(acc[:], sq[:]).then_inc(n_acc, 1)
                else:
                    dve.wait_ge(n_acc, KD * q + k)
                    dve.tensor_tensor(acc[:], acc[:], sq[:] if k % 2 == 0 else tn[:, 1], ALU.add).then_inc(n_acc, 1)

            def norm_rstd(q):
                rstd = NB[q][2]
                dve.wait_ge(n_std, q + 1)
                dve.reciprocal(rstd[:], rstd[:]).then_inc(n_rstd, 1)
                dve.wait_ge(n_rstd, q + 1)

            def norm_scale(q):
                for g in range(2):
                    v = (V_N1, V_N2, V_NF)[q]
                    sc = (SC1, SC2, SCF)[q]
                    dve.scalar_tensor_tensor(asc[:, q, :, g], modT[:, sc:sc + KD, g], 1.0, vT[:, v:v + KD],
                                             ALU.add, ALU.mult).then_inc(asc_done, 1)

            def norm_t(q, k):
                if k >= 2:
                    dve.wait_ge(n_hf, 16 * q + 2 * k - 2)
                dve.tensor_tensor(NB[q][3][:, k % 2], xT[:, k, :], NB[q][2][:], ALU.mult).then_inc(n_t, 1)

            def norm_lo(q, k):
                dve.wait_ge(n_hi, KD * q + k + 1)
                dve.tensor_tensor(act[:, 1, k, :], NB[q][4][:, k % 2], act[:, 0, k, :], ALU.subtract).then_inc(n_lo, 1)

            def norm_apply(q):
                for k in range(KD + 1):
                    if k < KD:
                        norm_t(q, k)
                    if k >= 1:
                        norm_lo(q, k - 1)

            def split_mod(mt):
                raw_m, mhi, mlo = mod_bufs(mt)
                dve.wait_ge(ld_mod[mt % 2], 16 * (mt // 2 + 1))
                dve.wait_ge(m_hi, mt + 1)
                dve.tensor_tensor(mlo[:, mt % 2], raw_m[:, mt % 2], mhi[:, mt % 2], ALU.subtract).then_inc(m_lo, 1)

            def mod_rows(b):
                mt, n = MOD_BATCH[b]
                dve.wait_ge(mod_used, mt + n)
                if b >= 1:
                    dve.wait_ge(m_sum, b)
                dve.tensor_copy(mrow[:, 0:P * n], wk[0:4, 1536:1536 + P * n]).then_inc(m_row, 1)

            def mod_out(b):
                mt, n = MOD_BATCH[b]
                dve.wait_ge(m_sum, b + 1)
                for g in range(2):
                    last = dve.tensor_tensor(
                        modT[:, mt:mt + n, g], wk[:, 1920:1920 + 2 * n].rearrange("p (j g) -> p j g", g=2)[:, :, g],
                        vT[:, V_BA + mt:V_BA + mt + n], ALU.add)
                last.then_inc(mod_done, 1)

            def chain(ins):
                steps[0] += 1
                ins.then_inc(f_step, 1)
                dve.wait_ge(f_step, steps[0])

            steps = [0]
            dve.wait_ge(vt_ready, 1)
            dve.tensor_copy(vT[:], wk[:, 1024:1024 + V_N]).then_inc(vt_copied, 1)
            dve.tensor_copy(cwT[:], wk[:, 1280:1316]).then_inc(vt_copied, 1)
            dve.wait_ge(csig_done, 1)
            dve.wait_ge(vt_copied, 2)
            dve.tensor_tensor(cact[:], csig[:], vT[:, V_C:V_C + 16], ALU.mult).then_inc(cact_done, 1)
            dve.tensor_tensor(sel[:], ident[0:4, 0:2], ident[0:4, 2:4], ALU.add).then_inc(sel_done, 1)
            dve.wait_ge(cst_hi, 1)
            dve.tensor_tensor(cst[:, :, 2:4], cact[:].rearrange("p (g k) -> p k g", g=2), cst[:, :, 0:2],
                              ALU.subtract).then_inc(cst_lo, 1)
            dve.wait_ge(ld_filt, 16 * 6)
            for layer in range(2):
                dve.wait_ge(fm_ready, layer + 1)
                chain(dve.tensor_scalar(fa[:], acc_ps[0:64, layer, 0:T], fv[:, 2 * layer:2 * layer + 1],
                                        fv[:, 2 * layer + 1:2 * layer + 2], ALU.add, ALU.mult))
                chain(dve.tensor_scalar(fk[:], fa[:], 0.5 / PI, MAGIC, ALU.mult, ALU.add))
                chain(dve.tensor_scalar(fk[:], fk[:], MAGIC, None, ALU.subtract))
                if layer == 1:
                    dve.wait_ge(f_sin, 1)
                for part, src in ((TWO_PI_A, fa), (TWO_PI_B, fb), (TWO_PI_C, fb)):
                    chain(dve.scalar_tensor_tensor(fb[:], fk[:], -part, src[:], ALU.mult, ALU.add))
                dve.tensor_scalar(fb[:], fb[:], 3.1415925, -3.1415925, ALU.min, ALU.max).then_inc(f_arg, 1)
                if layer == 0:
                    dve.wait_ge(ld_filt2, 16 * 5)
                    dve.tensor_tensor(w3eo[:, 0, :], w3[:, 0:1024], w3[:, 1024:2048], ALU.add)
                    dve.tensor_tensor(w3eo[:, 1, :], w3[:, 0:1024], w3[:, 1024:2048], ALU.subtract).then_inc(w3_sum, 1)
            for k in range(KD):
                norm_acc(0, k)
            split_mod(0)
            split_mod(1)
            e = 0
            for f, (g, r, kind, p, q) in enumerate(FU):
                mt = f - 2
                if mt in MOD_ENDS:
                    mod_rows(MOD_ENDS.index(mt))
                dve.wait_ge(f_ready, f + 1)
                if kind == 0:
                    prev = [spec_end[x] for x in ((0, 0), (0, 1), (1, 0), (1, 1)) if spec_end[x] <= f]
                    if prev:
                        dve.wait_ge(f_ready, prev[-1])
                    d = dec if g == 0 else dec_p
                    dve.tensor_tensor(taps[:, p, 2 * q:2 * q + 2, :].rearrange("p m n -> p (m n)"),
                                      acc_ps[:, f % 2, :], d[:, 2 * q:2 * q + 2, :].rearrange("p m n -> p (m n)"),
                                      ALU.mult).then_inc(f_free, 1)
                else:
                    dve.wait_ge(f_even, e + 1)
                    if e >= 2:
                        dve.wait_ge(f_stored[e % 2], 16 * (e // 2))
                    odd = acc_ps[:, f % 2, 512:1024]
                    dve.tensor_tensor(fout[:, e % 2, 0, :], odd, fE[:], ALU.add)
                    a0, a1 = (fE[:], odd) if p == 0 else (odd, fE[:])
                    dve.tensor_tensor(fout[:, e % 2, 1, :], a0, a1, ALU.subtract).then_inc(f_free, 1)
                    e += 1
                if mt in MOD_ENDS:
                    mod_out(MOD_ENDS.index(mt))
                if 2 <= f < MOD_A:
                    split_mod(f)
                if f in (7, 9):
                    split_w((f - 7) // 2)
            dve.wait_ge(mod_done, MB_A)
            norm_scale(0)
            norm_rstd(0)
            norm_apply(0)

            def conv_sides(t):
                s, m = t % 2, t - T_HY
                dve.wait_ge(cv_mid, m + 1)
                for c0, L in GROUPS:
                    dve.scalar_tensor_tensor(xv[:, m, c0 + 1:c0 + L], acc_ps[:, s, c0:c0 + L - 1], cwT[:, m:m + 1],
                                             xv[:, m, c0 + 1:c0 + L], ALU.mult, ALU.add).then_inc(cv_part, 1)
                for g, (c0, L) in enumerate(GROUPS):
                    dve.wait_ge(cv_part, 2 * m + 1 + g)
                    last = dve.scalar_tensor_tensor(xv[:, m, c0:c0 + L - 1], acc_ps[:, s, c0 + 1:c0 + L],
                                                    cwT[:, 24 + m:25 + m], xv[:, m, c0:c0 + L - 1], ALU.mult, ALU.add)
                last.then_inc(acc_free[s], 1)

            def rope(j):
                dve.wait_ge(rot_ready, j + 1)
                if j >= 1:
                    dve.wait_ge(rope_done, j)
                dve.tensor_tensor(rt[:], wk[:, 0:T], sin[:], ALU.mult).then_inc(rope_step, 1)
                dve.tensor_tensor(qk[:, j, :], qk[:, j, :], cos[:], ALU.mult).then_inc(rope_mul, 1)
                dve.wait_ge(rope_step, j + 1)
                dve.wait_ge(rope_mul, j + 1)
                dve.tensor_tensor(qk[:, j, :], qk[:, j, :], rt[:], ALU.add).then_inc(rope_done, 1)

            def softmax_in(n):
                qb, kv = ATT[n]
                _, nk, m0 = att_keys(qb)
                b = n % 2
                if n >= 2:
                    dve.wait_ge(p_ready, sum(att_keys(q)[1] for q, _ in ATT[:n - 1]))
                for j in range(NJ):
                    c = bank("scores", n, j)
                    dve.wait_ge(s_ready, NJ * n + j + 1)
                    dve.tensor_tensor_reduce(S[:, b, j, 0:P * nk], wk[:, c:c + P * nk], mask[:, m0:m0 + P * nk],
                                             HD ** -0.5, sink[:, NJ * kv + j:NJ * kv + j + 1], ALU.add, ALU.max,
                                             mx[:, b, j:j + 1]).then_inc(s_max, 1)
                dve.wait_ge(s_max, NJ * n + NJ)
                dve.tensor_scalar(nmx[:, b], mx[:, b], -1.0, None, ALU.mult).then_inc(s_neg, 1)
                dve.tensor_tensor(sd[:, b], sink[:, NJ * kv:NJ * kv + NJ], mx[:, b], ALU.subtract).then_inc(s_sd, 1)

            def softmax_out(n):
                b = n % 2
                nk = att_keys(ATT[n][0])[1]
                dve.wait_ge(s_exp, NJ * n + NJ)
                dve.wait_ge(s_es, n + 1)
                dve.tensor_tensor(den[:, b], den[:, b], es[:, b], ALU.add).then_inc(s_den, 1)
                dve.wait_ge(s_den, n + 1)
                dve.reciprocal(rden[:, b], den[:, b]).then_inc(s_rden, 1)
                dve.wait_ge(s_rden, n + 1)
                for j in range(NJ):
                    last = dve.tensor_scalar(S[:, b, j, 0:P * nk], S[:, b, j, 0:P * nk], rden[:, b, j:j + 1], None, ALU.mult)
                last.then_inc(s_norm, 1)

            def products(n):
                dve.wait_ge(ld_spec[n % 2], 32 * (n // 2 + 1))
                for b in range(4):
                    dve.wait_ge(fwd_ready, 4 * n + b + 1)
                    if b >= 1:
                        dve.wait_ge(prod_done, 4 * n + b)
                    elif n >= 1:
                        dve.wait_ge(prod_done, 4 * n)
                    c = bank("forward", n, b)
                    src = wk[:, c:c + 512].rearrange("p (d n) -> p d n", d=2)
                    for pq in range(2):
                        dve.tensor_tensor(cm[:, 512 * pq:512 * pq + 512].rearrange("p (d n) -> p d n", d=2), src,
                                          spec[:, n % 2, pq, b:b + 1, :].broadcast_to([P, 2, 256]), ALU.mult).then_inc(cross_step, 1)
                    dve.wait_ge(cross_step, 8 * n + 2 * b + 2)
                    dve.tensor_tensor(Y[:, b, 0, :], cm[:, 0:256], cm[:, 768:1024], ALU.add)
                    dve.tensor_tensor(Y[:, b, 1, :], cm[:, 256:512], cm[:, 512:768], ALU.subtract).then_inc(prod_done, 1)

            def combine(n):
                u, r = STEPS[n]
                g, ct0, nct = UNITS[u]
                c0, L = GROUPS[g]
                full = yfull[:].rearrange("p (c n) -> p c n", n=L)
                dve.wait_ge(y_done, n + 1)
                for ct in range(nct):
                    hb = V_HB + 4 * r + ct0 + ct
                    dve.scalar_tensor_tensor(full[:, ct, :], xv[:, 8 + ct0 + ct, c0:c0 + L], vT[:, hb:hb + 1],
                                             full[:, ct, :], ALU.mult, ALU.add).then_inc(y_step, 1)
                    steps_y[0] += 1
                dve.wait_ge(y_step, steps_y[0])
                dve.tensor_tensor(xv[:, 8 + ct0:8 + ct0 + nct, c0:c0 + L], full,
                                  xv[:, 4 * r + ct0:4 * r + ct0 + nct, c0:c0 + L], ALU.mult).then_inc(z_done, 1)

            steps_y = [0]
            def attend(n):
                softmax_in(n)
                softmax_out(n)

            run = {"scores": attend, "values": lambda n: None, "turn": lambda n: None, "forward": products,
                   "inverse": combine}
            for i in range(2):
                split_mod(MOD_A + i)
            for t in range(T_MERGE):
                b = MB_A + t
                if 0 < t <= T_GATE:
                    mod_out(b - 1)
                if T_HY <= t < T_GATE:
                    conv_sides(t)
                if t == 1:
                    dve.wait_ge(ld_rope, 16 * 4)
                split_w(t + 2)
                if 1 <= t <= T_V:
                    rope(t - 1)
                if t == T_GATE:
                    dve.wait_ge(mod_done, len(MOD_BATCH))
                    norm_scale(1)
                    norm_scale(2)
                if t < T_GATE and MOD_BATCH[b][1] == 3:
                    split_mod(MOD_BATCH[b][0] + 2)
                for kind, n in STAGES[t]:
                    run[kind](n)
                if t < T_GATE:
                    mod_rows(b)
                if t < T_GATE - 1:
                    for i in range(2):
                        split_mod(MOD_BATCH[b + 1][0] + i)

            for k in range(KD):
                src = qk[:, k, :] if k < 4 else xv[:, 4 + k, :]
                dve.wait_ge(sp_hi, k + 1)
                dve.tensor_tensor(act[:, 1, k, :], src, act[:, 0, k, :], ALU.subtract).then_inc(sp_lo, 1)

            for m in range(KD):
                if m >= 1:
                    dve.wait_ge(mg_done, m)
                dve.wait_ge(ld_gate[m % 2], 32 * (m // 2 + 1))
                for x in range(2):
                    dve.wait_ge(acc_ready, A_MERGE + 2 * m + x + 1)
                    dve.tensor_tensor(tmp[:, x, :], acc_ps[:, x, 0:T], gin[:, m % 2, x, :], ALU.mult)\
                        .then_inc(acc_free[x], 1)
                mg = tmp[:, 2, :] if m % 2 else sqB[:]
                for x in range(2):
                    dve.wait_ge(acc_free[x], A_MERGE // 2 + m + 1)
                dve.tensor_tensor(mg, tmp[:, 0, :], tmp[:, 1, :], ALU.add).then_inc(mg_done, 1)
                split_w(T_MERGE + m + 2)
                dve.wait_ge(mg_hi, m + 1)
                dve.tensor_tensor(hid[:, 1, m, :], mg, hid[:, 0, m, :], ALU.subtract).then_inc(mg_lo, 1)

            def residual(s, m, gate, before):
                if before is not None:
                    dve.wait_ge(acc_free[s], before)
                for g, (c0, L) in enumerate(GROUPS):
                    row = xT[:, bass.ds(m, 1), c0:c0 + L].rearrange("p o n -> p (o n)")
                    last = dve.scalar_tensor_tensor(
                        row, acc_ps[:, s, c0:c0 + L], modT[:, bass.ds(gate + m, 1), g:g + 1].rearrange("p o n -> p (o n)"),
                        row, ALU.mult, ALU.add)
                last.then_inc(acc_free[s], 1)

            dve.wait_ge(ld_x2, 16)
            for m in range(KD):
                dve.wait_ge(acc_ready, A_OUT + m + 1)
                residual(m % 2, m, G1, None)
                if m < KD - 2:
                    split_w(T_OUT + m + 2)
                else:
                    split_w(T_OUT + m + 2, m % 2, 16 * (landed_base[m % 2] + 1))
                if m >= 1:
                    norm_acc(1, m - 1)
            norm_acc(1, KD - 1)
            norm_rstd(1)
            norm_apply(1)

            def up(c):
                with dve.Fori(0, KD // 2) as i:
                    for s in range(2):
                        u = c * 8 + i * 2 + s
                        dve.wait_ge(acc_free[s], A_MLP // 2 + 1 + c * 8 + i)
                        dve.tensor_tensor(hfB[:, s, :], tmp[:, s, :], tmp[:, s, :], ALU.mult).then_inc(up_sq, 1)
                        split_w(T_MLP + 2 + c * 16 + i * 2 + s, s, (landed_base[s] + 2 + c * 8 + i) * 16)
                        dve.wait_ge(hid_hi, u + 1)
                        m = bass.ds(i * 2 + s, 1)
                        dve.tensor_tensor(hid[:, 1, m, :].rearrange("p o n -> p (o n)"), hfB[:, s, :],
                                          hid[:, 0, m, :].rearrange("p o n -> p (o n)"), ALU.subtract).then_inc(hid_lo, 1)
                        dve.wait_ge(hid_lo, u + 1)

            with dve.Fori(0, NCH - 1) as c:
                up(c)
                with dve.Fori(0, KD // 2) as i:
                    for s in range(2):
                        dve.wait_ge(acc_ready, A_MLP + KD + 1 + c * 16 + i * 2 + s)
                        residual(s, i * 2 + s, G2, A_OUT // 2 + 1 + c * 8 + i)
                        split_w(T_MLP + KD + 2 + c * 16 + i * 2 + s, s, (landed_base[s] + 6 + c * 8 + i) * 16)
            up(NCH - 1)
            for m in range(KD):
                dve.wait_ge(acc_ready, A_MLP + 16 * (NCH - 1) + KD + m + 1)
                residual(m % 2, m, G2, A_OUT // 2 + 1 + KD * (NCH - 1) + m // 2)
                if m < KD - 2:
                    t = T_MLP + 16 * (NCH - 1) + KD + m + 2
                    split_w(t, m % 2, 16 * (landed_base[m % 2] + (t - T_MLP) // 2 + 1))
                if m >= 1:
                    norm_acc(2, m - 1)
            norm_acc(2, KD - 1)
            norm_rstd(2)
            for k in range(KD + 1):
                if k < KD:
                    norm_t(2, k)
                if k >= 1:
                    dve.wait_ge(y_turned, k)
                    dve.tensor_copy(onat[:, :, P * (k - 1):P * k],
                                    acc_ps[:, (k - 1) % 2, 0:T].rearrange("p (b n) -> p b n", b=NTB)).then_inc(y_copied, 1)


def tables():
    import numpy as np

    f = np.float32
    out = {"t_ident": np.eye(P)}
    dist = np.arange(3 * P)[None, :] - P - np.arange(P)[:, None]
    out["t_mask"] = np.where(np.abs(dist) <= 128, 0.0, -8e30)
    rot = np.zeros((P, P))
    for h in range(0, P, HD):
        for d in range(8):
            rot[h + d + 8, h + d] = -1.0
            rot[h + d, h + d + 8] = 1.0
    out["t_rot"] = rot
    pos = np.concatenate([np.arange(TS), np.arange(TP)])
    inv = f(500000.0) ** (-np.arange(8, dtype=f) * f(2.0) / f(16.0))
    ang = (pos.astype(f)[:, None] * inv[None, :]).astype(f).astype(np.float64)
    cos, sin = np.ones((P, T)), np.zeros((P, T))
    for h in range(0, P, HD):
        for d in range(16):
            cos[h + d] = np.cos(ang[:, d % 8])
            sin[h + d] = np.sin(ang[:, d % 8])
    out["t_cos"], out["t_sin"] = cos, sin
    zs = []
    for L in (TS, TP):
        t = np.linspace(0.0, 1.0, L, dtype=f)
        w = (f(2.0 * PI) * np.arange(L, dtype=f) / f(L)).astype(f)
        fr = np.linspace(1e-4, 15, 16, dtype=f)
        fw = (fr[:, None] * w[None, :]).astype(f).astype(np.float64)
        zs.append(np.concatenate([t[None].astype(np.float64), np.cos(fw), -np.sin(fw)], axis=0))
    out["t_z"] = np.concatenate(zs, axis=1)
    lo, hi = np.log(1e-2) / 1.5, np.log(1e-2) / 0.3
    deltas = np.abs(np.linspace(lo, hi, HW, dtype=f)).astype(np.float64)

    def rows(m):
        return m.reshape(-1, P, m.shape[1]).transpose(1, 0, 2)

    for L, n in ((TS, "s"), (TP, "p")):
        half = L // 2
        i = np.arange(half)
        m = np.concatenate([2 * i, 2 * i + 1])
        t = np.linspace(0.0, 1.0, L, dtype=f).astype(np.float64)[m]
        out[f"t_decay_{n}"] = rows(np.exp(-t[:, None] * deltas[None, :]) + 0.05)
        k1 = 2 * i
        k2 = L - 1 - k1
        mats = []
        for fn in (np.cos, np.sin):
            for odd in range(2):
                mats.append(rows(fn(np.pi * (k1[None, :] + 0.5) * (2 * i + odd)[:, None] / L)))
        out[f"t_filt_{n}"] = np.stack(mats, 1)
        fwd, inv_t = [], []
        for k in (k1, k2):
            th = np.pi * (k[None, :] + 0.5) * (i[:, None] + 0.5) / L
            for sg in (1, -1):
                m = np.cos(th) + sg * np.sin(th)
                fwd.append(rows(m))
                inv_t.append(rows(m.T / (2 * L)))
        out[f"t_fwd_{n}"] = np.stack(fwd, 1)
        out[f"t_inv_{n}"] = np.stack(inv_t, 1)
        if n == "p":
            for q in ("t_filt_p", "t_fwd_p", "t_inv_p"):
                out[q] = out[q][:, :, 0, :]
    return {k: np.ascontiguousarray(v.astype(f)) for k, v in out.items()}


_INS = ["x_prompt", "x_sample", "c_prompt", "c_sample", "w_ada", "b_ada", "norm1_g", "w_in", "attn_sink", "conv_w",
        "conv_b", "filt_w1", "filt_b1", "filt_freq1", "filt_w2", "filt_b2", "filt_freq2", "filt_w3", "hyena_bias",
        "w_attn_o", "w_hyena_o", "w_out", "norm2_g", "w_up", "w_down", "w_ada_final", "b_ada_final", "final_g"]


def kernel(**inputs):
    import numpy as np
    import concourse.bacc as bacc
    from concourse.bass_utils import run_bass_kernel_spmd

    nc = bacc.Bacc("TRN2", target_bir_lowering=False, num_devices=1)
    arrays, a = {}, {}
    host = {n: np.ascontiguousarray(inputs[n]) for n in _INS}
    host.update(tables())
    for n, v in host.items():
        arrays["in_" + n] = v
        a[n] = nc.dram_tensor("in_" + n, v.shape, mybir.dt.from_np(v.dtype), kind="ExternalInput").ap()
    out_p = nc.dram_tensor("out_p", (1, TP, D), F32, kind="ExternalOutput").ap()
    out_s = nc.dram_tensor("out_s", (1, TS, D), F32, kind="ExternalOutput").ap()
    program(nc, a, out_p, out_s)
    r = run_bass_kernel_spmd(nc, [arrays], core_ids=[0])
    return r.results[0]["out_p"], r.results[0]["out_s"]
```

```python
from contextlib import ExitStack

import concourse.bass as bass
from concourse import mybir

F32 = mybir.dt.float32
F32R = mybir.dt.float32r
ALU = mybir.AluOpType
ACT = mybir.ActivationFunctionType

P = 128
D = 1024
KD = D // P
TS, TP = 512, 256
T = TS + TP
NTB = T // P
GROUPS = ((0, TS), (TS, TP))
HD = 64
NJ = 4
QKV = 768
HY0 = QKV
HW = 512
GATE0 = HY0 + 3 * HW
DFF = 4 * D
NCH = DFF // D
EPS = 1e-6
PI = 3.141592653589793
TWO_PI_A = 6.28125
TWO_PI_B = 0.0019350051879882812
TWO_PI_C = 2 * PI - TWO_PI_A - TWO_PI_B
MAGIC = 12582912.0

T_Q, T_K, T_V, T_HY, T_GATE, T_MERGE, T_OUT, T_MLP = 0, 4, 5, 6, 18, 34, 42, 50
A_MERGE, A_OUT, A_MLP = 34, 50, 58
MOD_N = 64
MOD_A = 16
SH1, SC1, G1, SH2, SC2, G2, SHF, SCF = (8 * i for i in range(8))

V_C, V_N1, V_N2, V_NF, V_HB, V_BA, V_CB, V_N = 0, 16, 24, 32, 40, 48, 112, 124

UNITS = ((0, 0, 2), (0, 2, 2), (1, 0, 4))
STEPS = [(u, r) for r in range(2) for u in range(3)]
ATT = [(qb, kv) for qb in range(NTB) for kv in range(2)]

STAGES = {t: [] for t in range(T_MERGE)}
for _n in range(len(ATT)):
    STAGES[T_HY + 2 + _n].append(("values", _n))
for _n in range(len(ATT)):
    STAGES[T_HY + 1 + _n].append(("scores", _n))
for _n in range(len(STEPS)):
    STAGES[T_GATE + 1 + 2 * _n].insert(1 if _n == 0 else 0, ("turn", _n))
    STAGES[T_GATE + 2 + 2 * _n].append(("forward", _n))
    STAGES[T_GATE + 3 + 2 * _n].append(("inverse", _n))

MOD_BATCH = [(3 * b, min(3, MOD_A - 3 * b)) for b in range(6)]
for _t in range(T_GATE):
    MOD_BATCH.append((sum(MOD_BATCH[-1]), 2 if _t < T_HY else 3))
assert sum(MOD_BATCH[-1]) == MOD_N
MB_A = 6
MOD_ROWS = {_m + _n - 2: _b for _b, (_m, _n) in enumerate(MOD_BATCH[:MB_A])}
MOD_SUMS = {_f + 2: _b for _f, _b in MOD_ROWS.items()}


DVE_BLOCKS, POOL_BLOCKS = (0, 1, 3, 4), (2, 5)


def att_keys(qb):
    lo, hi = (0, 4) if qb < 4 else (4, 6)
    first, last = max(qb - 1, lo), min(qb + 1, hi - 1)
    return first, last - first + 1, P * (first - qb + 1)


def program(nc, a, out_p, out_s):
    with ExitStack() as ctx:
        def sem(name):
            return ctx.enter_context(nc.semaphore(name))

        def region(*layouts):
            def size(layout):
                total = 0
                for _, shape, _ in layout:
                    n = 1
                    for d in shape[1:]:
                        n *= d
                    total += n
                return total

            assert max(map(size, layouts)) == size(layouts[-1])
            got = []
            for layout in layouts[:-1]:
                with ExitStack() as e:
                    got.append([e.enter_context(nc.sbuf_tensor(*t)) for t in layout])
            got.append([ctx.enter_context(nc.sbuf_tensor(*t)) for t in layouts[-1]])
            return got

        def sb(name, shape, dt=F32):
            return ctx.enter_context(nc.sbuf_tensor(name, shape, dt))

        raw = [sb(f"w_raw{i}", [P, KD, P]) for i in range(2)]
        whi = [sb(f"w_hi{i}", [P, KD, P], F32R) for i in range(2)]
        wlo = [sb(f"w_lo{i}", [P, KD, P], F32R) for i in range(2)]
        (w3, w3eo, ftab, dec, taps), (shrow,), (act,) = region(
            [("filt_w3", [P, 2048], F32), ("filt_w3eo", [P, 2, 1024], F32), ("filt_tab", [P, 4, 2, 256], F32),
             ("filt_decay", [P, 4, 512], F32), ("filt_taps", [P, 2, 4, 512], F32)],
            [("shift_rows", [P, 2, D], F32)],
            [("act_hilo", [P, 2, KD, T], F32R)])
        ((zh, fa, fb, fk, h1, zst, fout, sqA, accA, tnA, hfA, vrow, vrow2, fE_b),
         (_, fout_b),
         (cos, sin, rt, vtmp, S, PT, _, mask, rot),
         (_, rawF, rawFp),
         (gst, tabFp_hi, tabIp, tabFp_lo, tabI, tabF_hi, tabF_lo, spec, cm), (hid,)) = region(
            [("filt_zh", [P, T], F32), ("filt_arg", [P, T], F32), ("filt_red", [P, T], F32),
             ("filt_turn", [P, T], F32), ("filt_h1", [64, T], F32), ("filt_h2_hilo", [P, T], F32R), ("filt_out", [P, 2, 2, 512], F32),
             ("n0_sq", [P, T], F32), ("n0_acc", [P, T], F32),
             ("n0_t", [P, 2, T], F32), ("n0_h", [P, 2, T], F32), ("vec_rows", [P, P], F32),
             ("conv_rows", [36, P], F32), ("filt_even_b", [P, 512], F32)],
            [("r2_gap0", [P, T], F32), ("filt_out_b", [P, 2, 2, 512], F32)],
            [("rope_cos", [P, T], F32), ("rope_sin", [P, T], F32), ("rope_rot", [P, T], F32),
             ("v_tmp", [P, T], F32), ("att_s", [P, 2, NJ, 384], F32), ("att_pT", [P, 2, 3, NJ * P], F32),
             ("r2_gap1", [P, 2560], F32), ("mask", [P, 384], F32), ("rope_perm", [P, P], F32)],
            [("r2_gap2", [P, 9216], F32), ("dft_fwd_raw", [P, 4, 2, 256], F32), ("dft_fwd_p_raw", [P, 4, P], F32)],
            [("gates_out", [P, 2, T], F32), ("dft_fwd_p_hi", [P, 4, P], F32R), ("dft_inv_p", [P, 4, P], F32),
             ("dft_fwd_p_lo", [P, 4, P], F32R), ("dft_inv", [P, 4, 2, 256], F32),
             ("dft_fwd_hi", [P, 4, 2, 256], F32R), ("dft_fwd_lo", [P, 4, 2, 256], F32R),
             ("hy_spec", [P, 2, 4, 256], F32), ("hy_cross", [P, 1024], F32)],
            [("hidden_hilo", [P, 2, KD, T], F32R)])
        (mrawB, mhiB, mloB), (eo, eoT_hi, Y, yeo, yfull), (xT,) = region(
            [("mod_rawB", [P, 2, KD, P], F32), ("mod_hiB", [P, 2, KD, P], F32R), ("mod_loB", [P, 2, KD, P], F32R)],
            [("hy_fold", [P, 1024], F32), ("hy_foldT_hi", [P, 1024], F32R), ("hy_prod", [P, 4, 2, 256], F32),
             ("hy_halves", [P, 1024], F32), ("hy_y", [P, 1024], F32)],
            [("xT", [P, KD, T], F32)])
        ((mrawA, mhiA, mloA, xnat, ftab_p, dec_p), (xv, qk, V), (_, eoT_lo), (_, gin),
         (tmp, sqB, accB, tnB, hfB, onat, _)) = region(
            [("mod_rawA", [P, 2, KD, P], F32), ("mod_hiA", [P, 2, KD, P], F32R), ("mod_loA", [P, 2, KD, P], F32R),
             ("x_rows", [P, NTB, D], F32), ("filt_tab_p", [P, 4, P], F32), ("filt_decay_p", [P, 2, 512], F32)],
            [("hy_xv", [P, 12, T], F32), ("qk", [P, 5, T], F32), ("v_rows", [P, NTB, P], F32)],
            [("r4_gap2", [P, 16 * T], F32), ("hy_foldT_lo", [P, 1024], F32R)],
            [("r4_gap", [P, 4 * T], F32), ("gates_in", [P, 2, 2, T], F32)],
            [("ev_tmp", [P, 3, T], F32), ("n_sq", [P, T], F32), ("n_acc", [P, T], F32),
             ("n_t", [P, 2, T], F32), ("n_h", [P, 2, T], F32), ("y_rows", [P, NTB, D], F32),
             ("r4_rest", [P, T], F32)])
        NB = [(sqA, accA, tnA, hfA), (sqB, accB, tnB, hfB), (sqB, accB, tnB, hfB)]

        ident = sb("ident", [P, P])
        ones = sb("ones", [P, P])
        cst = sb("c_hilo", [P, KD, 66], F32R)
        sel = sb("mod_sel", [4, 2])
        mrow = sb("mod_rows", [4, 3 * P])
        vT = sb("vecT", [P, V_N])
        cwT = sb("conv_wT", [P, 36])
        csig = sb("c_sig", [P, 16])
        cact = sb("c_act", [P, 16])
        modT = sb("modT", [P, 64, 2])
        asc = sb("norm_scale", [P, 3, KD, 2])
        fE = [sb("filt_even", [P, 512]), fE_b]
        fw1 = sb("filt_w1", [33, 64])
        fw2 = sb("filt_w2", [64, P])
        fv = sb("filt_vec", [P, 4])
        sink = sb("sink", [P, 8])
        mx = sb("att_max", [P, 2, NJ])
        nmx = sb("att_negmax", [P, 2, NJ])
        sd = sb("att_sinkd", [P, 2, NJ])
        es = sb("att_sinke", [P, 2, NJ])
        den = sb("att_den", [P, 2, NJ])
        rden = sb("att_rden", [P, 2, NJ])
        epsc = sb("eps", [P, 1])
        rs = sb("norm_rstd", [P, NTB])

        acc_ps = ctx.enter_context(nc.psum_tensor("acc_ps", [P, 2, 1024], F32))
        wk = ctx.enter_context(nc.psum_tensor("wk", [P, 2048], F32))

        xT_d = nc.dram_tensor("xT_spill", [P, KD * T], F32).ap()
        gate_d = nc.dram_tensor("gate_spill", [P, 16 * T], F32).ap().rearrange("p (i n) -> p i n", n=T)
        spec_d = [nc.dram_tensor(f"spec{g}", [2, 2, P, (4, 2)[g] * 512], F32).ap() for g in range(2)]

        landed = [sem(f"w_landed{i}") for i in range(2)]
        hi_done, lo_done = sem("w_hi_done"), sem("w_lo_done")
        acc_ready = sem("acc_ready")
        acc_free = [sem(f"acc_free{i}") for i in range(2)]
        ld_vec, ld_z, ld_filt, ld_filt_b, ld_w3, ld_filt2, ld_rope, ld_tab, ld_x2 = (
            sem(n) for n in ("ld_vec", "ld_z", "ld_filt", "ld_filt_b", "ld_w3", "ld_filt2", "ld_rope", "ld_tab", "ld_xback"))
        ld_x = [sem(f"ld_x{i}") for i in range(NTB)]
        ld_mod = [sem(f"ld_mod{i}") for i in range(2)]
        ld_spec, ld_fwd, tab_hi, tab_lo, turn_lo = (sem(n) for n in ("ld_spec", "ld_fwd", "tab_hi", "tab_lo", "turn_lo"))
        ld_gate = [sem(f"ld_gate{i}") for i in range(2)]
        gate_stored = [sem(f"gate_stored{i}") for i in range(2)]
        cst_zero, cst_hi, cst_lo, sel_done = (
            sem(n) for n in ("cst_zero", "cst_hi", "cst_lo", "sel_done"))
        m_hi, m_lo, m_row, m_sum = sem("mod_hi"), sem("mod_lo"), sem("mod_row"), sem("mod_sum")
        ones_set = sem("ones_set")
        vt_ready, vt_copied, csig_done, cact_done = (sem(n) for n in ("vt_ready", "vt_copied", "csig", "cact"))
        xt_ready, xt_copied, xt_spilled = sem("xt_ready"), sem("xt_copied"), sem("xt_spilled")
        fm_ready, f_arg, f_sin = sem("fm_ready"), sem("f_arg"), sem("f_sin")
        w3_sum, w3_hi, w3_lo, z_hi, z_lo = (sem(n) for n in ("w3_sum", "w3_hi", "w3_lo", "z_hi", "z_lo"))
        f_ready, f_free, f_even = sem("f_ready"), sem("f_free"), sem("f_even")
        f_stored = [sem(f"f_stored{i}") for i in range(4)]
        mod_used, mod_done, asc_done = sem("mod_used"), sem("mod_done"), sem("asc_done")
        n_sq, n_acc, n_ps, n_std, n_rstd, n_spread, n_t, n_hf, n_hi, n_lo = (
            sem(n) for n in ("n_sq", "n_acc", "n_ps", "n_std", "n_rstd", "n_spread", "n_t", "n_hf", "n_hi", "n_lo"))
        cv_mid, cv_part = sem("cv_mid"), sem("cv_part")
        rot_ready, rope_step, rope_done = sem("rot_ready"), sem("rope_step"), sem("rope_done")
        v_turned, v_rows = sem("v_turned"), sem("v_rows_done")
        fold_done, turn_ready, turn_copied = sem("fold_done"), sem("turn_ready"), sem("turn_copied")
        fwd_ready, cross_step, prod_done = sem("fwd_ready"), sem("cross_step"), sem("prod_done")
        inv_ready, inv_copied, y_done, y_step, z_done = (
            sem(n) for n in ("inv_ready", "inv_copied", "y_done", "y_step", "z_done"))
        s_ready, s_max, s_neg, s_sd, s_es, s_exp, s_den, s_rden, s_norm = (
            sem(n) for n in ("s_ready", "s_max", "s_neg", "s_sd", "s_es", "s_exp", "s_den", "s_rden", "s_norm"))
        p_ready, p_copied, o_ready, o_copied = (sem(n) for n in ("p_ready", "p_copied", "o_ready", "o_copied"))
        sp_hi, sp_lo = sem("sp_hi"), sem("sp_lo")
        f_step, rope_mul = sem("f_step"), sem("rope_mul")
        mg_done, mg_hi, mg_lo = sem("mg_done"), sem("mg_hi"), sem("mg_lo")
        up_sq, hid_hi, hid_lo = sem("up_sq"), sem("hid_hi"), sem("hid_lo")
        y_scaled, y_turned, y_copied, y_dve, y_normed, y_pool, stored = (
            sem(n) for n in ("y_scaled", "y_turned", "y_copied", "y_dve", "y_normed", "y_pool", "stored"))
        sh_ready, sh_copied = sem("sh_ready"), sem("sh_copied")

        def uses_to(t):
            if not isinstance(t, int) or t >= T_OUT:
                return t + A_OUT - T_OUT + 1
            return t + 1 if t < T_MERGE else A_MERGE + 2 * (t - T_MERGE) + 2

        n_dma = [2 if T_Q <= t < T_K else 3 if T_MERGE <= t < T_OUT else 1 for t in range(T_MLP)]
        landed_at = [16 * sum(n_dma[t % 2:t + 1:2]) for t in range(T_MLP)]
        landed_base = [sum(n_dma[s::2]) for s in range(2)]

        w_in = a["w_in"][0].rearrange("(k p) n -> p k n", p=P)
        w_ada = a["w_ada"][0].rearrange("(k p) n -> p k n", p=P)
        w_adaf = a["w_ada_final"].rearrange("(k p) n -> p k n", p=P)
        w_ao = a["w_attn_o"][0].rearrange("(h j p) n -> h p j n", h=2, p=HD)
        w_ho = a["w_hyena_o"][0].rearrange("(k p) n -> p k n", p=P)
        w_out = a["w_out"][0].rearrange("(k p) n -> p k n", p=P)
        w_up = a["w_up"][0].rearrange("(k p) n -> p k n", p=P)
        w_down = a["w_down"][0].rearrange("(c k p) n -> p c k n", k=KD, p=P)

        FU, tap_end, spec_end = [], {}, {}
        for part in (((0, 0),), ((0, 1),), ((1, 0), (1, 1))):
            for g, r in part:
                FU += [(g, r, 0, e, mp) for e in range(2) for mp in range(2 - g)]
                tap_end[g, r] = len(FU)
            for g, r in part:
                FU += [(g, r, 1, pq, kt) for pq in range(2) for kt in range(2 - g)]
                spec_end[g, r] = len(FU)
        taps_over = tap_end[1, 1]

        bank_of, bank_reader = {}, []

        def use(kind, n, readers):
            bank_of[kind, n] = len(bank_reader)
            bank_reader.extend(readers)

        p_first = [sum(att_keys(q)[1] for q, _ in ATT[:n]) for n in range(len(ATT))]
        for t in range(T_MERGE):
            for kind, n in STAGES[t]:
                if kind == "scores":
                    use(kind, n, [(s_max, NJ * n + j + 1) for j in range(NJ)])
                elif kind == "values":
                    use(kind, n, [(p_copied, p_first[n] + kb + 1) for kb in range(att_keys(ATT[n][0])[1])]
                        + [(o_copied, n + 1)])
                elif kind == "turn":
                    use(kind, n, [(turn_lo, 2 * n + e + 1) for e in range(2)])
                elif kind == "forward":
                    use(kind, n, [(prod_done, 4 * n + b + 1) for b in range(4)])
                else:
                    use(kind, n, [(inv_copied, 2 * n + e + 1) for e in range(2)])
        n_att = bank_of["turn", 0]
        place = [u % 3 if u < n_att else (u - n_att) % 4 for u in range(len(bank_reader))]

        def last_reader(u):
            before = [v for v in range(u) if place[v] == place[u]]
            if before:
                return bank_reader[before[-1]]
            return (mod_done, len(MOD_BATCH)) if place[u] == 3 else None

        def bank(kind, n, i):
            return 512 * place[bank_of[kind, n] + i]

        def mod_col(b):
            return 1024 if b < MB_A and b % 2 == 0 else 1536

        def mod_bufs(mt):
            return (mrawA, mhiA, mloA) if mt < MOD_A else (mrawB, mhiB, mloB)

        def flat(t):
            return t[:].rearrange("p k n -> p (k n)")

        def spec_out(e):
            return (fout, fout_b)[e % 4 // 2][:, e % 2]

        def out_rows(b):
            return out_s[0, P * b:P * b + P, :] if b < 4 else out_p[0, P * (b - 4):P * (b - 3), :]

        block = ctx.enter_context(nc.Block())

        @block.sync
        def _(sp):
            def weights(t):
                s = t % 2
                if t >= 2:
                    sp.wait_ge(hi_done, t - 1)
                    sp.wait_ge(lo_done, t - 1)
                if t < T_K:
                    j = t - T_Q
                    parts = [(raw[s][:, :, HD * h:HD * h + HD],
                              w_in[:, :, (NJ * h + j) * HD:(NJ * h + j + 1) * HD]) for h in range(2)]
                elif t < T_MERGE:
                    c = 2 * NJ * HD + P * (t - T_K)
                    parts = [(raw[s][:], w_in[:, :, c:c + P])]
                elif t < T_OUT:
                    c = P * (t - T_MERGE)
                    parts = [(raw[s][HD * h:HD * h + HD, 0:4, :], w_ao[h, :, :, c:c + P]) for h in range(2)]
                    parts.append((raw[s][:, 4:8, :], w_ho[:, :, c:c + P]))
                else:
                    c = P * (t - T_OUT)
                    parts = [(raw[s][:], w_out[:, :, c:c + P])]
                for dst, src in parts:
                    sp.dma_start(dst, src).then_inc(landed[s], 16)

            def mod_load(mt):
                if mt >= 2:
                    sp.wait_ge(m_hi, mt - 1)
                    sp.wait_ge(m_lo, mt - 1)
                src = w_ada[:, :, P * mt:P * mt + P] if mt < 48 else w_adaf[:, :, P * (mt - 48):P * (mt - 47)]
                sp.dma_start(mod_bufs(mt)[0][:, mt % 2], src).then_inc(ld_mod[mt % 2], 16)

            sp.dma_start(zh[0:33, :], a["t_z"]).then_inc(ld_z, 16)
            for b in range(NTB):
                if b == 2:
                    sp.wait_ge(ld_vec, 16 * 12)
                src = a["x_sample"][0, P * b:P * b + P, :] if b < 4 else a["x_prompt"][0, P * (b - 4):P * (b - 3), :]
                sp.dma_start(xnat[:, b], src).then_inc(ld_x[b], 16)
                if b in (2, 3):
                    mod_load(b - 2)
            for mt in range(2, MOD_A):
                mod_load(mt)
                if mt == 3:
                    weights(0)
                if mt == 5:
                    weights(1)
            sp.wait_ge(xt_copied, 12)
            sp.dma_start(xT_d, xT[:].rearrange("p k n -> p (k n)")).then_inc(xt_spilled, 16)
            weights(2)
            weights(3)
            sp.wait_ge(xt_spilled, 16)
            sp.wait_ge(n_t, KD)
            for mt in range(MOD_A, MOD_A + 2):
                mod_load(mt)
            sp.wait_ge(n_lo, KD)
            for i in range(4):
                sp.wait_ge(f_stored[i], 16 * 3)
            for dst, name in ((rot, "t_rot"), (cos, "t_cos"), (sin, "t_sin"), (mask, "t_mask")):
                sp.dma_start(dst[:], a[name]).then_inc(ld_rope, 16)
            mt = MOD_A + 2
            for t in range(2, T_MERGE + 2):
                if t >= 4:
                    weights(t)
                for _ in range(2 if t - 2 < T_HY else 3):
                    if mt < MOD_N:
                        mod_load(mt)
                        mt += 1
                if t == 10:
                    sp.wait_ge(v_rows, 1)
                    for dst, name in ((rawF, "t_fwd_s"), (rawFp, "t_fwd_p")):
                        sp.dma_start(dst[:], a[name]).then_inc(ld_fwd, 16)
                    sp.dma_start(tabIp[:], a["t_inv_p"]).then_inc(ld_tab, 16)
                n = (t - 23) // 2
                if t >= 23 and t % 2 and n < len(STEPS):
                    if n == 0:
                        sp.wait_ge(o_copied, len(ATT))
                        sp.dma_start(tabI[:], a["t_inv_s"]).then_inc(ld_tab, 16)
                        sp.wait_ge(tab_lo, 2)
                    else:
                        sp.wait_ge(prod_done, 4 * n)
                    u, rr = STEPS[n]
                    g, ct0, nct = UNITS[u]
                    for pq in range(2):
                        src = spec_d[g][rr, pq].rearrange("p (b n) -> p b n", b=4)
                        if g == 0:
                            src = src[:, :, P * ct0:P * ct0 + 256]
                        sp.dma_start(spec[:, pq], src).then_inc(ld_spec, 16)
            weights(T_MERGE + 2)
            weights(T_MERGE + 3)
            sp.wait_ge(z_done, len(STEPS))
            sp.dma_start(xT[:].rearrange("p k n -> p (k n)"), xT_d).then_inc(ld_x2, 16)
            for t in range(T_MERGE + 4, T_MLP):
                weights(t)
            with sp.Fori(0, NCH) as c:
                with sp.Fori(0, KD // 2) as i:
                    for s in range(2):
                        t = T_MLP + c * 16 + i * 2 + s
                        sp.wait_ge(hi_done, t - 1)
                        sp.wait_ge(lo_done, t - 1)
                        sp.dma_start(raw[s][:], w_up[:, :, bass.ds(c * D + i * 256 + s * P, P)]).then_inc(landed[s], 16)
                with sp.Fori(0, KD // 2) as i:
                    for s in range(2):
                        t = T_MLP + KD + c * 16 + i * 2 + s
                        sp.wait_ge(hi_done, t - 1)
                        sp.wait_ge(lo_done, t - 1)
                        sp.dma_start(raw[s][:], w_down[:, bass.ds(c, 1), :, bass.ds(i * 256 + s * P, P)]
                                     .rearrange("p c k n -> p (c k) n")).then_inc(landed[s], 16)
            for i, b in enumerate(DVE_BLOCKS):
                sp.wait_ge(y_dve, i + 1)
                sp.dma_start(out_rows(b), onat[:, b]).then_inc(stored, 16)
            sp.wait_ge(stored, 16 * NTB)

        @block.gpsimd
        def _(pool):
            pool.memset(cst[:].bitcast(F32), 0.0).then_inc(cst_zero, 1)
            pool.memset(ones[:], 1.0).then_inc(ones_set, 1)
            pool.memset(epsc[:], EPS).then_inc(ones_set, 1)
            pool.dma_start(fw1[:], a["filt_w1"][0]).then_inc(ld_filt, 16)
            for i, n in enumerate(("filt_b1", "filt_freq1")):
                pool.dma_start(fv[0:64, i:i + 1], a[n].rearrange("o f -> f o")).then_inc(ld_filt, 16)
            for h in range(2):
                pool.dma_start(fw2[:, 64 * h:64 * h + 64], a["filt_w2"][0]).then_inc(ld_filt_b, 16)
                for i, n in enumerate(("filt_b2", "filt_freq2")):
                    pool.dma_start(fv[64 * h:64 * h + 64, 2 + i:3 + i], a[n].rearrange("o f -> f o")).then_inc(ld_filt_b, 16)
            for h in range(2):
                pool.dma_start(w3[64 * h:64 * h + 64, :], a["filt_w3"][0]).then_inc(ld_w3, 16)
            pool.wait_ge(ld_vec, 16 * 12)
            pool.dma_start(dec[:], a["t_decay_s"]).then_inc(ld_filt2, 16)
            pool.dma_start(ftab[:], a["t_filt_s"]).then_inc(ld_filt2, 16)
            pool.dma_start(dec_p[:], a["t_decay_p"]).then_inc(ld_filt2, 16)
            pool.dma_start(ftab_p[:], a["t_filt_p"]).then_inc(ld_filt2, 16)
            pool.wait_ge(ld_w3, 32)
            for i, op in enumerate((ALU.add, ALU.subtract)):
                pool.tensor_tensor(w3eo[:, i, :], w3[:, 0:1024], w3[:, 1024:2048], op).then_inc(w3_sum, 1)
            for i in range(2):
                pool.wait_ge(w3_sum, i + 1)
                pool.wait_ge(w3_hi, i + 1)
                pool.tensor_tensor(flat(wlo[i]), w3eo[:, i, :], flat(whi[i]), ALU.subtract).then_inc(w3_lo, 1)
            e = 0
            for f, (g, r, kind, pq, kt) in enumerate(FU):
                if kind == 1:
                    pool.wait_ge(f_free, f + 1)
                    dst = spec_d[g][r, pq].rearrange("p (s k n) -> p s k n", s=2, n=512)[:, :, kt, :]
                    pool.dma_start(dst, spec_out(e)).then_inc(f_stored[e % 4], 16)
                    e += 1
                if f < KD:
                    pool.wait_ge(n_sq, f + 1)
                    if f == 0:
                        pool.tensor_copy(accA[:], sqA[:]).then_inc(n_acc, 1)
                    else:
                        pool.wait_ge(n_acc, f)
                        pool.tensor_tensor(accA[:], accA[:], tnA[:, 1] if f % 2 else sqA[:], ALU.add).then_inc(n_acc, 1)

            def fold(n):
                u, r = STEPS[n]
                g, ct0, nct = UNITS[u]
                c0, L = GROUPS[g]
                src = xv[:, 8 + ct0:8 + ct0 + nct, c0:c0 + L]
                back = src[:, :, ::-1]
                e4 = eo[:].rearrange("p (c e n) -> p c e n", e=2, n=L // 2)
                if n == 0:
                    for s in range(2):
                        pool.wait_ge(acc_free[s], T_GATE // 2)
                    pool.wait_ge(mod_used, MOD_N)
                if n >= 1:
                    pool.wait_ge(turn_ready, 2 * n)
                if r == 1:
                    pool.wait_ge(z_done, n - 2)
                for i, op in enumerate((ALU.add, ALU.subtract)):
                    last = pool.tensor_tensor(e4[:, :, i, :], src[:, :, 0:L // 2], back[:, :, 0:L // 2], op)
                last.then_inc(fold_done, 1)

            def unfold(n):
                u, r = STEPS[n]
                g, ct0, nct = UNITS[u]
                L = GROUPS[g][1]
                y4 = yeo[:].rearrange("p (c e n) -> p c e n", e=2, n=L // 2)
                full = yfull[:].rearrange("p (c n) -> p c n", n=L)
                pool.wait_ge(inv_copied, 2 * n + 2)
                if n >= 1:
                    pool.wait_ge(z_done, n)
                pool.tensor_tensor(full[:, :, 0:L // 2], y4[:, :, 0, :], y4[:, :, 1, :], ALU.add)
                pool.tensor_tensor(full[:, :, ::-1][:, :, 0:L // 2], y4[:, :, 0, :], y4[:, :, 1, :],
                                   ALU.subtract).then_inc(y_done, 1)

            fold(0)
            for n in range(len(STEPS)):
                if n + 1 < len(STEPS):
                    fold(n + 1)
                unfold(n)

            for i, b in enumerate(POOL_BLOCKS):
                pool.wait_ge(y_normed, i + 1)
                pool.tensor_tensor(onat[:, b], onat[:, b], shrow[:, 1 - b // 4], ALU.add).then_inc(y_pool, 1)

        @block.tensor
        def _(pe):
            def gemm_k(slot, s, k, kw, src, first, last):
                for i, (w, x) in enumerate(((whi[s], 0), (whi[s], 1), (wlo[s], 0))):
                    for c0, L in GROUPS:
                        mm = pe.matmul(acc_ps[:, slot, c0:c0 + L], w[:, kw, :], src[:, x, k, c0:c0 + L],
                                       start=(first and i == 0), stop=(last and i == 2))
                return mm

            def gemm(t, src, parts=None, k_waits=()):
                s = t % 2
                pe.wait_ge(hi_done, t + 1)
                pe.wait_ge(lo_done, t + 1)
                parts = parts or [(t, range(KD))]
                for a_i, ks in parts:
                    if a_i >= 2:
                        pe.wait_ge(acc_free[a_i % 2], a_i // 2)
                    for k in ks:
                        for sm, base in k_waits:
                            pe.wait_ge(sm, base + k)
                        mm = gemm_k(a_i % 2, s, k, k, src, k == ks[0], k == ks[-1])
                    if ks[-1] != KD - 1:
                        mm.then_inc(acc_ready, 1)
                mm.then_inc(acc_ready, 1)

            def gemm_pair(between=None):
                for i in range(KD + 2):
                    if i < KD:
                        yield 0, i
                    if i == KD and between:
                        between()
                    if i >= 2:
                        yield 1, i - 2

            def mod_tile(b, i):
                mt = MOD_BATCH[b][0] + i
                _, mhi, mlo = mod_bufs(mt)
                pe.wait_ge(m_hi, mt + 1)
                pe.wait_ge(m_lo, mt + 1)
                if i == 0 and b >= 2:
                    pe.wait_ge(mod_done, b - 1 if b < MB_A else b)
                o = wk[0:66, mod_col(b) + P * i:mod_col(b) + P * i + P]
                for k in range(KD):
                    pe.matmul(o, cst[:, k, :], mhi[:, mt % 2, k, :], start=(k == 0), stop=False)
                    mm = pe.matmul(o, cst[:, k, :], mlo[:, mt % 2, k, :], start=False, stop=(k == KD - 1))
                mm.then_inc(mod_used, 1)

            def mod_sum(b):
                pe.wait_ge(m_row, b + 1)
                for i in range(MOD_BATCH[b][1]):
                    mm = pe.matmul(wk[:, mod_col(b) + 384 + 2 * i:mod_col(b) + 386 + 2 * i], mrow[:, P * i:P * i + P], sel[:],
                                   start=True, stop=True)
                mm.then_inc(m_sum, 1)

            def norm_sum(q):
                pe.wait_ge(n_acc, KD * q + KD)
                o = acc_ps[:, 0, 0:NTB] if q == 2 else wk[:, 0:NTB]
                for b in range(NTB):
                    mm = pe.matmul(o[:, b:b + 1], NB[q][1][:, P * b:P * b + P], ones[:, 0:1], start=True, stop=True)
                mm.then_inc(n_ps, 1)

            def norm_spread(q):
                pe.wait_ge(n_rstd, q + 1)
                for b in range(NTB):
                    mm = pe.matmul(wk[:, P * b:P * b + P], rs[:, b:b + 1].broadcast_to([P, P]), ident[:],
                                   start=True, stop=True)
                mm.then_inc(n_spread, 1)

            pe.wait_ge(ld_vec, 16 * 12)
            pe.transpose(wk[:, 1024:1024 + V_N], vrow[0:V_N, :], ident[0:V_N, 0:V_N])
            pe.transpose(wk[:, 1280:1316], vrow2[:], ident[0:36, 0:36]).then_inc(vt_ready, 1)

            def filt_mlp(layer):
                for c0, L in GROUPS:
                    if layer == 0:
                        mm = pe.matmul(acc_ps[0:64, 0, c0:c0 + L], fw1[:], zh[0:33, c0:c0 + L], start=True, stop=True)
                    else:
                        mm = pe.matmul(acc_ps[:, 1, c0:c0 + L], fw2[:], h1[:, c0:c0 + L], start=True, stop=True)
                mm.then_inc(fm_ready, 1)

            def turn_x(u):
                b, h = u // 2, u % 2
                pe.wait_ge(ld_x[b], 16)
                if u >= 2:
                    pe.wait_ge(xt_copied, u - 1)
                for k in range(4):
                    mm = pe.transpose(wk[:, 512 * (u % 2) + P * k:512 * (u % 2) + P * k + P],
                                      xnat[:, b, P * (4 * h + k):P * (4 * h + k) + P], ident[:])
                mm.then_inc(xt_ready, 1)

            pe.wait_ge(ld_filt, 16 * 3)
            pe.wait_ge(ld_z, 16)
            filt_mlp(0)
            for u in range(6):
                turn_x(u)
            pe.wait_ge(f_sin, 1)
            pe.wait_ge(ld_filt_b, 16 * 6)
            filt_mlp(1)
            pe.wait_ge(cst_lo, 1)
            pe.wait_ge(sel_done, 1)
            mod_tile(0, 0)
            mod_tile(0, 1)
            for u in range(6, 12):
                turn_x(u)
            pe.wait_ge(z_lo, 1)
            pe.wait_ge(w3_lo, 2)
            pe.wait_ge(ld_filt2, 16 * 4)
            for f, (g, r, kind, p, q) in enumerate(FU):
                c0, L = GROUPS[g]
                n_e = 2 - g
                if f >= 2:
                    pe.wait_ge(f_free, f - 1)
                if kind == 0:
                    for j in range(2):
                        m = 2 * q + j
                        odd, jj = (m // n_e, m % n_e)
                        t0 = c0 + 256 * jj + odd
                        for i, w in enumerate((whi[p], wlo[p])):
                            mm = pe.matmul(acc_ps[:, f % 2, 512 * j:512 * j + 512], zst[:, t0:t0 + 255:2],
                                           flat(w)[:, 512 * r:512 * r + 512], start=(i == 0), stop=(i == 1))
                else:
                    pe.wait_ge(f_free, tap_end[g, r])
                    tab = ftab if g == 0 else ftab_p[:].rearrange("p m (j n) -> p m j n", j=1)
                    for odd in range(2):
                        for j in range(n_e):
                            mm = pe.matmul(acc_ps[:, f % 2, 512 * odd:512 * odd + 512],
                                           tab[:, 2 * p + odd, j, P * q:P * q + P], taps[:, p, (2 * r if g else 0) + odd * n_e + j, :],
                                           start=(j == 0), stop=(j == n_e - 1))
                mm.then_inc(f_ready, 1)
                if f in MOD_SUMS:
                    mod_sum(MOD_SUMS[f])
                if 1 <= f < MOD_A - 1:
                    mod_tile((f + 1) // 3, (f + 1) % 3)
                if f == 12:
                    pe.wait_ge(ones_set, 2)
                    norm_sum(0)
                if f == 15:
                    norm_spread(0)

            def rope_turn(j):
                pe.wait_ge(acc_free[(T_Q + j) % 2], (T_Q + j) // 2 + 1)
                if j == 0:
                    pe.wait_ge(ld_rope, 16 * 4)
                else:
                    pe.wait_ge(rope_step, j)
                for c0, L in GROUPS:
                    mm = pe.matmul(wk[:, c0:c0 + L], rot[:], qk[:, j, c0:c0 + L], start=True, stop=True)
                mm.then_inc(rot_ready, 1)

            def turn_v():
                pe.wait_ge(acc_free[T_V % 2], T_V // 2 + 1)
                pe.wait_ge(rope_step, 5)
                for b in range(NTB):
                    mm = pe.transpose(wk[:, P * b:P * b + P], vtmp[:, P * b:P * b + P], ident[:])
                mm.then_inc(v_turned, 1)

            def take(kind, n, i):
                reader = last_reader(bank_of[kind, n] + i)
                if reader:
                    pe.wait_ge(*reader)
                return bank(kind, n, i)

            def scores(n, b):
                qb, kv = ATT[n]
                first, nk, _ = att_keys(qb)
                h = slice(HD * kv, HD * kv + HD)
                for j in range(NJ):
                    if j == NJ - 1 and b is not None:
                        mod_tile(b, 1)
                    c = take("scores", n, j)
                    pe.matmul(wk[:, c:c + P * nk], qk[h, j, P * qb:P * qb + P], qk[h, 4, P * first:P * (first + nk)],
                              start=True, stop=True).then_inc(s_ready, 1)

            def values(n, b):
                qb, kv = ATT[n]
                first, nk, _ = att_keys(qb)
                pe.wait_ge(s_norm, n + 1)
                done = p_first[n]
                for kb in range(nk):
                    c = take("values", n, kb)
                    for j in range(NJ):
                        mm = pe.transpose(wk[:, c + P * j:c + P * j + P], S[:, n % 2, j, P * kb:P * kb + P], ident[:])
                    mm.then_inc(p_ready, 1)
                if b is not None:
                    mod_tile(b, 0)
                c = take("values", n, nk)
                for kb in range(nk):
                    pe.wait_ge(p_copied, done + kb + 1)
                    mm = pe.matmul(wk[:, c:c + 512], V[:, first + kb, :], PT[:, n % 2, kb, :],
                                   start=(kb == 0), stop=(kb == nk - 1))
                mm.then_inc(o_ready, 1)

            def turn(n):
                g, _, nct = UNITS[STEPS[n][0]]
                h = GROUPS[g][1] // 2
                e4 = eo[:].rearrange("p (c e n) -> p c e n", e=2, n=h)
                pe.wait_ge(fold_done, n + 1)
                for e in range(2):
                    c = take("turn", n, e)
                    for j in range(h // P):
                        for ct in range(nct):
                            mm = pe.transpose(wk[:, c + j * 256 + P * ct:c + j * 256 + P * ct + P],
                                              e4[:, ct, e, P * j:P * j + P], ident[:])
                    mm.then_inc(turn_ready, 1)

            def forward(n):
                g, _, nct = UNITS[STEPS[n][0]]
                pe.wait_ge(turn_lo, 2 * n + 2)
                if n == 0:
                    pe.wait_ge(tab_lo, 2)
                for b in range(4):
                    c = take("forward", n, b)
                    ks, x = b // 2, b % 2
                    for d in range(2):
                        e = ks ^ d
                        o = wk[:, c + 256 * d:c + 256 * d + 256]
                        passes = ((0, eoT_hi), (0, eoT_lo), (1, eoT_hi))
                        terms = []
                        for j in range(2 if g == 0 else 1):
                            if g == 0:
                                tabs = [tb[:, 2 * ks + d, j, P * x:P * x + P] for tb in (tabF_hi, tabF_lo)]
                            else:
                                tabs = [tb[:, 2 * ks + d, :] for tb in (tabFp_hi, tabFp_lo)]
                            c1 = 512 * e + 256 * (j if g == 0 else x)
                            terms += [(tabs[i], src[:, c1:c1 + 256]) for i, src in passes]
                        for i, (w, v) in enumerate(terms):
                            mm = pe.matmul(o, w, v, start=(i == 0), stop=(i == len(terms) - 1))
                    mm.then_inc(fwd_ready, 1)

            def inverse(n):
                g, _, nct = UNITS[STEPS[n][0]]
                pe.wait_ge(prod_done, 4 * n + 4)
                if n == 0:
                    pe.wait_ge(ld_tab, 16 * 2)
                for ct in range(nct):
                    per = nct // 2
                    if ct % per == 0:
                        c = take("inverse", n, ct // per)
                    for part in range(2):
                        if g == 0:
                            o = wk[:, c + 256 * part:c + 256 * part + 256]
                            terms = [(Y[:, 2 * ks + kt, ks ^ part, P * ct:P * ct + P], tabI[:, 2 * ks + (ks ^ part), kt, :])
                                     for ks in range(2) for kt in range(2)]
                        else:
                            o = wk[:, c + 256 * (ct % 2) + P * part:c + 256 * (ct % 2) + P * part + P]
                            terms = [(Y[:, 2 * ks + ct // 2, ks ^ part, P * (ct % 2):P * (ct % 2) + P],
                                      tabIp[:, 2 * ks + (ks ^ part), :]) for ks in range(2)]
                        for i, (w, x) in enumerate(terms):
                            mm = pe.matmul(o, w, x, start=(i == 0), stop=(i == len(terms) - 1))
                    if ct % per == per - 1:
                        mm.then_inc(inv_ready, 1)

            run = {"scores": scores, "values": values, "turn": turn, "forward": forward, "inverse": inverse}
            for t in range(T_MERGE):
                b = MB_A + t
                if t == 0:
                    def first_mods():
                        for i in range(2):
                            mod_tile(b, i)

                    for s in range(2):
                        pe.wait_ge(hi_done, s + 1)
                        pe.wait_ge(lo_done, s + 1)
                    for s, k in gemm_pair(first_mods):
                        if k == 0:
                            pe.wait_ge(f_free, len(FU) - 1 + s)
                        pe.wait_ge(n_hi, k + 1)
                        pe.wait_ge(n_lo, k + 1)
                        mm = gemm_k(s, s, k, k, act, k == 0, k == KD - 1)
                        if k == KD - 1:
                            mm.then_inc(acc_ready, 1)
                    continue
                if t > 1:
                    gemm(t, act)
                if t == 1:
                    rope_turn(0)
                if 0 < t <= T_GATE:
                    mod_sum(b - 1)
                if 1 < t <= T_V:
                    rope_turn(t - 1)
                if t == T_HY:
                    turn_v()
                if t == T_HY + 1:
                    pe.wait_ge(v_rows, 1)
                kinds = {kind for kind, _ in STAGES[t]}
                mods = t < T_GATE
                if mods and "values" not in kinds:
                    mod_tile(b, 0)
                for kind, n in STAGES[t]:
                    if kind in ("values", "scores"):
                        run[kind](n, b if mods else None)
                    else:
                        run[kind](n)
                if mods and "scores" not in kinds:
                    mod_tile(b, 1)
                if mods and MOD_BATCH[b][1] == 3:
                    mod_tile(b, 2)

            def shift_rows(g):
                c = D * (1 - g)
                for k in range(KD):
                    mm = pe.matmul(wk[:, c + P * k:c + P * k + P],
                                   modT[:, SHF + k, g:g + 1].broadcast_to([P, P]), ident[:], start=True, stop=True)
                mm.then_inc(sh_ready, 1)

            for m in range(KD):
                gemm(T_MERGE + m, act, parts=[(A_MERGE + 2 * m, range(4)), (A_MERGE + 2 * m + 1, range(4, 8))],
                     k_waits=((sp_hi, 1), (sp_lo, 1)) if m == 0 else ())
            for m in range(KD):
                gemm(T_OUT + m, hid, parts=[(A_OUT + m, range(KD))],
                     k_waits=((mg_hi, 1), (mg_lo, 1)) if m == 0 else ())
            shift_rows(0)
            norm_sum(1)

            norm_spread(1)

            def weights_in(t, s, use):
                pe.wait_ge(hi_done, t + 1)
                pe.wait_ge(lo_done, t + 1)
                pe.wait_ge(acc_free[s], use)

            def up(c, first=0):
                with pe.Fori(first, KD // 2) as i:
                    for s in range(2):
                        weights_in(T_MLP + c * 16 + i * 2 + s, s, A_MLP // 2 + c * 8 + i)
                        for k in range(KD):
                            mm = gemm_k(s, s, k, k, act, k == 0, k == KD - 1)
                        mm.then_inc(acc_ready, 1)

            def down_tile(c, i, s):
                weights_in(T_MLP + KD + c * 16 + i * 2 + s, s, A_MLP // 2 + KD // 2 + c * 8 + i)
                for k in range(KD):
                    if s == 0 and k in (0, KD - 2, KD - 1):
                        need = KD - 2 if k == 0 else k + 1
                        pe.wait_ge(hid_hi, need + c * 8)
                        pe.wait_ge(hid_lo, need + c * 8)
                    mm = gemm_k(s, s, k, k, hid, k == 0, k == KD - 1)
                mm.then_inc(acc_ready, 1)

            def down(c):
                with pe.Fori(0, KD // 2) as i:
                    for s in range(2):
                        down_tile(c, i, s)

            for s in range(2):
                weights_in(T_MLP + s, s, A_MLP // 2)
            for s, k in gemm_pair():
                pe.wait_ge(n_hi, KD + k + 1)
                pe.wait_ge(n_lo, KD + k + 1)
                mm = gemm_k(s, s, k, k, act, k == 0, k == KD - 1)
                if k == KD - 1:
                    mm.then_inc(acc_ready, 1)
            up(0, first=1)
            down(0)
            with pe.Fori(1, NCH - 1) as c:
                up(c)
                down(c)
            up(NCH - 1)
            shift_rows(1)

            def turn_y(m):
                pe.wait_ge(y_scaled, m + 1)
                if m == 0:
                    pe.wait_ge(sh_copied, 1)
                if m >= 2:
                    pe.wait_ge(y_copied, m - 1)
                for b in range(NTB):
                    c = 1024 * (m % 2) + P * b
                    mm = pe.transpose(wk[:, c:c + P], hfB[:, m % 2, P * b:P * b + P], ident[:])
                mm.then_inc(y_turned, 1)

            for m in range(KD):
                down_tile(NCH - 1, m // 2, m % 2)
                if m >= 1:
                    turn_y(m - 1)
            pe.wait_ge(acc_free[0], A_MLP // 2 + KD * NCH)
            norm_sum(2)
            turn_y(KD - 1)

        @block.scalar
        def _(act_e):
            r0 = 0
            for src, n in ((a["c_sample"], 8), (a["c_prompt"], 8), (a["norm1_g"], 8), (a["norm2_g"], 8)):
                act_e.dma_start(vrow[r0:r0 + n, :], src.rearrange("o (k p) -> (o k) p", p=P)).then_inc(ld_vec, 16)
                r0 += n
            act_e.dma_start(vrow[V_NF:V_HB, :], a["final_g"].rearrange("(k p) -> k p", p=P)).then_inc(ld_vec, 16)
            act_e.dma_start(vrow[V_HB:V_BA, :], a["hyena_bias"][0].rearrange("o (k p) -> (o k) p", p=P)).then_inc(ld_vec, 16)
            act_e.dma_start(vrow[V_BA:V_BA + 48, :], a["b_ada"].rearrange("o (k p) -> (o k) p", p=P)).then_inc(ld_vec, 16)
            act_e.dma_start(vrow[V_BA + 48:V_CB, :], a["b_ada_final"].rearrange("(k p) -> k p", p=P)).then_inc(ld_vec, 16)
            act_e.dma_start(vrow[V_CB:V_N, :], a["conv_b"].rearrange("o (k p) -> (o k) p", p=P)).then_inc(ld_vec, 16)
            act_e.dma_start(vrow2[:], a["conv_w"][0].rearrange("i (k p) -> (i k) p", p=P)).then_inc(ld_vec, 16)
            act_e.dma_start(ident[:], a["t_ident"]).then_inc(ld_vec, 16)
            act_e.dma_start(sink[:], a["attn_sink"].partition_broadcast(P)).then_inc(ld_vec, 16)

            def split_mod(mt):
                raw_m, mhi, _ = mod_bufs(mt)
                act_e.wait_ge(ld_mod[mt % 2], 16 * (mt // 2 + 1))
                if mt >= 2:
                    act_e.wait_ge(mod_used, mt - 1)
                act_e.activation(mhi[:, mt % 2], raw_m[:, mt % 2], ACT.Copy).then_inc(m_hi, 1)

            def split_w(t, s=None, count=None):
                s = t % 2 if s is None else s
                act_e.wait_ge(landed[s], landed_at[t] if count is None else count)
                if count is not None or t >= 2:
                    act_e.wait_ge(acc_ready, uses_to(t - 2))
                act_e.activation(whi[s][:], raw[s][:], ACT.Copy).then_inc(hi_done, 1)

            def square(q, k):
                sq, _, tn, _ = NB[q]
                if k >= 2:
                    act_e.wait_ge(n_acc, KD * q + k - 1)
                dst = sq[:] if k % 2 == 0 else tn[:, 1]
                act_e.activation(dst, xT[:, k, :], ACT.Square).then_inc(n_sq, 1)

            def norm_std(q):
                act_e.wait_ge(n_ps, q + 1)
                o = acc_ps[:, 0, 0:NTB] if q == 2 else wk[:, 0:NTB]
                act_e.activation(rs[:], o, ACT.Sqrt, bias=epsc[:, 0:1], scale=1.0 / D).then_inc(n_std, 1)

            def norm_h(q, k):
                tn, hf = NB[q][2], NB[q][3]
                act_e.wait_ge(n_t, KD * q + k + 1)
                if k >= 2:
                    act_e.wait_ge(n_lo, KD * q + k - 1)
                sh = (SH1, SH2)[q]
                for g, (c0, L) in enumerate(GROUPS):
                    act_e.activation(hf[:, k % 2, c0:c0 + L], tn[:, k % 2, c0:c0 + L], ACT.Identity,
                                     bias=modT[:, sh + k, g:g + 1], scale=asc[:, q, k, g:g + 1]).then_inc(n_hf, 1)

            def norm_hi(q, k):
                act_e.wait_ge(n_hf, 16 * q + 2 * k + 2)
                act_e.activation(act[:, 0, k, :], NB[q][3][:, k % 2, :], ACT.Copy).then_inc(n_hi, 1)

            act_e.wait_ge(vt_copied, 2)
            act_e.activation(csig[:], vT[:, V_C:V_C + 16], ACT.Sigmoid).then_inc(csig_done, 1)

            act_e.wait_ge(cact_done, 1)
            act_e.wait_ge(cst_zero, 1)
            act_e.activation(cst[:, :, 0:2], cact[:].rearrange("p (g k) -> p k g", g=2), ACT.Copy).then_inc(cst_hi, 1)

            def xt_copy(u):
                b, h = u // 2, u % 2
                act_e.wait_ge(xt_ready, u + 1)
                act_e.activation(xT[:, 4 * h:4 * h + 4, P * b:P * b + P],
                                 wk[:, 512 * (u % 2):512 * (u % 2) + 512].rearrange("p (k n) -> p k n", k=4),
                                 ACT.Copy).then_inc(xt_copied, 1)

            for u in range(6):
                xt_copy(u)
            act_e.wait_ge(f_arg, 1)
            act_e.activation(h1[:], fb[0:64, :], ACT.Sin).then_inc(f_sin, 1)
            split_mod(0)
            split_mod(1)
            for u in range(6, 12):
                if u in (6, 8):
                    i = (u - 6) // 2
                    act_e.wait_ge(w3_sum, i + 1)
                    act_e.activation(flat(whi[i]), w3eo[:, i, :], ACT.Copy).then_inc(w3_hi, 1)
                if u == 10:
                    act_e.wait_ge(f_arg, 2)
                    act_e.activation(zh[:], fb[:], ACT.Sin).then_inc(f_sin, 1)
                    act_e.wait_ge(f_sin, 2)
                    act_e.activation(zst[:], zh[:], ACT.Copy).then_inc(z_hi, 1)
                xt_copy(u)
            act_e.wait_ge(xt_copied, 12)
            specs = []
            split_mod(2)
            split_mod(3)
            for f, (g, r, kind, pq, kt) in enumerate(FU):
                if kind == 1:
                    act_e.wait_ge(f_ready, f + 1)
                    if f == len(FU) - 1:
                        norm_hi(0, 0)
                        norm_hi(0, 1)
                    if len(specs) >= 2:
                        act_e.wait_ge(f_free, specs[-2])
                    act_e.activation(fE[len(specs) % 2][:], acc_ps[:, f % 2, 0:512], ACT.Copy).then_inc(f_even, 1)
                    specs.append(f + 1)
                if 1 <= f < MOD_A - 3:
                    split_mod(f + 3)
                if f < KD:
                    square(0, f)
                if f == 13:
                    norm_std(0)
                if f in (taps_over, taps_over + 1):
                    split_w(f - taps_over)
                if f == 21:
                    act_e.wait_ge(asc_done, 2)
                    norm_h(0, 0)
                    norm_h(0, 1)
            for k in range(2, KD):
                norm_h(0, k)
                norm_hi(0, k)

            def expo(n):
                b = n % 2
                nk = att_keys(ATT[n][0])[1]
                act_e.wait_ge(s_sd, n + 1)
                act_e.activation(es[:, b], sd[:, b], ACT.Exp).then_inc(s_es, 1)
                for j in range(NJ):
                    act_e.activation(S[:, b, j, 0:P * nk], S[:, b, j, 0:P * nk], ACT.Exp, bias=nmx[:, b, j:j + 1],
                                     accum_out=den[:, b, j:j + 1]).then_inc(s_exp, 1)

            def turned_out(n):
                nk = att_keys(ATT[n][0])[1]
                for kb in range(nk):
                    c = bank("values", n, kb)
                    act_e.wait_ge(p_ready, p_first[n] + kb + 1)
                    act_e.activation(PT[:, n % 2, kb, :], wk[:, c:c + 512], ACT.Copy).then_inc(p_copied, 1)

            def values_out(n):
                qb, kv = ATT[n]
                h = slice(HD * kv, HD * kv + HD)
                act_e.wait_ge(o_ready, n + 1)
                c = bank("values", n, att_keys(qb)[1])
                act_e.activation(qk[h, 0:NJ, P * qb:P * qb + P], wk[h, c:c + 512].rearrange("p (j n) -> p j n", j=NJ),
                                 ACT.Copy).then_inc(o_copied, 1)

            def turn_out(n):
                for e in range(2):
                    c = bank("turn", n, e)
                    act_e.wait_ge(turn_ready, 2 * n + e + 1)
                    if n >= 1:
                        act_e.wait_ge(fwd_ready, 4 * n)
                    act_e.activation(eoT_hi[:, 512 * e:512 * e + 512], wk[:, c:c + 512], ACT.Copy).then_inc(turn_copied, 1)
                if n == 0:
                    act_e.wait_ge(o_copied, len(ATT))
                    act_e.wait_ge(ld_fwd, 32)
                    act_e.activation(tabF_hi[:], rawF[:], ACT.Copy).then_inc(tab_hi, 1)
                    act_e.activation(tabFp_hi[:], rawFp[:], ACT.Copy).then_inc(tab_hi, 1)

            def inverse_out(n):
                for h in range(2):
                    c = bank("inverse", n, h)
                    act_e.wait_ge(inv_ready, 2 * n + h + 1)
                    if n >= 1:
                        act_e.wait_ge(y_done, n)
                    act_e.activation(yeo[:, 512 * h:512 * h + 512], wk[:, c:c + 512], ACT.Copy).then_inc(inv_copied, 1)

            def split_out(k):
                src = qk[:, k, :] if k < 4 else xv[:, 4 + k, :]
                act_e.activation(act[:, 0, k, :], src, ACT.Copy).then_inc(sp_hi, 1)

            run = {"scores": expo, "turn": turn_out, "inverse": inverse_out,
                   "forward": lambda n: None}
            for i in range(2):
                split_mod(MOD_A + i)
            for t in range(T_MERGE):
                s = t % 2
                act_e.wait_ge(acc_ready, t + 1)
                if t == T_MERGE - 1:
                    act_e.wait_ge(o_copied, len(ATT))
                    for k in range(2):
                        split_out(k)
                src = acc_ps[:, s, 0:T]
                if t < T_V:
                    act_e.activation(qk[:, t, :], src, ACT.Copy).then_inc(acc_free[s], 1)
                elif t == T_V:
                    act_e.activation(vtmp[:], src, ACT.Copy).then_inc(acc_free[s], 1)
                elif t < T_GATE:
                    m = t - T_HY
                    act_e.activation(xv[:, m, :], src, ACT.Identity, bias=vT[:, V_CB + m:V_CB + m + 1],
                                     scale=cwT[:, 12 + m:13 + m]).then_inc(cv_mid, 1)
                else:
                    i = t - T_GATE
                    if i >= 2:
                        act_e.wait_ge(gate_stored[i % 2], 16 * (i // 2))
                    act_e.activation(gst[:, i % 2, :], src, ACT.Sigmoid).then_inc(acc_free[s], 1)
                if t == T_HY:
                    act_e.wait_ge(v_turned, 1)
                    act_e.activation(V[:].rearrange("p b n -> p (b n)"), wk[:, 0:T], ACT.Copy).then_inc(v_rows, 1)
                if t == T_MERGE - 1:
                    for k in range(2, 4):
                        split_out(k)
                for kind, n in STAGES[t]:
                    if kind == "values":
                        turned_out(n)
                third = MOD_BATCH[MB_A + t][0] + 2 if t < T_GATE and MOD_BATCH[MB_A + t][1] == 3 else None
                if t == T_HY:
                    split_mod(third)
                split_w(t + 2)
                if t >= T_GATE:
                    i = t - T_GATE
                    act_e.wait_ge(acc_free[s], t // 2 + 1)
                    act_e.dma_start(gate_d[:, i, :], gst[:, i % 2, :]).then_inc(gate_stored[i % 2], 16)
                b = MB_A + t
                for kind, n in STAGES[t]:
                    if kind == "values":
                        values_out(n)
                if third is not None and t > T_HY:
                    split_mod(third)
                for kind, n in STAGES[t]:
                    if kind != "values":
                        run[kind](n)
                if t < T_GATE - 1:
                    for i in range(2):
                        split_mod(MOD_BATCH[b + 1][0] + i)

            def gates_back(m):
                act_e.wait_ge(gate_stored[m % 2], 16 * ((KD + m) // 2 + 1))
                for x in range(2):
                    act_e.dma_start(gin[:, m % 2, x, :], gate_d[:, KD * x + m, :]).then_inc(ld_gate[m % 2], 16)

            act_e.wait_ge(z_done, len(STEPS))
            gates_back(0)
            gates_back(1)
            for k in range(4, KD):
                split_out(k)

            for m in range(KD):
                act_e.wait_ge(mg_done, m + 1)
                act_e.activation(hid[:, 0, m, :], tmp[:, 2, :] if m % 2 else sqB[:], ACT.Copy).then_inc(mg_hi, 1)
                if m + 2 < KD:
                    gates_back(m + 2)
                split_w(T_MERGE + m + 2)
            for m in range(KD):
                act_e.wait_ge(acc_free[m % 2], A_OUT // 2 + m // 2 + 1)
                square(1, m)
                if m < KD - 2:
                    split_w(T_OUT + m + 2)
                else:
                    s = m % 2
                    split_w(T_OUT + m + 2, s, 16 * (landed_base[s] + 1))
            norm_std(1)
            act_e.wait_ge(asc_done, 4)
            for k in range(KD):
                norm_h(1, k)
                norm_hi(1, k)

            def up(c):
                with act_e.Fori(0, KD // 2) as i:
                    for s in range(2):
                        u = c * 8 + i * 2 + s
                        act_e.wait_ge(acc_ready, A_MLP + 1 + c * 16 + i * 2 + s)
                        act_e.activation(tmp[:, s, :], acc_ps[:, s, 0:T], ACT.Relu)\
                            .then_inc(acc_free[s], 1)
                        split_w(T_MLP + 2 + c * 16 + i * 2 + s, s, (landed_base[s] + 2 + c * 8 + i) * 16)
                        act_e.wait_ge(up_sq, u + 1)
                        act_e.activation(hid[:, 0, bass.ds(i * 2 + s, 1), :].rearrange("p o n -> p (o n)"),
                                         hfB[:, s, :], ACT.Copy).then_inc(hid_hi, 1)

            with act_e.Fori(0, NCH - 1) as c:
                up(c)
                with act_e.Fori(0, KD // 2) as i:
                    for s in range(2):
                        split_w(T_MLP + KD + 2 + c * 16 + i * 2 + s, s, (landed_base[s] + 6 + c * 8 + i) * 16)
            up(NCH - 1)

            def y_copy(m):
                act_e.wait_ge(y_turned, m + 1)
                c = 1024 * (m % 2)
                act_e.activation(onat[:, :, P * m:P * m + P], wk[:, c:c + T].rearrange("p (b n) -> p b n", b=NTB),
                                 ACT.Copy).then_inc(y_copied, 1)

            act_e.wait_ge(asc_done, 6)
            for m in range(KD):
                if m < KD - 2:
                    t = T_MLP + 16 * (NCH - 1) + KD + m + 2
                    split_w(t, m % 2, 16 * (landed_base[m % 2] + (t - T_MLP) // 2 + 1))
                if m == 0:
                    act_e.wait_ge(sh_ready, 2)
                    act_e.activation(shrow[:].rearrange("p g n -> p (g n)"), wk[:], ACT.Copy).then_inc(sh_copied, 1)
                    act_e.wait_ge(hid_lo, KD * NCH)
                act_e.wait_ge(acc_free[m % 2], A_OUT // 2 + 1 + KD * NCH + m // 2)
                square(2, m)
                if m >= 2:
                    act_e.wait_ge(y_turned, m - 1)
                for g, (c0, L) in enumerate(GROUPS):
                    last = act_e.activation(hfB[:, m % 2, c0:c0 + L], xT[:, m, c0:c0 + L], ACT.Copy,
                                            scale=asc[:, 2, m, g:g + 1])
                last.then_inc(y_scaled, 1)
                if m >= 1:
                    y_copy(m - 1)
            norm_std(2)
            y_copy(KD - 1)
            act_e.wait_ge(n_rstd, 3)
            act_e.wait_ge(y_copied, KD)
            for b in POOL_BLOCKS:
                act_e.activation(onat[:, b], onat[:, b], ACT.Copy, scale=rs[:, b:b + 1]).then_inc(y_normed, 1)
            for i, b in enumerate(POOL_BLOCKS):
                act_e.wait_ge(y_pool, i + 1)
                act_e.dma_start(out_rows(b), onat[:, b]).then_inc(stored, 16)

        @block.vector
        def _(dve):
            def split_w(t, s=None, count=None):
                s = t % 2 if s is None else s
                dve.wait_ge(landed[s], landed_at[t] if count is None else count)
                dve.wait_ge(hi_done, t + 1)
                dve.tensor_tensor(wlo[s][:], raw[s][:], whi[s][:], ALU.subtract).then_inc(lo_done, 1)

            def norm_acc(q, k):
                sq, acc, tn, _ = NB[q]
                dve.wait_ge(n_sq, KD * q + k + 1)
                if k == 0:
                    dve.tensor_copy(acc[:], sq[:]).then_inc(n_acc, 1)
                else:
                    dve.wait_ge(n_acc, KD * q + k)
                    dve.tensor_tensor(acc[:], acc[:], sq[:] if k % 2 == 0 else tn[:, 1], ALU.add).then_inc(n_acc, 1)

            def norm_rstd(q):
                dve.wait_ge(n_std, q + 1)
                dve.reciprocal(rs[:], rs[:]).then_inc(n_rstd, 1)

            def norm_scale(q):
                for g in range(2):
                    v = (V_N1, V_N2, V_NF)[q]
                    sc = (SC1, SC2, SCF)[q]
                    dve.scalar_tensor_tensor(asc[:, q, :, g], modT[:, sc:sc + KD, g], 1.0, vT[:, v:v + KD],
                                             ALU.add, ALU.mult).then_inc(asc_done, 1)

            def norm_t(q, k):
                if k == 0:
                    dve.wait_ge(n_spread, q + 1)
                if k >= 2:
                    dve.wait_ge(n_hf, 16 * q + 2 * k - 2)
                dve.tensor_tensor(NB[q][2][:, k % 2], xT[:, k, :], wk[:, 0:T], ALU.mult).then_inc(n_t, 1)

            def norm_lo(q, k):
                dve.wait_ge(n_hi, KD * q + k + 1)
                dve.tensor_tensor(act[:, 1, k, :], NB[q][3][:, k % 2], act[:, 0, k, :], ALU.subtract).then_inc(n_lo, 1)

            def norm_apply(q, first_t=0, first_lo=0):
                for k in range(first_t, KD + 1):
                    if k < KD:
                        norm_t(q, k)
                    if k >= first_lo + 1:
                        norm_lo(q, k - 1)

            def split_mod(mt):
                raw_m, mhi, mlo = mod_bufs(mt)
                dve.wait_ge(ld_mod[mt % 2], 16 * (mt // 2 + 1))
                dve.wait_ge(m_hi, mt + 1)
                dve.tensor_tensor(mlo[:, mt % 2], raw_m[:, mt % 2], mhi[:, mt % 2], ALU.subtract).then_inc(m_lo, 1)

            def mod_rows(b):
                mt, n = MOD_BATCH[b]
                dve.wait_ge(mod_used, mt + n)
                if b >= 1:
                    dve.wait_ge(m_sum, b)
                dve.tensor_copy(mrow[:, 0:P * n], wk[0:4, mod_col(b):mod_col(b) + P * n]).then_inc(m_row, 1)

            def mod_out(b):
                mt, n = MOD_BATCH[b]
                dve.wait_ge(m_sum, b + 1)
                c = mod_col(b) + 384
                for g in range(2):
                    last = dve.tensor_tensor(
                        modT[:, mt:mt + n, g], wk[:, c:c + 2 * n].rearrange("p (j g) -> p j g", g=2)[:, :, g],
                        vT[:, V_BA + mt:V_BA + mt + n], ALU.add)
                last.then_inc(mod_done, 1)

            def chain(ins):
                steps[0] += 1
                ins.then_inc(f_step, 1)
                dve.wait_ge(f_step, steps[0])

            steps = [0]
            dve.wait_ge(vt_ready, 1)
            dve.tensor_copy(vT[:], wk[:, 1024:1024 + V_N]).then_inc(vt_copied, 1)
            dve.tensor_copy(cwT[:], wk[:, 1280:1316]).then_inc(vt_copied, 1)
            dve.wait_ge(csig_done, 1)
            dve.wait_ge(vt_copied, 2)
            dve.tensor_tensor(cact[:], csig[:], vT[:, V_C:V_C + 16], ALU.mult).then_inc(cact_done, 1)
            dve.tensor_tensor(sel[:], ident[0:4, 0:2], ident[0:4, 2:4], ALU.add).then_inc(sel_done, 1)
            dve.wait_ge(cst_hi, 1)
            dve.tensor_tensor(cst[:, :, 2:4], cact[:].rearrange("p (g k) -> p k g", g=2), cst[:, :, 0:2],
                              ALU.subtract).then_inc(cst_lo, 1)
            dve.wait_ge(ld_filt, 16 * 3)
            for layer in range(2):
                dve.wait_ge(fm_ready, layer + 1)
                h = slice(0, P if layer else 64)
                if layer == 1:
                    dve.wait_ge(ld_filt_b, 16 * 6)
                chain(dve.tensor_scalar(fa[h], acc_ps[h, layer, 0:T], fv[h, 2 * layer:2 * layer + 1],
                                        fv[h, 2 * layer + 1:2 * layer + 2], ALU.add, ALU.mult))
                chain(dve.tensor_scalar(fk[h], fa[h], 0.5 / PI, MAGIC, ALU.mult, ALU.add))
                chain(dve.tensor_scalar(fk[h], fk[h], MAGIC, None, ALU.subtract))
                if layer == 1:
                    dve.wait_ge(f_sin, 1)
                for part, src in ((TWO_PI_A, fa), (TWO_PI_B, fb), (TWO_PI_C, fb)):
                    chain(dve.scalar_tensor_tensor(fb[h], fk[h], -part, src[h], ALU.mult, ALU.add))
                dve.tensor_scalar(fb[h], fb[h], 3.1415925, -3.1415925, ALU.min, ALU.max).then_inc(f_arg, 1)
                if layer == 0:
                    split_mod(0)
                    split_mod(1)
            dve.wait_ge(z_hi, 1)
            dve.tensor_tensor(zst[64:P, :], zh[64:P, :], zst[64:P, :], ALU.subtract).then_inc(z_lo, 1)
            split_mod(2)
            split_mod(3)
            e = 0
            for f, (g, r, kind, p, q) in enumerate(FU):
                if f - 1 in MOD_ROWS:
                    mod_rows(MOD_ROWS[f - 1])
                dve.wait_ge(f_ready, f + 1)
                if f == len(FU) - 1:
                    norm_lo(0, 0)
                    norm_t(0, 2)
                    norm_lo(0, 1)
                if f == 0:
                    dve.wait_ge(ld_filt2, 16 * 4)
                if kind == 0:
                    prev = [spec_end[x] for x in ((0, 0), (0, 1), (1, 0), (1, 1)) if spec_end[x] <= f]
                    if prev:
                        dve.wait_ge(f_ready, prev[-1])
                    d = dec if g == 0 else dec_p
                    m0 = 2 * r if g else 2 * q
                    dve.tensor_tensor(taps[:, p, m0:m0 + 2, :].rearrange("p m n -> p (m n)"),
                                      acc_ps[:, f % 2, :], d[:, 2 * q:2 * q + 2, :].rearrange("p m n -> p (m n)"),
                                      ALU.mult).then_inc(f_free, 1)
                else:
                    dve.wait_ge(f_even, e + 1)
                    if e >= 4:
                        dve.wait_ge(f_stored[e % 4], 16 * (e // 4))
                    even = fE[e % 2]
                    odd = acc_ps[:, f % 2, 512:1024]
                    dve.tensor_tensor(spec_out(e)[:, 0, :], odd, even[:], ALU.add)
                    a0, a1 = (even[:], odd) if p == 0 else (odd, even[:])
                    dve.tensor_tensor(spec_out(e)[:, 1, :], a0, a1, ALU.subtract).then_inc(f_free, 1)
                    e += 1
                if f in MOD_SUMS:
                    mod_out(MOD_SUMS[f])
                if 2 <= f < MOD_A - 2:
                    split_mod(f + 2)
                if f == 13:
                    norm_rstd(0)
                if f in (taps_over, taps_over + 1):
                    split_w(f - taps_over)
                if f == 20:
                    dve.wait_ge(mod_done, MB_A)
                    norm_scale(0)
                    norm_t(0, 0)
                    norm_t(0, 1)
            norm_apply(0, first_t=3, first_lo=2)

            def conv_sides(t):
                s, m = t % 2, t - T_HY
                dve.wait_ge(cv_mid, m + 1)
                for c0, L in GROUPS:
                    dve.scalar_tensor_tensor(xv[:, m, c0 + 1:c0 + L], acc_ps[:, s, c0:c0 + L - 1], cwT[:, m:m + 1],
                                             xv[:, m, c0 + 1:c0 + L], ALU.mult, ALU.add).then_inc(cv_part, 1)
                for g, (c0, L) in enumerate(GROUPS):
                    dve.wait_ge(cv_part, 2 * m + 1 + g)
                    last = dve.scalar_tensor_tensor(xv[:, m, c0:c0 + L - 1], acc_ps[:, s, c0 + 1:c0 + L],
                                                    cwT[:, 24 + m:25 + m], xv[:, m, c0:c0 + L - 1], ALU.mult, ALU.add)
                last.then_inc(acc_free[s], 1)

            def rope(j):
                dve.wait_ge(rot_ready, j + 1)
                if j >= 1:
                    dve.wait_ge(rope_done, j)
                dve.tensor_tensor(rt[:], wk[:, 0:T], sin[:], ALU.mult).then_inc(rope_step, 1)
                dve.tensor_tensor(qk[:, j, :], qk[:, j, :], cos[:], ALU.mult).then_inc(rope_mul, 1)
                dve.wait_ge(rope_step, j + 1)
                dve.wait_ge(rope_mul, j + 1)
                dve.tensor_tensor(qk[:, j, :], qk[:, j, :], rt[:], ALU.add).then_inc(rope_done, 1)

            def softmax_in(n, last_mod):
                qb, kv = ATT[n]
                _, nk, m0 = att_keys(qb)
                b = n % 2
                if n >= 2:
                    dve.wait_ge(p_ready, sum(att_keys(q)[1] for q, _ in ATT[:n - 1]))
                for j in range(NJ):
                    c = bank("scores", n, j)
                    dve.wait_ge(s_ready, NJ * n + j + 1)
                    dve.tensor_tensor_reduce(S[:, b, j, 0:P * nk], wk[:, c:c + P * nk], mask[:, m0:m0 + P * nk],
                                             HD ** -0.5, sink[:, NJ * kv + j:NJ * kv + j + 1], ALU.add, ALU.max,
                                             mx[:, b, j:j + 1]).then_inc(s_max, 1)
                    if j == 0 and last_mod is not None:
                        split_mod(last_mod)
                dve.wait_ge(s_max, NJ * n + NJ)
                dve.tensor_scalar(nmx[:, b], mx[:, b], -1.0, None, ALU.mult).then_inc(s_neg, 1)
                dve.tensor_tensor(sd[:, b], sink[:, NJ * kv:NJ * kv + NJ], mx[:, b], ALU.subtract).then_inc(s_sd, 1)

            def softmax_out(n):
                b = n % 2
                nk = att_keys(ATT[n][0])[1]
                dve.wait_ge(s_exp, NJ * n + NJ)
                dve.wait_ge(s_es, n + 1)
                dve.tensor_tensor(den[:, b], den[:, b], es[:, b], ALU.add).then_inc(s_den, 1)
                dve.wait_ge(s_den, n + 1)
                dve.reciprocal(rden[:, b], den[:, b]).then_inc(s_rden, 1)
                dve.wait_ge(s_rden, n + 1)
                for j in range(NJ):
                    last = dve.tensor_scalar(S[:, b, j, 0:P * nk], S[:, b, j, 0:P * nk], rden[:, b, j:j + 1], None, ALU.mult)
                last.then_inc(s_norm, 1)

            def products(n):
                dve.wait_ge(ld_spec, 32 * (n + 1))
                dve.wait_ge(tab_lo, 2)
                for b in range(4):
                    dve.wait_ge(fwd_ready, 4 * n + b + 1)
                    if b >= 1:
                        dve.wait_ge(prod_done, 4 * n + b)
                    elif n >= 1:
                        dve.wait_ge(prod_done, 4 * n)
                    c = bank("forward", n, b)
                    src = wk[:, c:c + 512].rearrange("p (d n) -> p d n", d=2)
                    for pq in range(2):
                        dve.tensor_tensor(cm[:, 512 * pq:512 * pq + 512].rearrange("p (d n) -> p d n", d=2), src,
                                          spec[:, pq, b:b + 1, :].broadcast_to([P, 2, 256]), ALU.mult).then_inc(cross_step, 1)
                    dve.wait_ge(cross_step, 8 * n + 2 * b + 2)
                    dve.tensor_tensor(Y[:, b, 0, :], cm[:, 0:256], cm[:, 768:1024], ALU.add)
                    dve.tensor_tensor(Y[:, b, 1, :], cm[:, 256:512], cm[:, 512:768], ALU.subtract).then_inc(prod_done, 1)

            def turn_low(n):
                for e in range(2):
                    c = bank("turn", n, e)
                    dve.wait_ge(turn_copied, 2 * n + e + 1)
                    dve.tensor_tensor(eoT_lo[:, 512 * e:512 * e + 512], wk[:, c:c + 512], eoT_hi[:, 512 * e:512 * e + 512],
                                      ALU.subtract).then_inc(turn_lo, 1)
                if n == 0:
                    for i, (lo, rw, hi) in enumerate(((tabF_lo, rawF, tabF_hi), (tabFp_lo, rawFp, tabFp_hi))):
                        dve.wait_ge(tab_hi, i + 1)
                        dve.tensor_tensor(lo[:], rw[:], hi[:], ALU.subtract).then_inc(tab_lo, 1)

            def combine(n):
                u, r = STEPS[n]
                g, ct0, nct = UNITS[u]
                c0, L = GROUPS[g]
                full = yfull[:].rearrange("p (c n) -> p c n", n=L)
                dve.wait_ge(y_done, n + 1)
                for ct in range(nct):
                    hb = V_HB + 4 * r + ct0 + ct
                    dve.scalar_tensor_tensor(full[:, ct, :], xv[:, 8 + ct0 + ct, c0:c0 + L], vT[:, hb:hb + 1],
                                             full[:, ct, :], ALU.mult, ALU.add).then_inc(y_step, 1)
                    steps_y[0] += 1
                dve.wait_ge(y_step, steps_y[0])
                dve.tensor_tensor(xv[:, 8 + ct0:8 + ct0 + nct, c0:c0 + L], full,
                                  xv[:, 4 * r + ct0:4 * r + ct0 + nct, c0:c0 + L], ALU.mult).then_inc(z_done, 1)

            steps_y = [0]
            def attend(n, last_mod=None):
                softmax_in(n, last_mod)
                softmax_out(n)

            def split_out(k):
                src = qk[:, k, :] if k < 4 else xv[:, 4 + k, :]
                dve.wait_ge(sp_hi, k + 1)
                dve.tensor_tensor(act[:, 1, k, :], src, act[:, 0, k, :], ALU.subtract).then_inc(sp_lo, 1)

            run = {"values": lambda n: None, "turn": turn_low, "forward": products,
                   "inverse": combine}
            for i in range(2):
                split_mod(MOD_A + i)
            for t in range(T_MERGE):
                b = MB_A + t
                if 0 < t <= T_GATE:
                    mod_out(b - 1)
                if T_HY <= t < T_GATE:
                    conv_sides(t)
                if t == 1:
                    dve.wait_ge(ld_rope, 16 * 4)
                if t == T_MERGE - 1:
                    for k in range(4):
                        split_out(k)
                last_mod = MOD_BATCH[b][0] + 2 if t < T_GATE and MOD_BATCH[b][1] == 3 else None
                if t == T_HY:
                    split_mod(last_mod)
                    last_mod = None
                split_w(t + 2)
                if 1 <= t <= T_V:
                    rope(t - 1)
                if t == T_GATE:
                    dve.wait_ge(mod_done, len(MOD_BATCH))
                    norm_scale(1)
                    norm_scale(2)
                for kind, n in STAGES[t]:
                    if kind == "scores":
                        attend(n, last_mod)
                        last_mod = None
                    else:
                        run[kind](n)
                if last_mod is not None:
                    split_mod(last_mod)
                if t < T_GATE:
                    mod_rows(b)
                if t < T_GATE - 1:
                    for i in range(2):
                        split_mod(MOD_BATCH[b + 1][0] + i)

            for k in range(4, KD):
                split_out(k)

            for m in range(KD):
                if m >= 1:
                    dve.wait_ge(mg_done, m)
                dve.wait_ge(ld_gate[m % 2], 32 * (m // 2 + 1))
                for x in range(2):
                    dve.wait_ge(acc_ready, A_MERGE + 2 * m + x + 1)
                    dve.tensor_tensor(tmp[:, x, :], acc_ps[:, x, 0:T], gin[:, m % 2, x, :], ALU.mult)\
                        .then_inc(acc_free[x], 1)
                mg = tmp[:, 2, :] if m % 2 else sqB[:]
                for x in range(2):
                    dve.wait_ge(acc_free[x], A_MERGE // 2 + m + 1)
                dve.tensor_tensor(mg, tmp[:, 0, :], tmp[:, 1, :], ALU.add).then_inc(mg_done, 1)
                split_w(T_MERGE + m + 2)
                dve.wait_ge(mg_hi, m + 1)
                dve.tensor_tensor(hid[:, 1, m, :], mg, hid[:, 0, m, :], ALU.subtract).then_inc(mg_lo, 1)

            def residual(s, m, gate, before):
                if before is not None:
                    dve.wait_ge(acc_free[s], before)
                for g, (c0, L) in enumerate(GROUPS):
                    row = xT[:, bass.ds(m, 1), c0:c0 + L].rearrange("p o n -> p (o n)")
                    last = dve.scalar_tensor_tensor(
                        row, acc_ps[:, s, c0:c0 + L], modT[:, bass.ds(gate + m, 1), g:g + 1].rearrange("p o n -> p (o n)"),
                        row, ALU.mult, ALU.add)
                last.then_inc(acc_free[s], 1)

            dve.wait_ge(ld_x2, 16)
            for m in range(KD):
                dve.wait_ge(acc_ready, A_OUT + m + 1)
                residual(m % 2, m, G1, None)
                if m < KD - 2:
                    split_w(T_OUT + m + 2)
                elif m < KD - 1:
                    split_w(T_OUT + m + 2, m % 2, 16 * (landed_base[m % 2] + 1))
                if m >= 1:
                    norm_acc(1, m - 1)
            norm_acc(1, KD - 1)
            split_w(T_MLP + 1, 1, 16 * (landed_base[1] + 1))
            norm_rstd(1)
            norm_apply(1)

            def up(c):
                with dve.Fori(0, KD // 2) as i:
                    for s in range(2):
                        u = c * 8 + i * 2 + s
                        dve.wait_ge(acc_free[s], A_MLP // 2 + 1 + c * 8 + i)
                        dve.tensor_tensor(hfB[:, s, :], tmp[:, s, :], tmp[:, s, :], ALU.mult).then_inc(up_sq, 1)
                        split_w(T_MLP + 2 + c * 16 + i * 2 + s, s, (landed_base[s] + 2 + c * 8 + i) * 16)
                        dve.wait_ge(hid_hi, u + 1)
                        m = bass.ds(i * 2 + s, 1)
                        dve.tensor_tensor(hid[:, 1, m, :].rearrange("p o n -> p (o n)"), hfB[:, s, :],
                                          hid[:, 0, m, :].rearrange("p o n -> p (o n)"), ALU.subtract).then_inc(hid_lo, 1)
                        dve.wait_ge(hid_lo, u + 1)

            with dve.Fori(0, NCH - 1) as c:
                up(c)
                with dve.Fori(0, KD // 2) as i:
                    for s in range(2):
                        dve.wait_ge(acc_ready, A_MLP + KD + 1 + c * 16 + i * 2 + s)
                        residual(s, i * 2 + s, G2, A_OUT // 2 + 1 + c * 8 + i)
                        split_w(T_MLP + KD + 2 + c * 16 + i * 2 + s, s, (landed_base[s] + 6 + c * 8 + i) * 16)
            up(NCH - 1)
            for m in range(KD):
                dve.wait_ge(acc_ready, A_MLP + 16 * (NCH - 1) + KD + m + 1)
                residual(m % 2, m, G2, A_OUT // 2 + 1 + KD * (NCH - 1) + m // 2)
                if m < KD - 2:
                    t = T_MLP + 16 * (NCH - 1) + KD + m + 2
                    split_w(t, m % 2, 16 * (landed_base[m % 2] + (t - T_MLP) // 2 + 1))
                if m >= 1:
                    norm_acc(2, m - 1)
            norm_acc(2, KD - 1)
            norm_rstd(2)
            dve.wait_ge(n_rstd, 3)
            dve.wait_ge(y_copied, KD)
            for b in DVE_BLOCKS:
                dve.scalar_tensor_tensor(onat[:, b], onat[:, b], rs[:, b:b + 1], shrow[:, 1 - b // 4], ALU.mult,
                                         ALU.add).then_inc(y_dve, 1)


def tables():
    import numpy as np

    f = np.float32
    out = {"t_ident": np.eye(P)}
    dist = np.arange(3 * P)[None, :] - P - np.arange(P)[:, None]
    out["t_mask"] = np.where(np.abs(dist) <= 128, 0.0, -8e30)
    rot = np.zeros((P, P))
    for h in range(0, P, HD):
        for d in range(8):
            rot[h + d + 8, h + d] = -1.0
            rot[h + d, h + d + 8] = 1.0
    out["t_rot"] = rot
    pos = np.concatenate([np.arange(TS), np.arange(TP)])
    inv = f(500000.0) ** (-np.arange(8, dtype=f) * f(2.0) / f(16.0))
    ang = (pos.astype(f)[:, None] * inv[None, :]).astype(f).astype(np.float64)
    cos, sin = np.ones((P, T)), np.zeros((P, T))
    for h in range(0, P, HD):
        for d in range(16):
            cos[h + d] = np.cos(ang[:, d % 8])
            sin[h + d] = np.sin(ang[:, d % 8])
    out["t_cos"], out["t_sin"] = cos, sin
    zs = []
    for L in (TS, TP):
        t = np.linspace(0.0, 1.0, L, dtype=f)
        w = (f(2.0 * PI) * np.arange(L, dtype=f) / f(L)).astype(f)
        fr = np.linspace(1e-4, 15, 16, dtype=f)
        fw = (fr[:, None] * w[None, :]).astype(f).astype(np.float64)
        zs.append(np.concatenate([t[None].astype(np.float64), np.cos(fw), -np.sin(fw)], axis=0))
    out["t_z"] = np.concatenate(zs, axis=1)
    lo, hi = np.log(1e-2) / 1.5, np.log(1e-2) / 0.3
    deltas = np.abs(np.linspace(lo, hi, HW, dtype=f)).astype(np.float64)

    def rows(m):
        return m.reshape(-1, P, m.shape[1]).transpose(1, 0, 2)

    for L, n in ((TS, "s"), (TP, "p")):
        half = L // 2
        i = np.arange(half)
        m = np.concatenate([2 * i, 2 * i + 1])
        t = np.linspace(0.0, 1.0, L, dtype=f).astype(np.float64)[m]
        out[f"t_decay_{n}"] = rows(np.exp(-t[:, None] * deltas[None, :]) + 0.05)
        k1 = 2 * i
        k2 = L - 1 - k1
        mats = []
        for fn in (np.cos, np.sin):
            for odd in range(2):
                mats.append(rows(fn(np.pi * (k1[None, :] + 0.5) * (2 * i + odd)[:, None] / L)))
        out[f"t_filt_{n}"] = np.stack(mats, 1)
        fwd, inv_t = [], []
        for k in (k1, k2):
            th = np.pi * (k[None, :] + 0.5) * (i[:, None] + 0.5) / L
            for sg in (1, -1):
                m = np.cos(th) + sg * np.sin(th)
                fwd.append(rows(m))
                inv_t.append(rows(m.T / (2 * L)))
        out[f"t_fwd_{n}"] = np.stack(fwd, 1)
        out[f"t_inv_{n}"] = np.stack(inv_t, 1)
        if n == "p":
            for q in ("t_filt_p", "t_fwd_p", "t_inv_p"):
                out[q] = out[q][:, :, 0, :]
    return {k: np.ascontiguousarray(v.astype(f)) for k, v in out.items()}


_INS = ["x_prompt", "x_sample", "c_prompt", "c_sample", "w_ada", "b_ada", "norm1_g", "w_in", "attn_sink", "conv_w",
        "conv_b", "filt_w1", "filt_b1", "filt_freq1", "filt_w2", "filt_b2", "filt_freq2", "filt_w3", "hyena_bias",
        "w_attn_o", "w_hyena_o", "w_out", "norm2_g", "w_up", "w_down", "w_ada_final", "b_ada_final", "final_g"]


def kernel(**inputs):
    import numpy as np
    import concourse.bacc as bacc
    from concourse.bass_utils import run_bass_kernel_spmd

    nc = bacc.Bacc("TRN2", target_bir_lowering=False, num_devices=1)
    arrays, a = {}, {}
    host = {n: np.ascontiguousarray(inputs[n]) for n in _INS}
    host.update(tables())
    for n, v in host.items():
        arrays["in_" + n] = v
        a[n] = nc.dram_tensor("in_" + n, v.shape, mybir.dt.from_np(v.dtype), kind="ExternalInput").ap()
    out_p = nc.dram_tensor("out_p", (1, TP, D), F32, kind="ExternalOutput").ap()
    out_s = nc.dram_tensor("out_s", (1, TS, D), F32, kind="ExternalOutput").ap()
    program(nc, a, out_p, out_s)
    r = run_bass_kernel_spmd(nc, [arrays], core_ids=[0])
    return r.results[0]["out_p"], r.results[0]["out_s"]
```
